# Optimizing a Trainium2 kernel written in Bass

```python
import jax, jax.numpy as jnp
from jax import lax
import numpy as np

D_MODEL = 1024
BATCH = 1
SEQ = 512
DEPTH = 1
DEC_BATCH = 8
DEC_SEQ = 8
PAST_LEN = 1024
PAGE_SIZE = 128

HEAD_DIM = 64
N_HEADS = D_MODEL // (2 * HEAD_DIM)
N_KV_HEADS = N_HEADS // 2
KV_GROUP = N_HEADS // N_KV_HEADS
ATTN_WIDTH = N_HEADS * HEAD_DIM
KV_WIDTH = N_KV_HEADS * HEAD_DIM
N_IDX_HEADS = 8
IDX_DIM = 64
TOPK_MAX = 256
Q_BLOCK = 128
ROPE_THETA = 10000.0
POOL_WINDOWS = (2, 4, 8, 16)
N_POOL_GROUPS = len(POOL_WINDOWS)
POOL_WIDTH = D_MODEL // 2
POOL_GROUP = POOL_WIDTH // N_POOL_GROUPS
POOL_HIST = max(POOL_WINDOWS) - 1
N_GROUPS = 4
EXPERTS_PER_GROUP = 8
N_EXPERTS = N_GROUPS * EXPERTS_PER_GROUP
TOP_K = 2
D_EXPERT = D_MODEL // 2
MOE_BLOCK = 128
RMS_EPS = 1e-6
SEGMENTS = (ATTN_WIDTH, KV_WIDTH, KV_WIDTH, N_IDX_HEADS * IDX_DIM, IDX_DIM, N_IDX_HEADS,
            POOL_WIDTH, D_MODEL, D_MODEL)
PROJ_WIDTH = sum(SEGMENTS)

kernel_name = 'dsa_pool_gated_hmoe_step'

def rms_norm(x, g):
    xf = x.astype(jnp.float32)
    y = xf * lax.rsqrt(jnp.mean(xf * xf, axis=-1, keepdims=True) + RMS_EPS)
    return (y * g.astype(jnp.float32)).astype(x.dtype)

def rope(x, pos):
    half = x.shape[-1] // 2
    inv_freq = 1.0 / (ROPE_THETA ** (jnp.arange(half, dtype=jnp.float32) / half))
    ang = pos.astype(jnp.float32)[:, None] * inv_freq[None, :]
    cos = jnp.cos(ang)[None, :, None, :]
    sin = jnp.sin(ang)[None, :, None, :]
    xf = x.astype(jnp.float32)
    x1, x2 = xf[..., :half], xf[..., half:]
    return jnp.concatenate([x1 * cos - x2 * sin, x1 * sin + x2 * cos], axis=-1).astype(x.dtype)

def project_mixer_inputs(xn, w_in, pos):
    B, T, _ = xn.shape
    cuts = [int(c) for c in np.cumsum(SEGMENTS)[:-1]]
    q, k, v, qi, ki, wi, u, ga, gb = jnp.split(xn @ w_in, cuts, axis=-1)
    q = rope(q.reshape(B, T, N_HEADS, HEAD_DIM), pos)
    k = rope(k.reshape(B, T, N_KV_HEADS, HEAD_DIM), pos)
    v = v.reshape(B, T, N_KV_HEADS, HEAD_DIM)
    qi = rope(qi.reshape(B, T, N_IDX_HEADS, IDX_DIM), pos)
    ki = rope(ki[:, :, None, :], pos)[:, :, 0, :]
    return q, k, v, qi, ki, wi, u, ga, gb

def indexer_select(qi, wi, ki_all, q_pos, n_sel):
    L = ki_all.shape[1]
    s = jnp.einsum('bqhd,bld->bqhl', qi, ki_all).astype(jnp.float32) * (IDX_DIM ** -0.5)
    w = wi.astype(jnp.float32) * (N_IDX_HEADS ** -0.5)
    score = jnp.einsum('bqhl,bqh->bql', jax.nn.relu(s), w)
    admissible = jnp.arange(L)[None, None, :] <= q_pos[None, :, None]
    score = jnp.where(admissible, score, -jnp.inf)
    _, idx = lax.top_k(score, n_sel)
    valid = idx <= q_pos[None, :, None]
    return idx, valid

def attend_selected(q, k_s, v_s, valid):
    B, Q = q.shape[:2]
    qg = q.reshape(B, Q, N_KV_HEADS, KV_GROUP, HEAD_DIM)
    logits = jnp.einsum('bqhgd,bqnhd->bqhgn', qg, k_s).astype(jnp.float32) * (HEAD_DIM ** -0.5)
    logits = jnp.where(valid[:, :, None, None, :], logits, -jnp.inf)
    p = jax.nn.softmax(logits, axis=-1)
    o = jnp.einsum('bqhgn,bqnhd->bqhgd', p.astype(v_s.dtype), v_s)
    return o.reshape(B, Q, ATTN_WIDTH)

def prompt_sparse_attention(q, k, v, qi, ki, wi):
    B, S = q.shape[:2]
    n_sel = min(TOPK_MAX, S // 4)
    nb = S // Q_BLOCK
    bidx = jnp.arange(B)[:, None, None]

    def to_blocks(a):
        return jnp.moveaxis(a.reshape((B, nb, Q_BLOCK) + a.shape[2:]), 1, 0)

    def one_block(args):
        qb, qib, wib, posb = args
        idx, valid = indexer_select(qib, wib, ki, posb, n_sel)
        return attend_selected(qb, k[bidx, idx], v[bidx, idx], valid)

    pos = jnp.arange(S).reshape(nb, Q_BLOCK)
    o = lax.map(one_block, (to_blocks(q), to_blocks(qi), to_blocks(wi), pos))
    return jnp.moveaxis(o, 0, 1).reshape(B, S, ATTN_WIDTH)

def sample_sparse_attention(q, k_new, v_new, qi, ki_new, wi, l, cache_k, cache_v, cache_idx_k, page_table):
    DB, DS = q.shape[:2]
    ps = cache_k.shape[2]
    past = page_table.shape[1] * ps
    n_sel = min(TOPK_MAX, (past + DS) // 4)
    ki_past = cache_idx_k[l, page_table].reshape(DB, past, IDX_DIM)
    ki_all = jnp.concatenate([ki_past.astype(ki_new.dtype), ki_new], axis=1)
    q_pos = past + jnp.arange(DS)
    idx, valid = indexer_select(qi, wi, ki_all, q_pos, n_sel)
    bidx = jnp.arange(DB)[:, None, None]
    in_past = (idx < past)[..., None, None]
    ip = jnp.minimum(idx, past - 1)
    phys = page_table[bidx, ip // ps]
    off = ip % ps
    jn = jnp.clip(idx - past, 0, DS - 1)
    k_s = jnp.where(in_past, cache_k[l, phys, off].astype(k_new.dtype), k_new[bidx, jn])
    v_s = jnp.where(in_past, cache_v[l, phys, off].astype(v_new.dtype), v_new[bidx, jn])
    return attend_selected(q, k_s, v_s, valid)

def multiscale_pool_diff(u_all, n_hist):
    B, Ltot, C = u_all.shape
    uf = u_all.astype(jnp.float32)
    csum = jnp.concatenate([jnp.zeros((B, 1, C), jnp.float32), jnp.cumsum(uf, axis=1)], axis=1)
    i = jnp.arange(n_hist, Ltot)
    hi = csum[:, i + 1]
    cur = uf[:, n_hist:]
    outs = []
    for g, w in enumerate(POOL_WINDOWS):
        lo = jnp.maximum(i + 1 - w, 0)
        cnt = (i + 1 - lo).astype(jnp.float32)[None, :, None]
        sl = slice(g * POOL_GROUP, (g + 1) * POOL_GROUP)
        outs.append((hi[..., sl] - csum[:, lo, sl]) / cnt - cur[..., sl])
    return jnp.concatenate(outs, axis=-1).astype(u_all.dtype)

def pool_branch(u_all, n_hist, w_pool, pool_scale):
    d = multiscale_pool_diff(u_all, n_hist)
    B, T, _ = d.shape
    y = jnp.einsum('btgc,gcd->btgd', d.reshape(B, T, N_POOL_GROUPS, POOL_GROUP), w_pool)
    return y.reshape(B, T, POOL_WIDTH) * pool_scale

def merge_branches(x, attn_o, pool_o, ga, gb, w_branch_attn, w_branch_pool, w_out):
    m = jax.nn.sigmoid(ga) * (attn_o @ w_branch_attn) + jax.nn.sigmoid(gb) * (pool_o @ w_branch_pool)
    return x + m @ w_out

def moe_ffn(xn, w_router_group, b_router_group, w_router_expert, b_router_expert,
            w_exp_gate, w_exp_up, w_exp_down):
    shp = xn.shape
    xt = xn.reshape(-1, shp[-1])
    T = xt.shape[0]
    xf = xt.astype(jnp.float32)
    g_logits = xf @ w_router_group.astype(jnp.float32) + b_router_group.astype(jnp.float32)
    g_sel = jnp.argmax(g_logits, axis=-1)
    g_w = jnp.take_along_axis(jax.nn.softmax(g_logits, axis=-1), g_sel[:, None], axis=-1)[:, 0]
    e_logits = (xf @ w_router_expert.astype(jnp.float32) + b_router_expert.astype(jnp.float32))
    e_logits = e_logits.reshape(T, N_GROUPS, EXPERTS_PER_GROUP)
    e_in_group = jnp.take_along_axis(e_logits, g_sel[:, None, None], axis=1)[:, 0]
    top_v, top_i = lax.top_k(e_in_group, TOP_K)
    e_w = jax.nn.softmax(top_v, axis=-1) * g_w[:, None]
    e_id = g_sel[:, None] * EXPERTS_PER_GROUP + top_i
    n_assign = T * TOP_K
    e_flat = e_id.reshape(-1)
    tok_flat = jnp.repeat(jnp.arange(T, dtype=jnp.int32), TOP_K)
    w_flat = e_w.reshape(-1)
    order = jnp.argsort(e_flat)
    e_sorted = e_flat[order]
    counts = jnp.zeros((N_EXPERTS,), jnp.int32).at[e_flat].add(1)
    padded = (counts + MOE_BLOCK - 1) // MOE_BLOCK * MOE_BLOCK
    start = jnp.cumsum(counts) - counts
    pend = jnp.cumsum(padded)
    pstart = pend - padded
    dest = pstart[e_sorted] + (jnp.arange(n_assign) - start[e_sorted])
    n_blocks = (n_assign + N_EXPERTS * (MOE_BLOCK - 1)) // MOE_BLOCK + 1
    buf_tok = jnp.zeros((n_blocks * MOE_BLOCK,), jnp.int32).at[dest].set(tok_flat[order])
    buf_w = jnp.zeros((n_blocks * MOE_BLOCK,), jnp.float32).at[dest].set(w_flat[order])
    block_e = jnp.minimum(jnp.searchsorted(pend, jnp.arange(n_blocks) * MOE_BLOCK, side='right'),
                          N_EXPERTS - 1)

    def run_block(args):
        tok, wt, e = args
        xb = xt[tok]
        hb = jax.nn.silu(xb @ w_exp_gate[e]) * (xb @ w_exp_up[e])
        return (hb @ w_exp_down[e]) * wt[:, None].astype(xb.dtype)

    yb = lax.map(run_block, (buf_tok.reshape(n_blocks, MOE_BLOCK), buf_w.reshape(n_blocks, MOE_BLOCK), block_e))
    out = jnp.zeros_like(xt).at[buf_tok].add(yb.reshape(-1, shp[-1]).astype(xt.dtype))
    return out.reshape(shp)

def prompt_layer(x, lw):
    (attn_norm_g, w_in, w_pool, pool_scale, w_branch_attn, w_branch_pool, w_out, ffn_norm_g,
     w_rg, b_rg, w_re, b_re, w_eg, w_eu, w_ed) = lw
    S = x.shape[1]
    pos = jnp.arange(S)
    xn = rms_norm(x, attn_norm_g)
    q, k, v, qi, ki, wi, u, ga, gb = project_mixer_inputs(xn, w_in, pos)
    attn_o = prompt_sparse_attention(q, k, v, qi, ki, wi)
    pool_o = pool_branch(u, 0, w_pool, pool_scale)
    h = merge_branches(x, attn_o, pool_o, ga, gb, w_branch_attn, w_branch_pool, w_out)
    h = h + moe_ffn(rms_norm(h, ffn_norm_g), w_rg, b_rg, w_re, b_re, w_eg, w_eu, w_ed)
    return h, k, v, ki, u[:, -POOL_HIST:]

def sample_layer(x, l, cache_k, cache_v, cache_idx_k, state_pool, page_table, lw):
    (attn_norm_g, w_in, w_pool, pool_scale, w_branch_attn, w_branch_pool, w_out, ffn_norm_g,
     w_rg, b_rg, w_re, b_re, w_eg, w_eu, w_ed) = lw
    DS = x.shape[1]
    past = page_table.shape[1] * cache_k.shape[2]
    pos = past + jnp.arange(DS)
    xn = rms_norm(x, attn_norm_g)
    q, k, v, qi, ki, wi, u, ga, gb = project_mixer_inputs(xn, w_in, pos)
    attn_o = sample_sparse_attention(q, k, v, qi, ki, wi, l, cache_k, cache_v, cache_idx_k, page_table)
    n_hist = state_pool.shape[2]
    u_all = jnp.concatenate([state_pool[l].astype(u.dtype), u], axis=1)
    pool_o = pool_branch(u_all, n_hist, w_pool, pool_scale)
    h = merge_branches(x, attn_o, pool_o, ga, gb, w_branch_attn, w_branch_pool, w_out)
    h = h + moe_ffn(rms_norm(h, ffn_norm_g), w_rg, b_rg, w_re, b_re, w_eg, w_eu, w_ed)
    return h, k, v, ki, u_all[:, -n_hist:]

def setup_inputs(seed: int = 0) -> dict:
    key = jax.random.key(seed)
    ks = jax.random.split(key, 24)
    f32 = jnp.float32
    n_pages = PAST_LEN // PAGE_SIZE
    n_phys = (DEC_BATCH * n_pages * 5) // 4

    def nrm(k, shape, scale):
        return jax.random.normal(k, shape, f32) * scale

    def gain(k, shape):
        return 1.0 + 0.1 * jax.random.normal(k, shape, f32)

    page_table = jax.random.permutation(ks[6], n_phys)[: DEC_BATCH * n_pages]
    page_table = page_table.reshape(DEC_BATCH, n_pages).astype(jnp.int32)
    return {
        'x_prompt': nrm(ks[0], (BATCH, SEQ, D_MODEL), 1.0),
        'x_sample': nrm(ks[1], (DEC_BATCH, DEC_SEQ, D_MODEL), 1.0),
        'cache_k': nrm(ks[2], (DEPTH, n_phys, PAGE_SIZE, N_KV_HEADS, HEAD_DIM), 1.0),
        'cache_v': nrm(ks[3], (DEPTH, n_phys, PAGE_SIZE, N_KV_HEADS, HEAD_DIM), 1.0),
        'cache_idx_k': nrm(ks[4], (DEPTH, n_phys, PAGE_SIZE, IDX_DIM), 1.0),
        'state_pool': nrm(ks[5], (DEPTH, DEC_BATCH, POOL_HIST, POOL_WIDTH), 1.0),
        'page_table': page_table,
        'attn_norm_g': gain(ks[7], (DEPTH, D_MODEL)),
        'w_in': nrm(ks[8], (DEPTH, D_MODEL, PROJ_WIDTH), D_MODEL ** -0.5),
        'w_pool': nrm(ks[9], (DEPTH, N_POOL_GROUPS, POOL_GROUP, POOL_GROUP), POOL_GROUP ** -0.5),
        'pool_scale': gain(ks[10], (DEPTH, POOL_WIDTH)),
        'w_branch_attn': nrm(ks[11], (DEPTH, ATTN_WIDTH, D_MODEL), ATTN_WIDTH ** -0.5),
        'w_branch_pool': nrm(ks[12], (DEPTH, POOL_WIDTH, D_MODEL), POOL_WIDTH ** -0.5),
        'w_out': nrm(ks[13], (DEPTH, D_MODEL, D_MODEL), D_MODEL ** -0.5),
        'ffn_norm_g': gain(ks[14], (DEPTH, D_MODEL)),
        'w_router_group': nrm(ks[15], (DEPTH, D_MODEL, N_GROUPS), D_MODEL ** -0.5),
        'b_router_group': nrm(ks[16], (DEPTH, N_GROUPS), 0.01),
        'w_router_expert': nrm(ks[17], (DEPTH, D_MODEL, N_EXPERTS), D_MODEL ** -0.5),
        'b_router_expert': nrm(ks[18], (DEPTH, N_EXPERTS), 0.01),
        'w_exp_gate': nrm(ks[19], (DEPTH, N_EXPERTS, D_MODEL, D_EXPERT), D_MODEL ** -0.5),
        'w_exp_up': nrm(ks[20], (DEPTH, N_EXPERTS, D_MODEL, D_EXPERT), D_MODEL ** -0.5),
        'w_exp_down': nrm(ks[21], (DEPTH, N_EXPERTS, D_EXPERT, D_MODEL), D_EXPERT ** -0.5),
        'final_norm_g': gain(ks[22], (D_MODEL,)),
    }

def reference(x_prompt, x_sample, cache_k, cache_v, cache_idx_k, state_pool, page_table,
              attn_norm_g, w_in, w_pool, pool_scale, w_branch_attn, w_branch_pool, w_out,
              ffn_norm_g, w_router_group, b_router_group, w_router_expert, b_router_expert,
              w_exp_gate, w_exp_up, w_exp_down, final_norm_g):
    hp, hs = x_prompt, x_sample
    kp_l, vp_l, kip_l, up_l = [], [], [], []
    ks_l, vs_l, kis_l, us_l = [], [], [], []
    for l in range(DEPTH):
        lw = (attn_norm_g[l], w_in[l], w_pool[l], pool_scale[l], w_branch_attn[l], w_branch_pool[l],
              w_out[l], ffn_norm_g[l], w_router_group[l], b_router_group[l], w_router_expert[l],
              b_router_expert[l], w_exp_gate[l], w_exp_up[l], w_exp_down[l])
        hp, kp, vp, kip, up = prompt_layer(hp, lw)
        hs, ks_, vs, kis, us = sample_layer(hs, l, cache_k, cache_v, cache_idx_k, state_pool, page_table, lw)
        kp_l.append(kp); vp_l.append(vp); kip_l.append(kip); up_l.append(up)
        ks_l.append(ks_); vs_l.append(vs); kis_l.append(kis); us_l.append(us)
    y_prompt = rms_norm(hp, final_norm_g)
    y_sample = rms_norm(hs, final_norm_g)
    new_k_prompt = jnp.stack(kp_l, 0)
    new_v_prompt = jnp.stack(vp_l, 0)
    new_idx_k_prompt = jnp.stack(kip_l, 0)
    new_pool_prompt = jnp.stack(up_l, 0)
    new_k_sample = jnp.stack(ks_l, 0)
    new_v_sample = jnp.stack(vs_l, 0)
    new_idx_k_sample = jnp.stack(kis_l, 0)
    new_pool_sample = jnp.stack(us_l, 0)
    return (y_prompt, y_sample, new_k_prompt, new_v_prompt, new_idx_k_prompt, new_pool_prompt,
            new_k_sample, new_v_sample, new_idx_k_sample, new_pool_sample)


_drawn_inputs = setup_inputs


def setup_inputs(seed=0):
    import zlib

    import numpy as np

    out = dict(_drawn_inputs(seed))
    spreads = {}
    factors = {'b_router_group': 7.087, 'b_router_expert': 3.319}
    for name, (base, spread) in spreads.items():
        noise = np.random.default_rng([zlib.crc32(name.encode()), seed]).standard_normal(out[name].shape)
        drawn = base * np.exp(spread * noise) if base else spread * noise
        out[name] = __import__('jax').numpy.asarray(drawn.astype(out[name].dtype))
    for name, factor in factors.items():
        out[name] = (out[name] * factor).astype(out[name].dtype)
    return out
```

```python
import numpy as np
from contextlib import ExitStack

import concourse.bass as bass
from concourse import mybir

F32 = mybir.dt.float32
BF16 = mybir.dt.bfloat16
I32 = mybir.dt.int32
ALU = mybir.AluOpType
ACT = mybir.ActivationFunctionType
AX = mybir.AxisListType.X

P = 128
D = 1024
KD = D // P
SEQ, DB, DS = 512, 8, 8
NS = DB * DS
NT = SEQ + NS
PAST, PAGE = 1024, 128
NPAGE = PAST // PAGE
NPHYS = DB * NPAGE * 5 // 4
LS = PAST + DS
HD, NH, NKV, NI = 64, 8, 4, 8
HALF = HD // 2
TILES = 5
PT_TILES = SEQ // P
SEL_P = min(256, SEQ // 4)
SEL_S = min(256, LS // 4)
WINDOWS = (2, 4, 8, 16)
NG = len(WINDOWS)
HIST = max(WINDOWS) - 1
UW = D // 2
EG, EPG = 4, 8
NE = EG * EPG
DE = D // 2
KE = DE // P
CAP = 64
MAXB = -(-NT // CAP)
NB = MAXB - 1
FIRST = NE * CAP
SLOTS = NE * CAP * MAXB
NEG = 1e30
LOW = -3e38
SCALE = HD ** -0.5
EPS = 1e-6
C_Q, C_K, C_QI, C_KI, C_U, C_GA, C_GB = 0, 512, 1024, 1536, 1608, 2120, 3144
KIW = HD + NI
HN = NT // 2


def rows_of(i):
    return P if i < PT_TILES else NS


def constants():
    parts = {}
    parts["ident"] = np.eye(P)
    pos = np.zeros((TILES, P))
    pos[:PT_TILES] = np.arange(SEQ).reshape(PT_TILES, P)
    pos[PT_TILES, :NS] = PAST + np.arange(NS) % DS
    inv = (np.float32(1) / np.float32(10000.0) ** (np.arange(HALF, dtype=np.float32) / np.float32(HALF))).astype(np.float32)
    ang = (pos.astype(np.float32)[:, :, None] * inv).astype(np.float64)
    for name, t in (("cos", np.cos(ang)), ("nsin", -np.sin(ang)), ("sin", np.sin(ang))):
        parts[name] = t.transpose(1, 0, 2).reshape(P, TILES * HALF)
    t_in, t_out = np.arange(P)[:, None], np.arange(P)[None, :]
    cur, prev, first, new, hist = [], [], [], [], []
    for w in WINDOWS:
        inside = (t_in <= t_out) & (t_in > t_out - w)
        cur.append(inside / w - (t_in == t_out))
        prev.append((t_in - P > t_out - w) / w)
        first.append(inside / np.minimum(t_out + 1, w) - (t_in == t_out))
        b_out, s_out = np.arange(NS)[None, :] // DS, np.arange(NS)[None, :] % DS
        b_in, s_in = np.arange(P)[:, None] // DS, np.arange(P)[:, None] % DS
        new.append(((b_in == b_out) & (s_in <= s_out) & (s_in > s_out - w)) / w
                   - ((b_in == b_out) & (s_in == s_out)))
        b_in, s_in = np.arange(P)[:, None] // HIST, np.arange(P)[:, None] % HIST - HIST
        hist.append(((b_in == b_out) & (s_in > s_out - w)) / w)
    for name, m in (("bandcur", cur), ("bandprev", prev), ("bandfirst", first),
                    ("bandnew", new), ("bandhist", hist)):
        parts[name] = np.concatenate(m, axis=1)
    parts["causal"] = np.where(t_out <= t_in, 0.0, -NEG)
    parts["newcausal"] = np.where(np.arange(DS)[None, :] <= t_in % DS, 0.0, -NEG)
    c = np.arange(P)
    cb, ch, cq = c // (NH * DS), c // DS % NH, c % DS
    parts["headrep"] = (t_in == ch[None, :]) * 1.0
    r = np.arange(NS)
    dmask = [(2 * bp + cb[:, None] == r[None, :] // DS) & (cq[:, None] == r[None, :] % DS) for bp in range(DB // 2)]
    parts["dmask"] = np.concatenate(dmask, axis=1) * 1.0
    expand = np.zeros((P, DB // 2, P))
    for bp in range(DB // 2):
        expand[:NS, bp] = dmask[bp].T
    parts["expand"] = expand.reshape(P, -1)
    parts["tri"] = (t_in < t_out) * 1.0
    parts["ones"] = np.ones((P, P))
    parts["iota"] = np.tile(np.arange(NE), (P, 1))
    parts["base"] = np.tile(np.arange(NE) * CAP, (P, 1))
    parts["jump"] = np.tile(FIRST - CAP + np.arange(NE) * (NB - 1) * CAP, (P, 1))
    parts["lane"] = t_in % (P // NPAGE)
    parts["tok"] = np.arange(TILES)[None, :] * P + t_in
    parts["valid"] = (np.arange(TILES)[None, :] * P + t_in < NT) * 1.0
    where, at = {}, 0
    for name, a in parts.items():
        where[name] = (at, a.shape[1])
        at += a.shape[1]
    return where, np.concatenate([np.asarray(a, np.float32) for a in parts.values()], axis=1)


def program(nc, consts, where, x_prompt, x_sample, cache_k, cache_v, cache_idx_k, state_pool, page_table,
            attn_norm_g, w_in, w_pool, pool_scale, w_branch_attn, w_branch_pool, w_out, ffn_norm_g,
            w_router_group, b_router_group, w_router_expert, b_router_expert,
            w_exp_gate, w_exp_up, w_exp_down, final_norm_g,
            y_prompt, y_sample, nk_prompt, nv_prompt, ni_prompt, np_prompt,
            nk_sample, nv_sample, ni_sample, np_sample):
    x_rows = [x_prompt[0, i * P:(i + 1) * P, :] for i in range(PT_TILES)] + [x_sample.rearrange("b s d -> (b s) d")]
    y_rows = [y_prompt[0, i * P:(i + 1) * P, :] for i in range(PT_TILES)] + [y_sample.rearrange("b s d -> (b s) d")]

    def token_rows(prompt, sample, tail):
        p = prompt[0, 0].rearrange(f"s {tail} -> s ({tail})") if " " in tail else prompt[0, 0]
        s = sample[0].rearrange(f"b s {tail} -> (b s) ({tail})")
        return [p[i * P:(i + 1) * P, :] for i in range(PT_TILES)] + [s]

    nk_rows = token_rows(nk_prompt, nk_sample, "h d")
    nv_rows = token_rows(nv_prompt, nv_sample, "h d")
    ni_rows = token_rows(ni_prompt, ni_sample, "d")
    GR = P // NPAGE
    RP = PAGE // GR
    k_groups = cache_k[0].rearrange("n (g r) h d -> (n g) (r h d)", g=GR)
    v_groups = cache_v[0].rearrange("n (g r) h d -> (n g) (r h d)", g=GR)
    i_groups = cache_idx_k[0].rearrange("n (g r) d -> (n g) (r d)", g=GR)
    w_in_v = w_in[0].rearrange("(k p) n -> p k n", p=P)

    ctx = ExitStack()
    with ctx:
        AW = 53200
        arena = ctx.enter_context(nc.sbuf_tensor("arena", [P, AW], F32))
        psum = ctx.enter_context(nc.psum_tensor("psum", [P, 8 * 512], F32))
        sems = {}

        def sem(name):
            sems[name] = ctx.enter_context(nc.semaphore(name))
            return sems[name]

        def at(off, *dims, rows=P):
            n = int(np.prod(dims))
            assert off + n <= AW, (off, dims)
            v = arena[0:rows, off:off + n]
            if len(dims) == 2:
                return v.rearrange("p (a b) -> p a b", b=dims[1])
            if len(dims) == 3:
                return v.rearrange("p (a b c) -> p a b c", b=dims[1], c=dims[2])
            return v

        def const(name, rows=P):
            o, n = where[name]
            return arena[0:rows, o:o + n]

        def bank(b, n=512, rows=slice(0, P), at0=0):
            return psum[rows, b * 512 + at0:b * 512 + at0 + n]

        cst_w = sum(n for _, n in where.values())
        XNT = 4160
        ATT = XNT + KD * NT
        POT = ATT + 4 * NT
        RING = POT + 4 * NT
        SLOT = KD * 512
        SMALL = RING + 2 * SLOT
        assert cst_w <= XNT - 80
        xnT = at(XNT, KD, NT)
        attnT = at(ATT, 4, NT)
        poT = at(POT, 4, NT)
        ring = [at(RING + s * SLOT, KD, 512) for s in range(2)]
        stats = at(XNT - 64, 64)
        gain1 = stats[:, 0:8]
        gain2 = stats[:, 8:16]
        pscale = stats[:, 16:20]
        ss1, rt1, rstd1 = stats[:, 20:25], stats[:, 25:30], stats[:, 30:35]
        ss2, rt2, rstd2 = stats[:, 35:40], stats[:, 40:45], stats[:, 45:50]
        ss3, rt3, rstd3 = stats[:, 50:55], stats[:, 55:60], stats[:, 20:25]
        eps = stats[:, 60:61]
        o = SMALL
        kiT2 = at(o, NT); o += NT
        vnat = at(o, TILES, NKV * HD); o += TILES * NKV * HD
        kT = at(o, 2, NT); o += 2 * NT
        qs = at(o, DB, 2, 32); o += DB * 64
        wiS = at(o, TILES, NI); o += TILES * NI
        w2T = at(o, NS, rows=NI); o += NS
        expand_b = arena[0:NS, o:o + 256].bitcast(BF16); o += 256
        cols = at(o, 40); o += 40
        kir = at(o, TILES, P); o += TILES * P
        kiraw = at(o, TILES, HD); o += TILES * HD
        raw = [at(o + s * 512, 512) for s in range(2)]; RAW = o; o += 1024
        roped = [at(o + s * 1024, 1024) for s in range(2)]; o += 2048
        rtmp = [at(o + s * 512, 512) for s in range(2)]; o += 1024
        MP = o
        maskp = {i: at(MP + P * (i * (i + 1) // 2 - 1), P * (i + 1)) for i in range(1, PT_TILES)}
        o += P * 9
        msk = arena[0:NS, o:o + LS // 2].bitcast(BF16); o += LS // 2
        QZ = o
        qz = at(o, NH, SEQ)
        idxk = at(o, DB, RP * HD)
        o += NH * SEQ
        ZA = o
        score = {i: at(ZA + P * (i * (i + 1) // 2 - 1), P * (i + 1)) for i in range(1, PT_TILES)}
        o = ZA + P * 9
        sc_s = at(o, LS, rows=NS); o += LS
        work = at(o, LS); o += LS
        gtm = at(o, LS); o += LS
        eqm = at(o, LS); o += LS
        rnk = at(o, LS); o += LS
        ZB = o
        o = ZA
        ml = [at(o + s * 512, 512) for s in range(2)]; o += 1024
        prob = [at(o + s * 512, 512) for s in range(2)]; o += 1024
        probT = [at(o + s * 512, 4, P) for s in range(2)]; o += 1024
        o = ZA
        probs = at(o, LS); o += LS
        probsT = at(o, 9, P); o += 9 * P
        onat = at(o, NKV * HD); o += NKV * HD
        o = max(o, ZA + 3072)
        kTb1 = at(o, 2, LS); o += 2 * LS
        assert o <= ZB
        o = ZB
        xin = [at(ZB + i * D, D) for i in range(TILES)]
        qiz = [at(o + s * 1024, NI, P) for s in range(2)]; o += 2048
        qlo = at(o, DB, 64); o += 512
        qhi = at(o, DB, 64); o += 512
        kst = at(o, 2, 512); o += 1024
        rls = at(o, LS); o += LS
        wl = at(o, DB // 2, NS); o += DB // 2 * NS
        rl = [at(o + s * 512, 512) for s in range(2)]; o += 1024
        xs = [at(o + s * D, D) for s in range(2)]
        unat = at(o, TILES, UW)
        o += 2560
        kiww = at(o, KD, KIW); o += KD * KIW
        hist = at(o, UW); o += UW
        wpool = at(o, NG, P); o += NG * P
        assert o <= AW
        kb = at(ZB, 2, RP * 256)
        vb = at(ZB + 4096, 2, RP * 256)
        kTb = [at(ZB + 8192, 2, LS), kTb1]
        vnew = at(RAW, DB, 256, rows=DS)
        pgi = at(XNT - 80, 8).bitcast(I32)
        gidx = at(XNT - 72, 8).bitcast(I32)
        dT = attnT
        rmax, nmax, esum, rsum = (cols[:, 4 * j:4 * j + 4] for j in range(4))
        smax, snmax, ssum, srec = (cols[:, 25 + j:26 + j] for j in range(4))
        o = SMALL
        SG = o
        sgA = at(o, KD, NT); o += KD * NT
        sgB = at(o, KD, NT); o += KD * NT
        W0 = o; o += 12288
        resid = at(o, TILES, D); o += TILES * D
        g2row = at(o, D); o += D
        fgrow = at(o, D); o += D
        wr = at(o, KD, P); o += KD * P
        rbias = at(o, EG + NE); o += EG + NE
        lg = at(o, TILES, EG + NE); o += TILES * (EG + NE)
        RT = o
        t32 = [at(o + j * 160, TILES, NE) for j in range(5)]; o += 800
        gmax, least, top1, top2, vdf, vex, gw, s2, w1, w2 = (at(o + j * TILES, TILES) for j in range(10)); o += 10 * TILES
        ghot, gsh, gex = (at(o + j * TILES * EG, TILES, EG) for j in range(3)); o += 3 * TILES * EG
        ab = at(o, 80).bitcast(BF16).rearrange("p (t e) -> p t e", e=NE); o += 80
        dest = arena[:, o:o + 2 * TILES].bitcast(I32).rearrange("p (k t) -> p k t", t=TILES); o += 2 * TILES
        toki = arena[:, o:o + TILES].bitcast(I32); o += TILES
        flag = arena[:, o:o + 1].bitcast(I32); o += 1
        assert o <= AW, o
        xs2 = [at(XNT + s * D, D) for s in range(2)]
        xn2 = [at(XNT + 2 * D + s * D, D) for s in range(2)]
        xn2T = [at(ATT + s * D, KD, P) for s in range(2)]
        W1 = SMALL - 12288
        assert W1 >= ATT
        o = SG
        xg = [at(o + s * D, D, rows=CAP) for s in range(2)]; o += 2 * D
        xT = [at(o + s * 512, KD, CAP) for s in range(2)]; o += 1024
        sg = [at(o + s * 512, DE, rows=CAP) for s in range(2)]; o += 1024
        hb = [at(o + s * 512, DE, rows=CAP) for s in range(2)]; o += 1024
        hT = [at(o + s * 256, KE, CAP) for s in range(2)]; o += 512
        yo = [at(o + s * 512, 512) for s in range(2)]; o += 1024
        sidx = [arena[0:CAP, o + s:o + s + 1].bitcast(I32) for s in range(2)]; o += 2
        trib = at(o, 64).bitcast(BF16); o += 64
        oneb = at(o, 64).bitcast(BF16); o += 64
        assert o <= W0
        wg = [at(b, KD, DE) for b in (W0, W1)]
        wu = [at(b + 4096, KD, DE) for b in (W0, W1)]
        wd = [at(b + 8192, KE, D) for b in (W0, W1)]
        zeros = at(W1, 8 * D)
        YZ = (SLOTS - FIRST) // (8 * P)
        yg = [[at(W0 + (2 * s + k) * D, D) for k in range(2)] for s in range(2)]
        yout = [at(W0 + (4 + s) * D, D) for s in range(2)]

        xn2_d = nc.dram_tensor("xn2_d", (NT, D), F32, kind="Internal").ap()
        tab_d = nc.dram_tensor("tab_d", (SLOTS, 1), I32, kind="Internal").ap()
        y_d = nc.dram_tensor("y_d", (SLOTS, D), F32, kind="Internal").ap()

        ident = const("ident")
        tab3 = {n: const(n).rearrange("p (t c) -> p t c", c=HALF) for n in ("cos", "nsin", "sin")}
        band = {n: const(n).rearrange("p (g c) -> p g c", g=NG)
                for n in ("bandcur", "bandprev", "bandfirst", "bandnew", "bandhist")}
        dmask = const("dmask").rearrange("p (b c) -> p b c", c=NS)
        expand_f = const("expand", NS)

        S = {n: sem(n) for n in ("""
            const_in page_in gain_in kiww_in hist_in wpool_in vnew_in late_in st_ready
            gi_ready sq_done rt_done rstd_ready xs_ready xt_done xn_ready
            jp je ki_roped rope_done tp te qiz_zero qz_zero qs_zero wr_zero
            wi_done wl_ready is_done rl_ready acc_done ss_done ss_relu sw_done acc_ev 
            ki_out v_out u_out hist_out dt_done dt_ev po_done po_ev
            lg_done ml_done mx_done ex_done pn_done pv_done ot_ev mask_s ebf_ready
            sl_done smx_done sex_done srec_done spv_done son_done sot_done sot_ev knew_ev att_all
            g_done gate_ev br_ev m_done h_done h_add sq2 rt2 rs2 xs2_r x2t x2e xn2_r r_done r_add
            gexp_in gexp_out tri_ready a_ready rank_done flag_ready zero_st zero_w dest_ready sc_st
            y_comb sq3 rt3 rs3 fin_ready dvc plc passed y_zero""").split()}
        s_x = [sem(f"x_in{i}") for i in range(TILES)]
        s_res = sem("resid_in")
        s_ring = [sem(f"ring_in{s}") for s in range(2)]
        s_rs = [sem(f"roped_stored{s}") for s in range(2)]
        s_idx = sem("idxpage_in")
        s_kin = [sem(f"kpage_in{b}") for b in range(2)]
        s_vin = [sem(f"vpage_in{b}") for b in range(2)]
        s_xst = [sem(f"xn2_stored{s}") for s in range(2)]
        s_ygi = [[sem(f"ygather{s}{k}") for k in range(2)] for s in range(2)]
        s_yw = [sem(f"yout_stored{s}") for s in range(2)]
        M = [{n: sem(f"{n}{s}") for n in
              ("wg_in wu_in wd_in sidx_in xg_in xt_done xt_ev gu_done silu h_ready "
               "ht_done ht_ev y_done y_ev y_st").split()} for s in range(2)]
        OV, N0 = M[0], NE // 2

        RING_LOADS = [w_in_v[:, :, c:c + 512] for c in (C_QI, C_Q, C_K, C_U)]
        for mg in range(2):
            RING_LOADS += [w_in_v[:, :, C_GA + 512 * mg:C_GA + 512 * mg + 512],
                           w_in_v[:, :, C_GB + 512 * mg:C_GB + 512 * mg + 512], ("branch", mg)]
        w_out_v = w_out[0].rearrange("(k p) n -> p k n", p=P)
        RING_LOADS += [w_out_v[:, :, 0:512], w_out_v[:, :, 512:1024]]
        R_QI, R_Q, R_KV, R_U, R_GATES, R_OUT = 0, 1, 2, 3, 4, 10
        ring_total = [0, 0]
        RING_AT = []
        for n, what in enumerate(RING_LOADS):
            ring_total[n % 2] += 32 if isinstance(what, tuple) else 16
            RING_AT.append(ring_total[n % 2])

        RING_USED = [(S["jp"], v) for v in (9, 14, 19, 24)] + [(S["g_done"], v) for v in (8, 16, 32, 40, 48, 64)]

        QI_ORDER = [1, 2, 3, 4]
        JOBS = [("qi", i) for i in QI_ORDER] + [("q", i) for i in range(TILES)] + [("k", i) for i in range(TILES)]
        T_JOB = [3, 4, 5, 6] + list(range(15, 25))
        T0 = T_JOB[-1]
        stored = {s: 0 for s in range(2)}
        STORED_AT = []
        for n, (kind, _) in enumerate(JOBS):
            if kind == "k":
                stored[n % 2] += 16
            STORED_AT.append(stored[n % 2])

        def stores_done(eng):
            eng.wait_ge(S["ki_out"], 16 * TILES)
            eng.wait_ge(S["v_out"], 16 * TILES)
            eng.wait_ge(S["u_out"], 32)
            for s in range(2):
                eng.wait_ge(s_rs[s], stored[s])

        block = ctx.enter_context(nc.Block())

        @block.sync
        def _(sp):
            sp.dma_start(arena[:, 0:cst_w], consts).then_inc(S["const_in"], 16)
            with nc.allow_non_contiguous_dma(reason="a few small columns"):
                for j in range(NPAGE):
                    src = page_table[:, j:j + 1].rearrange("b j -> j b").to_broadcast([GR, DB])
                    sp.dma_start(pgi[GR * j:GR * (j + 1), :], src).then_inc(S["page_in"], 16)
                for i in range(TILES):
                    sp.dma_start(xin[i][0:rows_of(i), :], x_rows[i]).then_inc(s_x[i], 16)
                sp.dma_start(gain1, attn_norm_g[0].rearrange("(k p) -> p k", p=P)).then_inc(S["gain_in"], 16)
                sp.dma_start(pscale, pool_scale[0].rearrange("(k p) -> p k", p=P)).then_inc(S["gain_in"], 16)
                sp.dma_start(gain2, ffn_norm_g[0].rearrange("(k p) -> p k", p=P)).then_inc(S["gain_in"], 16)
                sp.dma_start(kiww, w_in_v[:, :, C_KI:C_KI + KIW]).then_inc(S["kiww_in"], 16)

            def load_ring(n):
                if n >= 2:
                    sp.wait_ge(*RING_USED[n - 2])
                s, what = n % 2, RING_LOADS[n]
                if isinstance(what, tuple):
                    c = slice(512 * what[1], 512 * what[1] + 512)
                    sp.dma_start(ring[s][:, 0:4, :], w_branch_attn[0].rearrange("(k p) n -> p k n", p=P)[:, :, c]).then_inc(s_ring[s], 16)
                    sp.dma_start(ring[s][:, 4:8, :], w_branch_pool[0].rearrange("(k p) n -> p k n", p=P)[:, :, c]).then_inc(s_ring[s], 16)
                else:
                    sp.dma_start(ring[s], what).then_inc(s_ring[s], 16)

            load_ring(0)
            sp.dma_start(hist[0:DB * HIST, :], state_pool[0].rearrange("b t c -> (b t) c")).then_inc(S["hist_in"], 16)
            sp.dma_start(wpool, w_pool[0].rearrange("g c d -> c g d")).then_inc(S["wpool_in"], 16)
            sp.dma_start(np_sample[0, :, 0:HIST - DS, :], state_pool[0, :, DS:HIST, :]).then_inc(S["hist_out"], 16)
            for n in range(1, 5):
                load_ring(n)
            sp.wait_ge(S["je"], 19)
            sp.wait_ge(S["tp"], T_JOB[-1])
            for s in range(2):
                sp.wait_ge(s_rs[s], stored[s])
            for b in range(DB):
                sp.dma_start(vnew[:, b, :], vnat[b * DS:(b + 1) * DS, PT_TILES, :]).then_inc(S["vnew_in"], 16)
            load_ring(5)
            sp.wait_ge(S["att_all"], 1)
            stores_done(sp)
            load_ring(6)
            load_ring(7)
            for i in range(TILES):
                sp.dma_start(resid[0:rows_of(i), i, :], x_rows[i]).then_inc(s_res, 16)
            with nc.allow_non_contiguous_dma(reason="router weights and rows for all partitions"):
                sp.dma_start(g2row, ffn_norm_g.to_broadcast([P, D])).then_inc(S["late_in"], 16)
                sp.dma_start(fgrow, final_norm_g.unsqueeze(0).to_broadcast([P, D])).then_inc(S["late_in"], 16)
                sp.dma_start(rbias[:, 0:EG], b_router_group.to_broadcast([P, EG])).then_inc(S["late_in"], 16)
                sp.dma_start(rbias[:, EG:], b_router_expert.to_broadcast([P, NE])).then_inc(S["late_in"], 16)
                sp.wait_ge(S["wr_zero"], 1)
                sp.dma_start(wr[:, :, 0:EG], w_router_group[0].rearrange("(k p) n -> p k n", p=P)).then_inc(S["late_in"], 16)
                sp.dma_start(wr[:, :, EG:EG + NE], w_router_expert[0].rearrange("(k p) n -> p k n", p=P)).then_inc(S["late_in"], 16)
            g_v = w_exp_gate[0].rearrange("e (p k) n -> e p (k n)", k=KD)
            u_v = w_exp_up[0].rearrange("e (p k) n -> e p (k n)", k=KD)
            d_v = w_exp_down[0].rearrange("e (p k) n -> e p (k n)", k=KE)

            def flat(t):
                return t.rearrange("p k n -> p (k n)")

            def load_expert(i, s):
                e = 2 * i + s
                m = M[s]
                if not isinstance(i, int):
                    sp.wait_ge(m["gu_done"], i)
                sp.dma_start(flat(wg[s]), g_v[bass.ds(e, 1), :, :].squeeze(0) if not isinstance(e, int) else g_v[e]).then_inc(m["wg_in"], 16)
                sp.dma_start(flat(wu[s]), u_v[bass.ds(e, 1), :, :].squeeze(0) if not isinstance(e, int) else u_v[e]).then_inc(m["wu_in"], 16)
                if not isinstance(i, int):
                    sp.wait_ge(m["y_done"], i)
                sp.dma_start(flat(wd[s]), d_v[bass.ds(e, 1), :, :].squeeze(0) if not isinstance(e, int) else d_v[e]).then_inc(m["wd_in"], 16)

            load_expert(0, 0)
            for n in range(8, len(RING_LOADS)):
                load_ring(n)
            sp.wait_ge(S["r_done"], TILES)
            load_expert(0, 1)
            with sp.Fori(1, NE // 2) as i:
                for s in range(2):
                    load_expert(i, s)
            sp.wait_ge(S["flag_ready"], 1)
            over = sp.value_load(flag[0:1, 0:1], min_val=0, max_val=NT)
            with sp.If(over > CAP):
                with sp.Fori(0, NE) as e:
                    sp.wait_ge(OV["y_done"], e * NB + N0)
                    sp.dma_start(flat(wg[0]), g_v[bass.ds(e, 1), :, :].squeeze(0)).then_inc(OV["wg_in"], 16)
                    sp.dma_start(flat(wu[0]), u_v[bass.ds(e, 1), :, :].squeeze(0)).then_inc(OV["wu_in"], 16)
                    sp.dma_start(flat(wd[0]), d_v[bass.ds(e, 1), :, :].squeeze(0)).then_inc(OV["wd_in"], 16)
            with sp.Else():
                sp.nop()
            for i in range(TILES):
                sp.wait_ge(S["fin_ready"], i + 1)
                sp.dma_start(y_rows[i], yout[i % 2][0:rows_of(i), :]).then_inc(s_yw[i % 2], 16)
            sp.wait_ge(s_yw[0], 48)
            sp.wait_ge(s_yw[1], 32)
            sp.wait_ge(S["hist_out"], 16)
            stores_done(sp)

        @block.tensor
        def _(pe):
            jn, tn = [0], [0]

            def j_bank():
                if jn[0] >= 2:
                    pe.wait_ge(S["je"], jn[0] - 1)
                jn[0] += 1
                return 2 + (jn[0] - 1) % 2

            def t_bank():
                if tn[0] >= 2:
                    pe.wait_ge(S["te"], tn[0] - 1)
                tn[0] += 1
                return (tn[0] - 1) % 2

            pe.wait_ge(S["const_in"], 16)
            for i in range(TILES):
                r = rows_of(i)
                pe.wait_ge(S["xs_ready"], i + 1)
                for half in range(2):
                    g = 2 * i + half
                    if g >= 2:
                        pe.wait_ge(S["xn_ready"], g - 1)
                    for k in range(4):
                        kk = 4 * half + k
                        last = pe.transpose(bank(g % 2, r, at0=k * P), xs[i % 2][0:r, kk * P:(kk + 1) * P], ident[0:r, 0:r])
                    last.then_inc(S["xt_done"], 1)

            def project(i, w, n):
                r = rows_of(i)
                b = j_bank()
                for k in range(KD):
                    last = pe.matmul(bank(b, n, slice(0, r)), xnT[:, k, i * P:i * P + r], w[:, k, 0:n],
                                     start=(k == 0), stop=(k == KD - 1))
                last.then_inc(S["jp"], 1)

            def ring_ready(n):
                pe.wait_ge(s_ring[n % 2], RING_AT[n])

            pe.wait_ge(S["kiww_in"], 16)
            for i in range(TILES):
                pe.wait_ge(S["xn_ready"], 2 * (i + 1))
                project(i, kiww, KIW)
            ring_ready(R_QI)
            project(QI_ORDER[0], ring[0], 512)
            pe.wait_ge(S["ki_roped"], PT_TILES)
            b = t_bank()
            for i in range(PT_TILES):
                last = pe.transpose(bank(b, P, at0=i * P), kir[:, i, :], ident)
            last.then_inc(S["tp"], 1)
            pe.wait_ge(S["ki_roped"], TILES)
            b = t_bank()
            pe.transpose(bank(b, NS), kir[0:NS, PT_TILES, :], ident[0:NS, 0:NS])
            pe.wait_ge(S["je"], TILES)
            pe.transpose(bank(b, NS, slice(0, NI), at0=NS), wiS[0:NS, PT_TILES, :], ident[0:NS, 0:NS]).then_inc(S["tp"], 1)

            def turn(job, n_blocks, rows, width):
                pe.wait_ge(S["rope_done"], job + 1)
                b = t_bank()
                for k in range(n_blocks):
                    last = pe.transpose(bank(b, rows, at0=k * width), roped[job % 2][0:rows, k * P:(k + 1) * P], ident[0:rows, 0:rows])
                last.then_inc(S["tp"], 1)

            def index_prompt(j):
                i = QI_ORDER[j]
                L = P * (i + 1)
                for h in range(NI):
                    u = j * NI + h
                    if h == 0:
                        pe.wait_ge(S["te"], tn[0])
                    if u >= 2:
                        pe.wait_ge(S["rl_ready"], u - 1)
                    pe.matmul(bank(4 + u % 2, L), qiz[j % 2][:, h, :], kiT2[:, 0:L], start=True, stop=True).then_inc(S["is_done"], 1)

            for j in range(3):
                project(QI_ORDER[j + 1], ring[0], 512)
                turn(j, 4, P, P)
                index_prompt(j)
            turn(3, 8, NS, NS)
            pe.wait_ge(S["te"], tn[0])
            pe.wait_ge(S["rl_ready"], 3 * NI)
            pe.matmul(bank(6, NS), const("headrep", NI), w2T, start=True, stop=True).then_inc(S["wi_done"], 1)
            pe.wait_ge(S["je"], jn[0])
            pe.wait_ge(S["wl_ready"], 1)
            for bp in range(DB // 2):
                for b2 in range(2):
                    if bp == b2 == 0:
                        pe.wait_ge(s_idx, 16 * DB)
                    b = t_bank()
                    for rr in range(4):
                        last = pe.transpose(bank(b, P, at0=rr * P), idxk[:, 2 * bp + b2, rr * P:(rr + 1) * P], ident)
                    last.then_inc(S["tp"], 1)
                if bp:
                    pe.wait_ge(S["ss_relu"], bp)
                pe.wait_ge(S["te"], tn[0])
                for par, q in enumerate((qlo, qhi)):
                    for b2 in range(2):
                        pe.matmul(bank(4 + par, 512, slice(64 * b2, 64 * b2 + 64)), q[:, 2 * bp + b2, :], kst[:, b2, :], start=True, stop=True)
                for b2 in range(2):
                    bb = 2 * bp + b2
                    last = pe.matmul(bank(6, DS, slice(64 * b2, 64 * b2 + 64)), qlo[:, bb, :],
                                     kiT2[:, SEQ + bb * DS:SEQ + (bb + 1) * DS], start=True, stop=True)
                last.then_inc(S["ss_done"], 1)
                pe.wait_ge(S["ss_relu"], bp + 1)
                for c, (b, n) in enumerate(((2, 512), (3, 512), (7, DS))):
                    last = pe.matmul(bank(b, n, slice(0, NS)), wl[:, bp, :], rls[:, 512 * c:512 * c + n],
                                     start=(bp == 0), stop=(bp == DB // 2 - 1), skip_group_check=True)
                last.then_inc(S["sw_done"], 1)
            pe.wait_ge(S["acc_ev"], 3)
            for what, slot, first in (("q", R_Q, 4), ("k", R_KV, 9)):
                ring_ready(slot)
                for i in range(TILES):
                    project(i, ring[slot % 2], 512)
                    if i:
                        turn(first + i - 1, 4 if what == "q" else 2, rows_of(i - 1), P)
                if what == "q":
                    turn(first + TILES - 1, 8, NS, NS)
                else:
                    turn(first + TILES - 1, 2, NS, P)
            ring_ready(R_U)
            for i in range(TILES):
                project(i, ring[R_U % 2], 512)
            pe.wait_ge(S["hist_in"], 16)
            for i in range(TILES):
                r = rows_of(i)
                pe.wait_ge(S["je"], jn[0] - TILES + i + 1)
                if i >= 2:
                    pe.wait_ge(S["dt_ev"], i - 1)
                for g in range(NG):
                    out = bank(4 + i % 2, r, at0=g * P)
                    c = slice(g * P, (g + 1) * P)
                    if i == 0:
                        last = pe.matmul(out, unat[:, 0, c], band["bandfirst"][:, g, :], start=True, stop=True)
                    elif i < PT_TILES:
                        pe.matmul(out, unat[:, i - 1, c], band["bandprev"][:, g, :], start=True, stop=False)
                        last = pe.matmul(out, unat[:, i, c], band["bandcur"][:, g, :], start=False, stop=True)
                    else:
                        pe.matmul(out, hist[0:DB * HIST, c], band["bandhist"][0:DB * HIST, g, :], start=True, stop=False)
                        last = pe.matmul(out, unat[0:NS, i, c], band["bandnew"][0:NS, g, :], start=False, stop=True)
                last.then_inc(S["dt_done"], 1)
            pe.wait_ge(S["dt_ev"], TILES)
            pe.wait_ge(S["wpool_in"], 16)
            for g in range(NG):
                if g:
                    pe.wait_ge(S["po_ev"], g)
                pe.matmul(bank(6), wpool[:, g, :], dT[:, g, 0:SEQ], start=True, stop=True)
                pe.matmul(bank(7, NS), wpool[:, g, :], dT[:, g, SEQ:NT], start=True, stop=True).then_inc(S["po_done"], 1)
            units = [(i, h) for i in range(PT_TILES) for h in range(NH)]
            U = len(units)
            pe.wait_ge(S["po_ev"], NG)
            pe.wait_ge(S["te"], tn[0])
            t0 = tn[0]
            for u in range(U + 2):
                if u < U:
                    i, h = units[u]
                    if u >= 2:
                        pe.wait_ge(S["ml_done"], u - 1)
                    pe.matmul(bank(4 + u % 2, P * (i + 1)), qz[:, h, i * P:(i + 1) * P], kT[:, h // 4, 0:P * (i + 1)],
                              start=True, stop=True).then_inc(S["lg_done"], 1)
                if 1 <= u <= U:
                    i, h = units[u - 1]
                    pe.wait_ge(S["pn_done"], u)
                    b = t_bank()
                    for j in range(i + 1):
                        last = pe.transpose(bank(b, P, at0=j * P), prob[(u - 1) % 2][:, j * P:(j + 1) * P], ident)
                    last.then_inc(S["tp"], 1)
                if u >= 2:
                    v = u - 2
                    i, h = units[v]
                    pe.wait_ge(S["te"], t0 + v + 1)
                    if h % 2 == 0 and v >= 4:
                        pe.wait_ge(S["ot_ev"], v // 2 - 1)
                    half = slice(64 * (h % 2), 64 * (h % 2) + 64)
                    for j in range(i + 1):
                        last = pe.matmul(bank(6 + (v // 2) % 2, P, half), vnat[:, j, (h // 2) * HD:(h // 2 + 1) * HD],
                                         probT[v % 2][:, j, :], start=(j == 0), stop=(j == i))
                    last.then_inc(S["pv_done"], 1)
            pe.wait_ge(S["ot_ev"], U // 2)
            pe.wait_ge(S["vnew_in"], 16 * DB)
            pe.wait_ge(S["ebf_ready"], 1)
            pe.wait_ge(S["mask_s"], 1)
            for bp in range(DB // 2):
                for b2 in range(2):
                    pe.wait_ge(s_kin[b2], 16 * (bp + 1))
                    for pr in range(2):
                        for rh in range(2):
                            b = t_bank()
                            for r in range(4):
                                c = (4 * rh + r) * 256 + pr * P
                                last = pe.transpose(bank(b, P, at0=r * P), kb[:, b2, c:c + P], ident)
                            last.then_inc(S["tp"], 1)
                pe.wait_ge(S["te"], tn[0])
                pe.wait_ge(S["knew_ev"], bp + 1)
                if bp:
                    pe.wait_ge(S["sex_done"], bp)
                for c, n in enumerate((512, 512, DS)):
                    cs = slice(512 * c, 512 * c + n)
                    pe.matmul(bank(4 + c, n), expand_b[:, bp * P:(bp + 1) * P], msk[:, cs], start=True, stop=False, skip_group_check=True)
                    for b2 in range(2):
                        for pr in range(2):
                            at_row = 64 * b2 + 32 * pr
                            last = pe.matmul(bank(4 + c, n, slice(at_row, at_row + 32)), qs[:, 2 * bp + b2, pr, :], kTb[b2][:, pr, cs],
                                             start=False, stop=True, skip_group_check=True, tile_position=(0, at_row))
                last.then_inc(S["sl_done"], 1)
                pe.wait_ge(S["sex_done"], bp + 1)
                for g in range(2):
                    b = t_bank()
                    for r in range(4):
                        last = pe.transpose(bank(b, P, at0=r * P), probs[:, (4 * g + r) * P:(4 * g + r + 1) * P], ident)
                    last.then_inc(S["tp"], 1)
                b = t_bank()
                pe.transpose(bank(b, P, slice(0, DS)), probs[:, PAST:LS], ident).then_inc(S["tp"], 1)
                pe.wait_ge(S["te"], tn[0])
                if bp:
                    pe.wait_ge(S["son_done"], bp)
                for b2 in range(2):
                    pe.wait_ge(s_vin[b2], 16 * (bp + 1))
                    rows = slice(64 * b2, 64 * b2 + 64)
                    for r in range(RP):
                        pe.matmul(bank(7, 256, rows), probsT[:, r, 64 * b2:64 * b2 + 64], vb[:, b2, r * 256:(r + 1) * 256],
                                  start=(r == 0), stop=False)
                    last = pe.matmul(bank(7, 256, rows), probsT[0:DS, RP, 64 * b2:64 * b2 + 64], vnew[:, 2 * bp + b2, :],
                                     start=False, stop=True)
                last.then_inc(S["spv_done"], 1)
                pe.wait_ge(S["son_done"], bp + 1)
                if bp:
                    pe.wait_ge(S["sot_ev"], bp)
                for pr in range(2):
                    last = pe.transpose(bank(3, P, at0=pr * P), onat[:, pr * P:(pr + 1) * P], ident)
                last.then_inc(S["sot_done"], 1)
            pe.wait_ge(S["sot_ev"], DB // 2)
            pe.sem_inc(S["att_all"], 1)
            evs = []
            counts = {"gate_ev": 0, "br_ev": 0}

            def g_bank():
                n = len(evs)
                if n >= 4:
                    name, v = evs[n - 4]
                    pe.wait_ge(S[name], v)
                return 4 + n % 4

            def g_evac(name):
                counts[name] += 1
                evs.append((name, counts[name]))

            for p6 in range(6):
                slot = R_GATES + p6
                ring_ready(slot)
                w = ring[slot % 2]
                for m in range(4):
                    for hh in range(2):
                        tc = slice(HN * hh, HN * hh + HN)
                        if p6 % 3 < 2:
                            b = g_bank()
                            for k in range(KD):
                                last = pe.matmul(bank(b, HN), w[:, k, m * P:(m + 1) * P], xnT[:, k, tc], start=(k == 0), stop=(k == KD - 1))
                            last.then_inc(S["g_done"], 1)
                            g_evac("gate_ev")
                        else:
                            for br, src in enumerate((attnT, poT)):
                                b = g_bank()
                                for k in range(4):
                                    last = pe.matmul(bank(b, HN), w[:, 4 * br + k, m * P:(m + 1) * P], src[:, k, tc], start=(k == 0), stop=(k == 3))
                                last.then_inc(S["g_done"], 1)
                                g_evac("br_ev")
            ring_ready(R_OUT)
            ring_ready(R_OUT + 1)
            pe.wait_ge(S["m_done"], KD * 2)
            pe.wait_ge(S["late_in"], 96)

            def out_proj(i):
                r = rows_of(i)
                if i >= 2:
                    pe.wait_ge(S["h_add"], i - 1)
                for half in range(2):
                    for k in range(KD):
                        last = pe.matmul(bank(4 + 2 * (i % 2) + half, 512, slice(0, r)), sgA[:, k, i * P:i * P + r], ring[half][:, k, :],
                                         start=(k == 0), stop=(k == KD - 1))
                last.then_inc(S["h_done"], 1)

            def route(i):
                r = rows_of(i)
                pe.wait_ge(S["xs2_r"], i + 1)
                for half in range(2):
                    g = 2 * i + half
                    if g >= 2:
                        pe.wait_ge(S["x2e"], g - 1)
                    for k in range(4):
                        kk = 4 * half + k
                        last = pe.transpose(bank(g % 2, r, at0=k * P), xs2[i % 2][0:r, kk * P:(kk + 1) * P], ident[0:r, 0:r])
                    last.then_inc(S["x2t"], 1)
                pe.wait_ge(S["x2e"], 2 * i + 2)
                if i >= 2:
                    pe.wait_ge(S["r_add"], i - 1)
                for k in range(KD):
                    last = pe.matmul(bank(2 + i % 2, P, slice(0, r)), xn2T[i % 2][:, k, 0:r], wr[:, k, :], start=(k == 0), stop=(k == KD - 1))
                last.then_inc(S["r_done"], 1)

            for i in range(TILES):
                out_proj(i)
                if i:
                    route(i - 1)
            route(TILES - 1)
            pe.wait_ge(S["a_ready"], 1)
            pe.wait_ge(S["tri_ready"], 1)
            pe.wait_ge(S["h_add"], TILES)
            for i in range(TILES + 1):
                for j in range(min(i, TILES - 1) + 1):
                    lhs = trib if j == i else oneb
                    last = pe.matmul(bank(4, NE, at0=i * NE), lhs, ab[:, j, :], start=(j == 0), stop=(j == min(i, TILES - 1)))
            last.then_inc(S["rank_done"], 1)

            def block_(m, s, n, waits, W):
                pe.wait_ge(m["xg_in"], 16 * (n + 1))
                pe.sem_inc(S["passed"], 1)
                for k in range(KD):
                    last = pe.transpose(bank(0, CAP, at0=k * CAP), xg[s][:, k:KD * (P - 1) + k + 1:KD], ident[0:CAP, 0:CAP])
                last.then_inc(m["xt_done"], 1)
                pe.wait_ge(m["xt_ev"], n + 1)
                waits(0)
                for k in range(KD):
                    for half, w in enumerate((wg[W], wu[W])):
                        last = pe.matmul(bank(2 + s, 512, slice(64 * half, 64 * half + 64)), xT[s][:, k, :], w[:, k, :],
                                         start=(k == 0), stop=(k == KD - 1))
                last.then_inc(m["gu_done"], 1)
                pe.wait_ge(m["h_ready"], n + 1)
                pe.sem_inc(S["passed"], 1)
                for k in range(KE):
                    last = pe.transpose(bank(1, CAP, at0=k * CAP), hb[s][:, k:KE * (P - 1) + k + 1:KE], ident[0:CAP, 0:CAP])
                last.then_inc(m["ht_done"], 1)
                pe.wait_ge(m["ht_ev"], n + 1)
                waits(1)
                for k in range(KE):
                    for half in range(2):
                        last = pe.matmul(bank(4 + s, 512, slice(64 * half, 64 * half + 64)), hT[s][:, k, :], wd[W][:, k, 512 * half:512 * half + 512],
                                         start=(k == 0), stop=(k == KE - 1))
                last.then_inc(m["y_done"], 1)

            def weights_in(stage, m, n):
                for name in (("wg_in", "wu_in"), ("wd_in",))[stage]:
                    pe.wait_ge(m[name], 16 * (n + 1))

            def expert_pair(i):
                for s in range(2):
                    block_(M[s], s, i, lambda stage: weights_in(stage, M[s], i), s)

            expert_pair(0)
            with pe.Fori(1, NE // 2) as i:
                expert_pair(i)
            pe.wait_ge(S["flag_ready"], 1)
            over = pe.value_load(flag[0:1, 0:1], min_val=0, max_val=NT)
            with pe.If(over > CAP):
                with pe.Fori(0, NE) as e:
                    with pe.Fori(0, NB) as b:
                        block_(OV, 0, e * NB + b + N0, lambda stage: weights_in(stage, OV, e + N0), 0)
            with pe.Else():
                pe.nop()

        @block.scalar
        def _(act):
            tn = [0]

            def turned(*copies):
                tn[0] += 1
                act.wait_ge(S["tp"], tn[0])
                b = (tn[0] - 1) % 2
                for out, src in copies:
                    last = act.copy(out, src(b))
                last.then_inc(S["te"], 1)

            act.wait_ge(S["st_ready"], 1)
            for i in range(TILES):
                r = rows_of(i)
                act.wait_ge(s_x[i], 16)
                if i >= 2:
                    act.wait_ge(S["sq_done"], i - 1)
                act.activation(psum[0:r, (4 + 2 * (i % 2)) * 512:(4 + 2 * (i % 2)) * 512 + D], xin[i][0:r, :], ACT.Square,
                               accum_out=ss1[0:r, i:i + 1]).then_inc(S["sq_done"], 1)
            act.wait_ge(S["sq_done"], TILES)
            act.activation(rt1, ss1, ACT.Sqrt, bias=eps, scale=1.0 / D).then_inc(S["rt_done"], 1)
            act.wait_ge(S["rstd_ready"], 1)
            for i in range(TILES):
                r = rows_of(i)
                if i >= 2:
                    act.wait_ge(S["xt_done"], 2 * (i - 1))
                act.activation(xs[i % 2][0:r, :], xin[i][0:r, :], ACT.Copy, scale=rstd1[0:r, i:i + 1]).then_inc(S["xs_ready"], 1)
            for i in range(TILES):
                r = rows_of(i)
                act.wait_ge(S["jp"], i + 1)
                act.copy(kiraw[0:r, i, :], bank(2 + i % 2, HD, slice(0, r)))
                act.activation(wiS[0:r, i, :], bank(2 + i % 2, NI, slice(0, r), HD), ACT.Copy,
                               scale=float(HD ** -0.5 * NI ** -0.5)).then_inc(S["je"], 1)

            def take_raw(job, jnum, n):
                r = rows_of(JOBS[job][1])
                act.wait_ge(S["jp"], jnum)
                if job >= 2:
                    act.wait_ge(S["rope_done"], job - 1)
                b = 2 + (jnum - 1) % 2
                last = act.copy(raw[job % 2][0:r, 0:n], bank(b, n, slice(0, r)))
                if JOBS[job][0] == "k":
                    last = act.copy(vnat[0:r, JOBS[job][1], :], bank(b, NKV * HD, slice(0, r), n))
                last.then_inc(S["je"], 1)

            take_raw(0, 6, 512)
            turned((kiT2[:, 0:SEQ], lambda b: bank(b)))
            turned((kiT2[:, SEQ:NT], lambda b: bank(b, NS)), (w2T, lambda b: bank(b, NS, slice(0, NI), NS)))
            act.wait_ge(S["qiz_zero"], 1)
            for j in range(3):
                take_raw(j + 1, 7 + j, 512)
                if j >= 2:
                    act.wait_ge(S["is_done"], (j - 1) * NI)
                pairs = qiz[j % 2].rearrange("p (k a) t -> p k a t", a=2)
                turned(*[(pairs[64 * a:64 * a + 64, :, a, :],
                          lambda b, a=a: bank(b, 512, slice(64 * a, 64 * a + 64)).rearrange("p (k t) -> p k t", t=P))
                         for a in range(2)])
                L = P * (QI_ORDER[j] + 1)
                for h in range(NI):
                    u = j * NI + h
                    act.wait_ge(S["is_done"], u + 1)
                    if u >= 2:
                        act.wait_ge(S["acc_done"], u - 1)
                    act.activation(rl[u % 2][:, 0:L], bank(4 + u % 2, L), ACT.Relu).then_inc(S["rl_ready"], 1)
            turned(*[(q[64 * a:64 * a + 64].rearrange("p b (h q) -> p b h q", q=DS),
                      lambda b, a=a: bank(b, 512, slice(64 * a, 64 * a + 64)).rearrange("p (h b q) -> p b h q", b=DB, q=DS))
                     for a, q in enumerate((qlo, qhi))])
            for bp in range(DB // 2):
                if bp:
                    act.wait_ge(S["ss_done"], bp)
                for b2 in range(2):
                    turned((kst[:, b2, :], lambda b: bank(b)))
                act.wait_ge(S["ss_done"], bp + 1)
                if bp:
                    act.wait_ge(S["sw_done"], bp)
                act.activation(rls, psum[:, 4 * 512:4 * 512 + LS], ACT.Relu).then_inc(S["ss_relu"], 1)
            act.wait_ge(S["sw_done"], DB // 2)
            natural = sc_s[:, 0:PAST].rearrange("q (p r) -> q r p", r=RP)
            for par in range(2):
                act.copy(natural[:, par::2, :], bank(2 + par, 512, slice(0, NS)).rearrange("q (r p) -> q r p", p=P)).then_inc(S["acc_ev"], 1)
            act.copy(sc_s[:, PAST:LS], bank(7, DS, slice(0, NS))).then_inc(S["acc_ev"], 1)

            def q_turned(i):
                if i < PT_TILES:
                    q4 = qz.rearrange("p (k a) t -> p k a t", a=2)
                    turned(*[(q4[64 * g:64 * g + 64, g::2, a, i * P:(i + 1) * P],
                              lambda b, g=g, a=a: bank(b, 512, slice(64 * a, 64 * a + 64)).rearrange("p (k t) -> p k t", t=P)[:, g::2, :])
                             for g in range(2) for a in range(2)])
                else:
                    copies = []
                    for pr in range(2):
                        for g in range(2):
                            out = qs[64 * g:64 * g + 64, :, pr, 16 * g:16 * g + 16].rearrange("p b (j q) -> p b j q", q=DS)
                            copies.append((out, lambda b, g=g, pr=pr: bank(b, 512, slice(64 * g, 64 * g + 64)).rearrange(
                                "p (h b q) -> p b h q", b=DB, q=DS)[:, :, 4 * pr + 2 * g:4 * pr + 2 * g + 2, :]))
                    turned(*copies)

            act.wait_ge(S["qz_zero"], 1)
            for i in range(TILES):
                take_raw(4 + i, 10 + i, 512)
                if i:
                    q_turned(i - 1)
            act.wait_ge(S["qs_zero"], 1)
            q_turned(PT_TILES)

            def k_turned(i):
                r = rows_of(i)
                turned((kT[:, :, i * P:i * P + r], lambda b: bank(b, 2 * P).rearrange("p (k t) -> p k t", t=P)[:, :, 0:r]))

            for i in range(TILES):
                take_raw(9 + i, 15 + i, 256)
                if i:
                    k_turned(i - 1)
            k_turned(PT_TILES)
            for i in range(TILES):
                r = rows_of(i)
                act.wait_ge(S["jp"], 20 + i)
                act.copy(unat[0:r, i, :], bank(2 + (19 + i) % 2, 512, slice(0, r))).then_inc(S["je"], 1)
            for i in range(TILES):
                r = rows_of(i)
                act.wait_ge(S["dt_done"], i + 1)
                act.copy(dT[:, :, i * P:i * P + r], bank(4 + i % 2).rearrange("p (g t) -> p g t", t=P)[:, :, 0:r]).then_inc(S["dt_ev"], 1)
            for g in range(NG):
                act.wait_ge(S["po_done"], g + 1)
                act.activation(poT[:, g, 0:SEQ], bank(6), ACT.Copy, scale=pscale[:, g:g + 1])
                act.activation(poT[:, g, SEQ:NT], bank(7, NS), ACT.Copy, scale=pscale[:, g:g + 1]).then_inc(S["po_ev"], 1)
            units = [(i, h) for i in range(PT_TILES) for h in range(NH)]
            U = len(units)
            for u in range(U + 2):
                if u < U:
                    L = P * (units[u][0] + 1)
                    act.wait_ge(S["mx_done"], u + 1)
                    if u >= 2:
                        act.wait_ge(S["tp"], T0 + u - 1)
                    act.activation(prob[u % 2][:, 0:L], ml[u % 2][:, 0:L], ACT.Exp, bias=nmax[:, u % 4:u % 4 + 1], scale=SCALE,
                                   accum_out=esum[:, u % 4:u % 4 + 1]).then_inc(S["ex_done"], 1)
                if 1 <= u <= U:
                    n = units[u - 1][0] + 1
                    if u >= 3:
                        act.wait_ge(S["pv_done"], u - 2)
                    turned((probT[(u - 1) % 2][:, 0:n, :], lambda b: bank(b, n * P).rearrange("p (j t) -> p j t", t=P)))
                if u >= 2 and units[u - 2][1] % 2:
                    i, h = units[u - 2]
                    act.wait_ge(S["pv_done"], u - 1)
                    act.copy(attnT[:, h // 2, i * P:(i + 1) * P], bank(6 + (u - 2) // 2 % 2, P)).then_inc(S["ot_ev"], 1)
            act.wait_ge(S["pv_done"], U)
            for bp in range(DB // 2):
                if bp:
                    act.wait_ge(S["sl_done"], bp)
                for b2 in range(2):
                    for pr in range(2):
                        for rh in range(2):
                            turned((kTb[b2][:, pr, 512 * rh:512 * rh + 512], lambda b: bank(b)))
                act.wait_ge(S["smx_done"], bp + 1)
                act.activation(probs, psum[:, 4 * 512:4 * 512 + LS], ACT.Exp, bias=snmax, scale=SCALE, accum_out=ssum).then_inc(S["sex_done"], 1)
                if bp:
                    act.wait_ge(S["spv_done"], bp)
                for g in range(2):
                    turned((probsT[:, 4 * g:4 * g + 4, :], lambda b: bank(b).rearrange("p (j t) -> p j t", t=P)))
                turned((probsT[0:DS, RP, :], lambda b: bank(b, P, slice(0, DS))))
                act.wait_ge(S["spv_done"], bp + 1)
                act.wait_ge(S["srec_done"], bp + 1)
                if bp:
                    act.wait_ge(S["sot_done"], bp)
                act.activation(onat, bank(7, 256), ACT.Copy, scale=srec).then_inc(S["son_done"], 1)
            stores_done(act)
            n = 0
            for p6 in range(6):
                if p6 % 3 == 2:
                    n += 16
                    continue
                dst = (sgA, sgB)[p6 % 3]
                for m in range(4):
                    for hh in range(2):
                        act.wait_ge(S["g_done"], n + 1)
                        act.activation(dst[:, 4 * (p6 // 3) + m, HN * hh:HN * hh + HN], bank(4 + n % 4, HN), ACT.Sigmoid).then_inc(S["gate_ev"], 1)
                        n += 1
            for i in range(TILES):
                r = rows_of(i)
                act.wait_ge(S["h_add"], i + 1)
                if i >= 2:
                    act.wait_ge(S["x2t"], 2 * (i - 1))
                    act.wait_ge(S["xn2_r"], i - 1)
                act.activation(xs2[i % 2][0:r, :], resid[0:r, i, :], ACT.Square, accum_out=ss2[0:r, i:i + 1]).then_inc(S["sq2"], 1)
                act.wait_ge(S["sq2"], i + 1)
                act.activation(rt2[0:r, i:i + 1], ss2[0:r, i:i + 1], ACT.Sqrt, bias=eps[0:r], scale=1.0 / D).then_inc(S["rt2"], 1)
                act.wait_ge(S["rs2"], i + 1)
                act.activation(xs2[i % 2][0:r, :], resid[0:r, i, :], ACT.Copy, scale=rstd2[0:r, i:i + 1]).then_inc(S["xs2_r"], 1)
            for n, (src, dst) in enumerate(((gsh, gex), (vdf, vex))):
                act.wait_ge(S["gexp_in"], n + 1)
                act.activation(dst, src, ACT.Exp).then_inc(S["gexp_out"], 1)

            def block_(m, s, n, first, store):
                act.wait_ge(m["xt_done"], n + 1)
                act.copy(xT[s].rearrange("p k t -> p (k t)"), bank(0)).then_inc(m["xt_ev"], 1)
                act.wait_ge(m["gu_done"], n + 1)
                act.activation(sg[s], bank(2 + s, DE, slice(0, CAP)), ACT.Silu).then_inc(m["silu"], 1)
                act.wait_ge(m["ht_done"], n + 1)
                act.copy(hT[s].rearrange("p k t -> p (k t)"), bank(1, KE * CAP)).then_inc(m["ht_ev"], 1)
                act.wait_ge(m["y_ev"], n + 1)
                for half in range(2):
                    act.dma_start(store(half), yo[s][64 * half:64 * half + 64, :]).then_inc(m["y_st"], 16)

            def expert_pair(i):
                for s in range(2):
                    block_(M[s], s, i, None, lambda half: y_d[bass.ds((2 * i + s) * CAP, CAP), 512 * half:512 * half + 512])

            expert_pair(0)
            with act.Fori(1, NE // 2) as i:
                expert_pair(i)
            act.wait_ge(S["flag_ready"], 1)
            over = act.value_load(flag[0:1, 0:1], min_val=0, max_val=NT)
            with act.If(over > CAP):
                act.wait_ge(S["y_zero"], 16 * YZ)
                with act.Fori(0, NE) as e:
                    with act.Fori(0, NB) as b:
                        block_(OV, 0, e * NB + b + N0, None,
                               lambda half: y_d[bass.ds((e * NB + b) * CAP + FIRST, CAP), 512 * half:512 * half + 512])
            with act.Else():
                act.nop()
            for i in range(TILES):
                r = rows_of(i)
                act.wait_ge(S["y_comb"], i + 1)
                if i >= 2:
                    act.wait_ge(s_yw[i % 2], 16 * (i // 2))
                act.activation(yout[i % 2][0:r, :], resid[0:r, i, :], ACT.Square, accum_out=ss3[0:r, i:i + 1]).then_inc(S["sq3"], 1)
                act.wait_ge(S["sq3"], i + 1)
                act.activation(rt3[0:r, i:i + 1], ss3[0:r, i:i + 1], ACT.Sqrt, bias=eps[0:r], scale=1.0 / D).then_inc(S["rt3"], 1)

        @block.vector
        def _(dve):
            chain = [0]

            def link(ins):
                chain[0] += 1
                ins.then_inc(S["dvc"], 1)
                dve.wait_ge(S["dvc"], chain[0])

            dve.memset(stats[:, 20:60], 1.0)
            dve.memset(eps, EPS).then_inc(S["st_ready"], 1)
            dve.wait_ge(S["const_in"], 16)
            dve.wait_ge(S["page_in"], 16 * NPAGE)
            dve.tensor_scalar(gidx, pgi, float(GR), const("lane"), ALU.mult, ALU.add).then_inc(S["gi_ready"], 1)
            dve.tensor_copy(expand_b, expand_f).then_inc(S["ebf_ready"], 1)
            dve.wait_ge(S["rt_done"], 1)
            dve.reciprocal(rstd1, rt1).then_inc(S["rstd_ready"], 1)
            dve.wait_ge(S["gain_in"], 48)
            for g in range(2 * TILES):
                i, half = g // 2, g % 2
                r = rows_of(i)
                dve.wait_ge(S["xt_done"], g + 1)
                dve.tensor_tensor(xnT[:, 4 * half:4 * half + 4, i * P:i * P + r], bank(g % 2).rearrange("p (k t) -> p k t", t=P)[:, :, 0:r],
                                  gain1[:, 4 * half:4 * half + 4].unsqueeze(2).to_broadcast([P, 4, r]), ALU.mult).then_inc(S["xn_ready"], 1)
            for j in range(3):
                i = QI_ORDER[j]
                L = P * (i + 1)
                for h in range(NI):
                    u = j * NI + h
                    dve.wait_ge(S["rl_ready"], u + 1)
                    w = wiS[:, i, h:h + 1]
                    if h == 0:
                        dve.tensor_scalar(score[i], rl[u % 2][:, 0:L], w, None, ALU.mult).then_inc(S["acc_done"], 1)
                    else:
                        dve.wait_ge(S["acc_done"], u)
                        dve.scalar_tensor_tensor(score[i], rl[u % 2][:, 0:L], w, score[i], ALU.mult, ALU.add).then_inc(S["acc_done"], 1)
            dve.wait_ge(S["wi_done"], 1)
            dve.tensor_tensor(wl, dmask, bank(6, NS).unsqueeze(1).to_broadcast([P, DB // 2, NS]), ALU.mult).then_inc(S["wl_ready"], 1)
            dve.wait_ge(S["zero_st"], 16)

            mx8, thr, ngt = cols[:, 16:24], cols[:, 23:24], cols[:, 24:25]

            def select(sc, L, k, rows, write_mask):
                w, gt, eq, rk = (a[0:rows, 0:L] for a in (work, gtm, eqm, rnk))
                m8, th, n = mx8[0:rows], thr[0:rows], ngt[0:rows]
                src = sc
                for rnd in range(k // 8):
                    link(dve.max(m8, src))
                    if rnd < k // 8 - 1:
                        link(dve.match_replace(w, m8, src, LOW))
                        src = w
                link(dve.tensor_scalar(gt, sc, th, 0.0, ALU.is_gt, ALU.add, accum_out=n))
                link(dve.tensor_scalar(eq, sc, th, None, ALU.is_equal))
                link(dve.tensor_tensor_scan(rk, eq, eq, 0.0, ALU.add, ALU.max))
                link(dve.tensor_scalar(n, n, -1.0, float(k), ALU.mult, ALU.add))
                link(dve.scalar_tensor_tensor(rk, rk, n, eq, ALU.is_le, ALU.mult))
                link(dve.tensor_tensor(gt, gt, rk, ALU.add))
                write_mask(gt)

            for i in range(1, PT_TILES):
                if i == 1:
                    dve.wait_ge(S["acc_done"], 3 * NI)
                L = P * (i + 1)
                link(dve.tensor_tensor(score[i][:, i * P:L], score[i][:, i * P:L], const("causal"), ALU.add))
                select(score[i], L, SEL_P, P, lambda g: link(dve.tensor_scalar(maskp[i], g, -1.0, NEG, ALU.add, ALU.mult)))
            dve.wait_ge(S["acc_ev"], 3)
            link(dve.tensor_tensor(sc_s[:, PAST:LS], sc_s[:, PAST:LS], const("newcausal", NS), ALU.add))

            def sample_mask(g):
                link(dve.tensor_scalar(msk[:, 0:PAST].rearrange("q (r p) -> q r p", p=P), g[:, 0:PAST].rearrange("q (p r) -> q r p", r=RP),
                                       -1.0, NEG, ALU.add, ALU.mult))
                dve.tensor_scalar(msk[:, PAST:LS], g[:, PAST:LS], -1.0, NEG, ALU.add, ALU.mult).then_inc(S["mask_s"], 1)

            select(sc_s, LS, SEL_S, NS, sample_mask)
            units = [(i, h) for i in range(PT_TILES) for h in range(NH)]
            U = len(units)
            for u in range(U + 1):
                if u < U:
                    i = units[u][0]
                    L = P * (i + 1)
                    c = slice(u % 4, u % 4 + 1)
                    dve.wait_ge(S["lg_done"], u + 1)
                    if u >= 2:
                        dve.wait_ge(S["ex_done"], u - 1)
                    dve.tensor_tensor_reduce(ml[u % 2][:, 0:L], bank(4 + u % 2, L), maskp[i] if i else const("causal"), 1.0, LOW,
                                             ALU.add, ALU.max, rmax[:, c]).then_inc(S["ml_done"], 1)
                    dve.wait_ge(S["ml_done"], u + 1)
                    dve.tensor_scalar(nmax[:, c], rmax[:, c], -SCALE, None, ALU.mult).then_inc(S["mx_done"], 1)
                if u:
                    v = u - 1
                    L = P * (units[v][0] + 1)
                    c = slice(v % 4, v % 4 + 1)
                    dve.wait_ge(S["ex_done"], v + 1)
                    link(dve.reciprocal(rsum[:, c], esum[:, c]))
                    dve.tensor_scalar(prob[v % 2][:, 0:L], prob[v % 2][:, 0:L], rsum[:, c], None, ALU.mult).then_inc(S["pn_done"], 1)
            for bp in range(DB // 2):
                dve.wait_ge(S["sl_done"], bp + 1)
                link(dve.reduce_max(smax, psum[:, 4 * 512:4 * 512 + LS], AX))
                dve.tensor_scalar(snmax, smax, -SCALE, None, ALU.mult).then_inc(S["smx_done"], 1)
                dve.wait_ge(S["sex_done"], bp + 1)
                if bp:
                    dve.wait_ge(S["son_done"], bp)
                dve.reciprocal(srec, ssum).then_inc(S["srec_done"], 1)
                dve.wait_ge(S["sot_done"], bp + 1)
                turned = bank(3, 2 * P).rearrange("p (k b h q) -> p k b h q", k=2, b=2, h=NH)
                for pr in range(2):
                    for g in range(2):
                        for j in range(2):
                            out = attnT[64 * j:64 * j + 64, 2 * pr + g, SEQ + 2 * DS * bp:SEQ + 2 * DS * (bp + 1)].rearrange("p (b q) -> p b q", q=DS)
                            last = dve.tensor_copy(out, turned[64 * g:64 * g + 64, pr, :, 4 * pr + 2 * g + j, :])
                last.then_inc(S["sot_ev"], 1)
            n = 0
            for mg in range(2):
                n += 16
                dve.wait_ge(S["gate_ev"], 16 * (mg + 1))
                for m in range(4):
                    for hh in range(2):
                        for dst in (sgA, sgB):
                            v = dst[:, 4 * mg + m, HN * hh:HN * hh + HN]
                            dve.wait_ge(S["g_done"], n + 1)
                            dve.tensor_tensor(v, bank(4 + n % 4, HN), v, ALU.mult).then_inc(S["br_ev"], 1)
                            n += 1
                        a, b = (t[:, 4 * mg + m, HN * hh:HN * hh + HN] for t in (sgA, sgB))
                        dve.wait_ge(S["br_ev"], n - 16 * (mg + 1))
                        dve.tensor_tensor(a, a, b, ALU.add).then_inc(S["m_done"], 1)
            stores_done(dve)
            dve.memset(lg, 0.0)

            def after_turn(i):
                r = rows_of(i)
                for half in range(2):
                    g = 2 * i + half
                    dve.wait_ge(S["x2t"], g + 1)
                    if i >= 2:
                        dve.wait_ge(S["r_done"], i - 1)
                    dve.tensor_tensor(xn2T[i % 2][:, 4 * half:4 * half + 4, 0:r], bank(g % 2).rearrange("p (k t) -> p k t", t=P)[:, :, 0:r],
                                      gain2[:, 4 * half:4 * half + 4].unsqueeze(2).to_broadcast([P, 4, r]), ALU.mult).then_inc(S["x2e"], 1)
                dve.wait_ge(S["r_done"], i + 1)
                dve.tensor_tensor(lg[0:r, i, :], bank(2 + i % 2, EG + NE, slice(0, r)), rbias[0:r, :], ALU.add).then_inc(S["r_add"], 1)

            for i in range(TILES):
                r = rows_of(i)
                dve.wait_ge(S["h_done"], i + 1)
                if i == 0:
                    dve.wait_ge(s_res, 16 * TILES)
                b = (4 + 2 * (i % 2)) * 512
                dve.tensor_tensor(resid[0:r, i, :], psum[0:r, b:b + D], resid[0:r, i, :], ALU.add).then_inc(S["h_add"], 1)
                dve.wait_ge(S["rt2"], i + 1)
                dve.reciprocal(rstd2[0:r, i:i + 1], rt2[0:r, i:i + 1]).then_inc(S["rs2"], 1)
                if i == 0:
                    dve.wait_ge(S["late_in"], 96)
                if i:
                    after_turn(i - 1)
            after_turn(TILES - 1)
            dve.wait_ge(S["r_add"], TILES)
            iota = const("iota")

            def first_of(v, n, top, hot, a, b):
                def over(x):
                    return x.unsqueeze(2).to_broadcast([P, TILES, n])
                link(dve.tensor_reduce(top, v, AX, ALU.max))
                link(dve.tensor_tensor(a, v, over(top), ALU.is_equal))
                link(dve.scalar_tensor_tensor(b, a, -64.0, iota[:, 0:n].unsqueeze(1).to_broadcast([P, TILES, n]), ALU.mult, ALU.add))
                link(dve.tensor_reduce(least, b, AX, ALU.min))
                link(dve.tensor_tensor(hot, b, over(least), ALU.is_equal))

            gl, el = lg[:, :, 0:EG], lg[:, :, EG:]
            first_of(gl, EG, gmax, ghot, t32[0][:, :, 0:EG], t32[1][:, :, 0:EG])
            dve.tensor_tensor(gsh, gl, gmax.unsqueeze(2).to_broadcast([P, TILES, EG]), ALU.subtract).then_inc(S["gexp_in"], 1)
            link(dve.tensor_scalar(ghot, ghot, NEG, -NEG, ALU.mult, ALU.add))
            for t in range(TILES):
                v = t32[2][:, t, :].rearrange("p (g e) -> p g e", e=EPG)
                link(dve.tensor_tensor(v, el[:, t, :].rearrange("p (g e) -> p g e", e=EPG), ghot[:, t, :].unsqueeze(2).to_broadcast([P, EG, EPG]), ALU.add))
            first_of(t32[2], NE, top1, t32[3], t32[0], t32[1])
            link(dve.scalar_tensor_tensor(t32[2], t32[3], -2 * NEG, t32[2], ALU.mult, ALU.add))
            first_of(t32[2], NE, top2, t32[4], t32[0], t32[1])
            dve.tensor_tensor(vdf, top2, top1, ALU.subtract).then_inc(S["gexp_in"], 1)
            dve.wait_ge(S["gexp_out"], 2)
            link(dve.tensor_reduce(gw, gex, AX, ALU.add))
            link(dve.tensor_scalar(s2, vex, 1.0, None, ALU.add))
            link(dve.tensor_tensor(gw, gw, s2, ALU.mult))
            link(dve.reciprocal(w1, gw))
            link(dve.tensor_tensor(w2, w1, vex, ALU.mult))
            valid = const("valid").unsqueeze(2).to_broadcast([P, TILES, NE])
            for hot in (t32[3], t32[4]):
                link(dve.tensor_tensor(hot, hot, valid, ALU.mult))
            dve.tensor_copy(trib, const("tri"))
            dve.tensor_copy(oneb, const("ones")).then_inc(S["tri_ready"], 1)
            dve.tensor_tensor(ab, t32[3], t32[4], ALU.add).then_inc(S["a_ready"], 1)
            dve.wait_ge(S["rank_done"], 1)
            link(dve.tensor_reduce(least[:, 0:1], bank(4, NE, at0=TILES * NE), AX, ALU.max))
            dve.tensor_copy(flag, least[:, 0:1]).then_inc(S["flag_ready"], 1)
            rank = bank(4, TILES * NE).rearrange("p (t e) -> p t e", e=NE)
            link(dve.scalar_tensor_tensor(t32[1], rank, CAP - 0.5, const("jump").unsqueeze(1).to_broadcast([P, TILES, NE]), ALU.is_gt, ALU.mult))
            link(dve.tensor_tensor(t32[0], rank, const("base").unsqueeze(1).to_broadcast([P, TILES, NE]), ALU.add))
            link(dve.tensor_tensor(t32[0], t32[0], t32[1], ALU.add))
            for k, hot in enumerate((t32[3], t32[4])):
                link(dve.tensor_tensor(t32[1], t32[0], hot, ALU.mult))
                link(dve.tensor_reduce(s2, t32[1], AX, ALU.add))
                link(dve.tensor_copy(dest[:, k, :], s2))
            dve.tensor_copy(toki, const("tok")).then_inc(S["dest_ready"], 1)

            def block_(m, s, n, first):
                dve.wait_ge(m["silu"], n + 1)
                dve.tensor_tensor(hb[s], sg[s], bank(2 + s, DE, slice(CAP, 2 * CAP)), ALU.mult).then_inc(m["h_ready"], 1)
                dve.wait_ge(m["y_done"], n + 1)
                if not first:
                    dve.wait_ge(m["y_st"], 32 * n)
                dve.tensor_copy(yo[s], bank(4 + s)).then_inc(m["y_ev"], 1)

            for s in range(2):
                block_(M[s], s, 0, True)
            with dve.Fori(1, NE // 2) as i:
                for s in range(2):
                    block_(M[s], s, i, False)
            dve.wait_ge(S["flag_ready"], 1)
            over = dve.value_load(flag[0:1, 0:1], min_val=0, max_val=NT)
            with dve.If(over > CAP):
                with dve.Fori(N0, N0 + NE * NB) as n:
                    block_(OV, 0, n, False)
            with dve.Else():
                dve.nop()
            for i in range(TILES):
                r = rows_of(i)
                for k, w in enumerate((w1, w2)):
                    dve.wait_ge(s_ygi[i % 2][k], 16 * (i // 2 + 1))
                    ins = dve.scalar_tensor_tensor(resid[0:r, i, :], yg[i % 2][k][0:r, :], w[0:r, i:i + 1], resid[0:r, i, :], ALU.mult, ALU.add)
                    if k == 0:
                        link(ins)
                ins.then_inc(S["y_comb"], 1)
                dve.wait_ge(S["rt3"], i + 1)
                dve.reciprocal(rstd3[0:r, i:i + 1], rt3[0:r, i:i + 1]).then_inc(S["rs3"], 1)
                dve.wait_ge(S["rs3"], i + 1)
                dve.scalar_tensor_tensor(yout[i % 2][0:r, :], resid[0:r, i, :], rstd3[0:r, i:i + 1], fgrow[0:r, :], ALU.mult, ALU.mult).then_inc(S["fin_ready"], 1)

        @block.gpsimd
        def _(pool):
            chain = [0]

            def link(ins):
                chain[0] += 1
                ins.then_inc(S["plc"], 1)
                pool.wait_ge(S["plc"], chain[0])

            def gather(out, src, index, done):
                pool.indirect_dma_start(out, None, src, bass.IndirectOffsetOnAxis(ap=index, axis=0)).then_inc(done, 16)

            pool.wait_ge(S["gi_ready"], 1)
            for b in range(DB):
                gather(idxk[:, b, :], i_groups, gidx[:, b:b + 1], s_idx)
            pool.memset(work[:, 0:SLOTS // P], 0.0).then_inc(S["zero_w"], 1)
            pool.wait_ge(S["zero_w"], 1)
            pool.dma_start(tab_d.rearrange("(p n) a -> p (n a)", p=P), work[:, 0:SLOTS // P].bitcast(I32)).then_inc(S["zero_st"], 16)
            pool.memset(qs, 0.0).then_inc(S["qs_zero"], 1)
            pool.wait_ge(S["xs_ready"], TILES)
            for t in (qiz[0], qiz[1], qlo):
                pool.memset(t, 0.0)
            pool.memset(qhi, 0.0).then_inc(S["qiz_zero"], 1)

            def rotate(src, i, heads, outs):
                r = rows_of(i)
                x = src.rearrange("p (h a c) -> p h a c", a=2, c=HALF)
                a = rtmp[0][0:r, 0:heads * HD].rearrange("p (h a c) -> p h a c", a=2, c=HALF)
                b = rtmp[1][0:r, 0:heads * HD].rearrange("p (h a c) -> p h a c", a=2, c=HALF)
                full = [r, heads, HALF]

                def t(name):
                    return tab3[name][0:r, i, :].unsqueeze(1).to_broadcast(full)

                for half in range(2):
                    pool.tensor_tensor(a[:, :, half, :], x[:, :, half, :], t("cos"), ALU.mult)
                pool.tensor_tensor(b[:, :, 0, :], x[:, :, 1, :], t("nsin"), ALU.mult)
                link(pool.tensor_tensor(b[:, :, 1, :], x[:, :, 0, :], t("sin"), ALU.mult))
                for n, out in enumerate(outs):
                    last = pool.tensor_tensor(out, rtmp[0][0:r, 0:heads * HD].rearrange("p (h c) -> p h c", c=HD),
                                              rtmp[1][0:r, 0:heads * HD].rearrange("p (h c) -> p h c", c=HD), ALU.add)
                return last

            for i in range(TILES):
                r = rows_of(i)
                pool.wait_ge(S["je"], i + 1)
                if i:
                    pool.wait_ge(S["ki_roped"], i)
                rotate(kiraw[0:r, i, :], i, 1, [kir[0:r, i, HD * d:HD * d + HD].unsqueeze(1) for d in range(2)]).then_inc(S["ki_roped"], 1)
                pool.wait_ge(S["ki_roped"], i + 1)
                pool.dma_start(ni_rows[i], kir[0:r, i, 0:HD]).then_inc(S["ki_out"], 16)
            for job, (kind, i) in enumerate(JOBS):
                r = rows_of(i)
                if kind == "q" and i == 0:
                    pool.wait_ge(S["tp"], T_JOB[3] + DB)
                    pool.memset(qz, 0.0).then_inc(S["qz_zero"], 1)
                pool.wait_ge(S["je"], 6 + job)
                if job:
                    pool.wait_ge(S["rope_done"], job)
                if job >= 2:
                    pool.wait_ge(S["tp"], T_JOB[job - 2])
                    if STORED_AT[job - 2]:
                        pool.wait_ge(s_rs[job % 2], STORED_AT[job - 2])
                heads = NKV if kind == "k" else NH
                if kind != "k" and i == PT_TILES:
                    twice = roped[job % 2][0:r, :].rearrange("p (h d c) -> p h d c", d=2, c=HD)
                    outs = [twice[:, :, d, :] for d in range(2)]
                else:
                    outs = [roped[job % 2][0:r, 0:heads * HD].rearrange("p (h c) -> p h c", c=HD)]
                rotate(raw[job % 2][0:r, 0:heads * HD], i, heads, outs).then_inc(S["rope_done"], 1)
                if kind == "k":
                    pool.wait_ge(S["rope_done"], job + 1)
                    pool.dma_start(nk_rows[i], roped[job % 2][0:r, 0:NKV * HD]).then_inc(s_rs[job % 2], 16)
                    pool.dma_start(nv_rows[i], vnat[0:r, i, :]).then_inc(S["v_out"], 16)
            pool.wait_ge(S["je"], 24)
            pool.dma_start(np_prompt[0, 0], unat[P - HIST:P, PT_TILES - 1, :]).then_inc(S["u_out"], 16)
            pool.dma_start(np_sample[0, :, HIST - DS:HIST, :], unat[0:NS, PT_TILES, :]).then_inc(S["u_out"], 16)
            pool.wait_ge(S["po_done"], NG)
            pool.wait_ge(S["u_out"], 32)
            for bp in range(DB // 2):
                if bp:
                    pool.wait_ge(S["tp"], T0 + 32 + 11 * (bp - 1) + 8)
                for b2 in range(2):
                    gather(kb[:, b2, :], k_groups, gidx[:, 2 * bp + b2:2 * bp + b2 + 1], s_kin[b2])
                if bp:
                    pool.wait_ge(S["spv_done"], bp)
                for b2 in range(2):
                    gather(vb[:, b2, :], v_groups, gidx[:, 2 * bp + b2:2 * bp + b2 + 1], s_vin[b2])
                if bp == 0:
                    pool.wait_ge(S["mask_s"], 1)
                    pool.wait_ge(S["te"], T0)
                else:
                    pool.wait_ge(S["sl_done"], bp)
                for b2 in range(2):
                    c = SEQ + (2 * bp + b2) * DS
                    last = pool.tensor_copy(kTb[b2][:, :, PAST:LS], kT[:, :, c:c + DS])
                last.then_inc(S["knew_ev"], 1)
            pool.wait_ge(S["att_all"], 1)
            stores_done(pool)
            pool.memset(wr, 0.0).then_inc(S["wr_zero"], 1)
            pool.wait_ge(S["late_in"], 96)
            for i in range(TILES):
                r = rows_of(i)
                pool.wait_ge(S["xs2_r"], i + 1)
                if i >= 2:
                    pool.wait_ge(s_xst[i % 2], 16 * (i // 2))
                pool.tensor_tensor(xn2[i % 2][0:r, :], xs2[i % 2][0:r, :], g2row[0:r, :], ALU.mult).then_inc(S["xn2_r"], 1)
                pool.wait_ge(S["xn2_r"], i + 1)
                pool.dma_start(xn2_d[i * P:i * P + r, :], xn2[i % 2][0:r, :]).then_inc(s_xst[i % 2], 16)
            pool.wait_ge(S["dest_ready"], 1)
            pool.wait_ge(S["zero_st"], 16)
            for i in range(TILES):
                r = rows_of(i)
                for k in range(2):
                    pool.indirect_dma_start(tab_d, bass.IndirectOffsetOnAxis(ap=dest[0:r, k, i:i + 1], axis=0),
                                            toki[0:r, i:i + 1], None).then_inc(S["sc_st"], 16)
            pool.wait_ge(S["sc_st"], 16 * 2 * TILES)
            pool.wait_ge(s_xst[0], 48)
            pool.wait_ge(s_xst[1], 32)

            def fetch(m, s, n, rows, first):
                if not first:
                    pool.wait_ge(m["xt_done"], n)
                pool.dma_start(sidx[s], rows).then_inc(m["sidx_in"], 16)
                pool.wait_ge(m["sidx_in"], 16 * (n + 1))
                pool.sem_inc(S["passed"], 1)
                gather(xg[s], xn2_d, sidx[s], m["xg_in"])

            for s in range(2):
                fetch(M[s], s, 0, tab_d[s * CAP:s * CAP + CAP, :], True)
            with pool.Fori(1, NE // 2) as i:
                for s in range(2):
                    fetch(M[s], s, i, tab_d[bass.ds((2 * i + s) * CAP, CAP), :], False)
            pool.wait_ge(S["flag_ready"], 1)
            over = pool.value_load(flag[0:1, 0:1], min_val=0, max_val=NT)
            for s in range(2):
                pool.wait_ge(M[s]["y_st"], 32 * (NE // 2))
                pool.wait_ge(M[s]["y_done"], NE // 2)

            def combine(rows):
                for i in range(TILES):
                    r = rows_of(i)
                    if i >= 2:
                        pool.wait_ge(S["y_comb"], i - 1)
                    for k in range(2):
                        gather(yg[i % 2][k][0:r, :], rows, dest[0:r, k, i:i + 1], s_ygi[i % 2][k])

            with pool.If(over > CAP):
                pool.memset(zeros, 0.0).then_inc(S["zero_w"], 1)
                pool.wait_ge(S["zero_w"], 2)
                beyond = y_d[FIRST:SLOTS, :].rearrange("(n p r) d -> n p (r d)", p=P, n=YZ)
                for n in range(YZ):
                    pool.dma_start(beyond[n], zeros).then_inc(S["y_zero"], 16)
                with pool.Fori(0, NE) as e:
                    with pool.Fori(0, NB) as b:
                        fetch(OV, 0, e * NB + b + N0, tab_d[bass.ds((e * NB + b) * CAP + FIRST, CAP), :], False)
                pool.wait_ge(OV["y_st"], 32 * (N0 + NE * NB))
                combine(y_d)
            with pool.Else():
                combine(y_d[0:FIRST, :])


INS = ("x_prompt", "x_sample", "cache_k", "cache_v", "cache_idx_k", "state_pool", "page_table", "attn_norm_g",
       "w_in", "w_pool", "pool_scale", "w_branch_attn", "w_branch_pool", "w_out", "ffn_norm_g", "w_router_group",
       "b_router_group", "w_router_expert", "b_router_expert", "w_exp_gate", "w_exp_up", "w_exp_down", "final_norm_g")
OUTS = ((1, SEQ, D), (DB, DS, D), (1, 1, SEQ, NKV, HD), (1, 1, SEQ, NKV, HD), (1, 1, SEQ, HD), (1, 1, HIST, UW),
        (1, DB, DS, NKV, HD), (1, DB, DS, NKV, HD), (1, DB, DS, HD), (1, DB, HIST, UW))


def kernel(**inputs):
    import concourse.bacc as bacc
    from concourse.bass_utils import run_bass_kernel_spmd

    nc = bacc.Bacc("TRN2", target_bir_lowering=False, num_devices=1)
    where, consts = constants()
    arrays = {"in_consts": consts}
    for name in INS:
        arrays["in_" + name] = np.ascontiguousarray(inputs[name])
    ins = [nc.dram_tensor(n, a.shape, mybir.dt.from_np(a.dtype), kind="ExternalInput").ap() for n, a in arrays.items()]
    outs = [nc.dram_tensor(f"out_{i}", s, F32, kind="ExternalOutput").ap() for i, s in enumerate(OUTS)]
    program(nc, ins[0], where, *ins[1:], *outs)
    r = run_bass_kernel_spmd(nc, [arrays], core_ids=[0])
    return tuple(r.results[0][f"out_{i}"] for i in range(len(OUTS)))
```

```python
import numpy as np
from contextlib import ExitStack

import concourse.bass as bass
from concourse import mybir

F32 = mybir.dt.float32
BF16 = mybir.dt.bfloat16
I32 = mybir.dt.int32
ALU = mybir.AluOpType
ACT = mybir.ActivationFunctionType
AX = mybir.AxisListType.X

P = 128
D = 1024
KD = D // P
SEQ, DB, DS = 512, 8, 8
NS = DB * DS
NT = SEQ + NS
PAST, PAGE = 1024, 128
NPAGE = PAST // PAGE
NPHYS = DB * NPAGE * 5 // 4
LS = PAST + DS
HD, NH, NKV, NI = 64, 8, 4, 8
HALF = HD // 2
TILES = 5
PT_TILES = SEQ // P
SEL_P = min(256, SEQ // 4)
SEL_S = min(256, LS // 4)
WINDOWS = (2, 4, 8, 16)
NG = len(WINDOWS)
HIST = max(WINDOWS) - 1
UW = D // 2
EG, EPG = 4, 8
NE = EG * EPG
DE = D // 2
KE = DE // P
CAP = 64
MAXB = -(-NT // CAP)
NB = MAXB - 1
FIRST = NE * CAP
SLOTS = NE * CAP * MAXB
NEG = 1e30
LOW = -3e38
SCALE = HD ** -0.5
EPS = 1e-6
C_Q, C_K, C_QI, C_KI, C_U, C_GA, C_GB = 0, 512, 1024, 1536, 1608, 2120, 3144
KIW = HD + NI
HN = NT // 2


def rows_of(i):
    return P if i < PT_TILES else NS


def split_rows(i, n):
    return rows_of(i) == 64 and n == 512


def constants():
    parts = {}
    t_in, t_out = np.arange(P)[:, None], np.arange(P)[None, :]
    parts["ident"] = np.eye(P)
    parts["lane"] = t_in % (P // NPAGE)
    pos = np.zeros((TILES, P))
    pos[:PT_TILES] = np.arange(SEQ).reshape(PT_TILES, P)
    pos[PT_TILES, :NS] = PAST + np.arange(NS) % DS
    inv = (np.float32(1) / np.float32(10000.0) ** (np.arange(HALF, dtype=np.float32) / np.float32(HALF))).astype(np.float32)
    ang = (pos.astype(np.float32)[:, :, None] * inv).astype(np.float64)
    for name, t in (("cos", np.cos(ang)), ("nsin", -np.sin(ang)), ("sin", np.sin(ang))):
        parts[name] = t.transpose(1, 0, 2).reshape(P, TILES * HALF)
    cur, prev, first, new, hist = [], [], [], [], []
    for w in WINDOWS:
        inside = (t_in <= t_out) & (t_in > t_out - w)
        cur.append(inside / w - (t_in == t_out))
        prev.append((t_in - P > t_out - w) / w)
        first.append(inside / np.minimum(t_out + 1, w) - (t_in == t_out))
        b_out, s_out = np.arange(NS)[None, :] // DS, np.arange(NS)[None, :] % DS
        b_in, s_in = np.arange(P)[:, None] // DS, np.arange(P)[:, None] % DS
        new.append(((b_in == b_out) & (s_in <= s_out) & (s_in > s_out - w)) / w
                   - ((b_in == b_out) & (s_in == s_out)))
        b_in, s_in = np.arange(P)[:, None] // HIST, np.arange(P)[:, None] % HIST - HIST
        hist.append(((b_in == b_out) & (s_in > s_out - w)) / w)
    for name, m in (("bandcur", cur), ("bandprev", prev), ("bandfirst", first),
                    ("bandnew", new), ("bandhist", hist)):
        parts[name] = np.concatenate(m, axis=1)
    parts["causal"] = np.where(t_out <= t_in, 0.0, -NEG)
    parts["newcausal"] = np.where(np.arange(DS)[None, :] <= t_in % DS, 0.0, -NEG)
    c = np.arange(P)
    cb, ch, cq = c // (NH * DS), c // DS % NH, c % DS
    parts["headrep"] = (t_in == ch[None, :]) * 1.0
    r = np.arange(NS)
    dmask = [(2 * bp + cb[:, None] == r[None, :] // DS) & (cq[:, None] == r[None, :] % DS) for bp in range(DB // 2)]
    parts["dmask"] = np.concatenate(dmask, axis=1) * 1.0
    expand = np.zeros((P, DB // 2, P))
    for bp in range(DB // 2):
        expand[:NS, bp] = dmask[bp].T
    parts["expand"] = expand.reshape(P, -1)
    parts["tri"] = (t_in < t_out) * 1.0
    parts["ones"] = np.ones((P, P))
    parts["iota"] = np.tile(np.arange(NE), (P, 1))
    parts["base"] = np.tile(np.arange(NE) * CAP, (P, 1))
    parts["jump"] = np.tile(FIRST - CAP + np.arange(NE) * (NB - 1) * CAP, (P, 1))
    parts["tok"] = np.arange(TILES)[None, :] * P + t_in
    parts["valid"] = (np.arange(TILES)[None, :] * P + t_in < NT) * 1.0
    where, at = {}, 0
    for name, a in parts.items():
        where[name] = (at, a.shape[1])
        at += a.shape[1]
    return where, np.concatenate([np.asarray(a, np.float32) for a in parts.values()], axis=1)


def program(nc, consts, where, x_prompt, x_sample, cache_k, cache_v, cache_idx_k, state_pool, page_table,
            attn_norm_g, w_in, w_pool, pool_scale, w_branch_attn, w_branch_pool, w_out, ffn_norm_g,
            w_router_group, b_router_group, w_router_expert, b_router_expert,
            w_exp_gate, w_exp_up, w_exp_down, final_norm_g,
            y_prompt, y_sample, nk_prompt, nv_prompt, ni_prompt, np_prompt,
            nk_sample, nv_sample, ni_sample, np_sample):
    x_rows = [x_prompt[0, i * P:(i + 1) * P, :] for i in range(PT_TILES)] + [x_sample.rearrange("b s d -> (b s) d")]
    y_rows = [y_prompt[0, i * P:(i + 1) * P, :] for i in range(PT_TILES)] + [y_sample.rearrange("b s d -> (b s) d")]

    def token_rows(prompt, sample, tail):
        p = prompt[0, 0].rearrange(f"s {tail} -> s ({tail})") if " " in tail else prompt[0, 0]
        s = sample[0].rearrange(f"b s {tail} -> (b s) ({tail})")
        return [p[i * P:(i + 1) * P, :] for i in range(PT_TILES)] + [s]

    nk_rows = token_rows(nk_prompt, nk_sample, "h d")
    nv_rows = token_rows(nv_prompt, nv_sample, "h d")
    ni_rows = token_rows(ni_prompt, ni_sample, "d")
    GR = P // NPAGE
    RP = PAGE // GR
    k_groups = cache_k[0].rearrange("n (g r) h d -> (n g) (r h d)", g=GR)
    v_groups = cache_v[0].rearrange("n (g r) h d -> (n g) (r h d)", g=GR)
    i_groups = cache_idx_k[0].rearrange("n (g r) d -> (n g) (r d)", g=GR)
    w_in_v = w_in[0].rearrange("(k p) n -> p k n", p=P)

    ctx = ExitStack()
    with ctx:
        AW = 53200
        arena = ctx.enter_context(nc.sbuf_tensor("arena", [P, AW], F32))
        psum = ctx.enter_context(nc.psum_tensor("psum", [P, 8 * 512], F32))
        sems = {}

        def sem(name):
            sems[name] = ctx.enter_context(nc.semaphore(name))
            return sems[name]

        def at(off, *dims, rows=P):
            n = int(np.prod(dims))
            assert off + n <= AW, (off, dims)
            v = arena[0:rows, off:off + n]
            if len(dims) == 2:
                return v.rearrange("p (a b) -> p a b", b=dims[1])
            if len(dims) == 3:
                return v.rearrange("p (a b c) -> p a b c", b=dims[1], c=dims[2])
            return v

        def const(name, rows=P):
            o, n = where[name]
            return arena[0:rows, o:o + n]

        def bank(b, n=512, rows=slice(0, P), at0=0):
            return psum[rows, b * 512 + at0:b * 512 + at0 + n]

        cst_w = sum(n for _, n in where.values())
        XNT = 4160
        ATT = XNT + KD * NT
        POT = ATT + 4 * NT
        RING = POT + 4 * NT
        SLOT = KD * 512
        SMALL = RING + 2 * SLOT
        assert cst_w <= XNT - 80
        xnT = at(XNT, KD, NT)
        attnT = at(ATT, 4, NT)
        poT = at(POT, 4, NT)
        ring = [at(RING + s * SLOT, KD, 512) for s in range(2)]
        stats = at(XNT - 64, 64)
        gain1 = stats[:, 0:8]
        gain2 = stats[:, 8:16]
        pscale = stats[:, 16:20]
        ss1, rt1, rstd1 = stats[:, 20:25], stats[:, 25:30], stats[:, 30:35]
        ss2, rt2, rstd2 = stats[:, 35:40], stats[:, 40:45], stats[:, 45:50]
        ss3, rt3, rstd3 = stats[:, 50:55], stats[:, 55:60], stats[:, 20:25]
        eps = stats[:, 60:61]
        o = SMALL
        kiT2 = at(o, NT); o += NT
        vnat = at(o, TILES, NKV * HD); o += TILES * NKV * HD
        kT = at(o, 2, NT); o += 2 * NT
        qs = at(o, DB, 2, 32); o += DB * 64
        wiS = at(o, TILES, NI); o += TILES * NI
        w2T = at(o, NS, rows=NI); o += NS
        expand_b = arena[0:NS, o:o + 256].bitcast(BF16); o += 256
        cols = at(o, 40); o += 40
        KIR = o
        kir = at(o, TILES, P); o += TILES * P
        kiraw = at(o, TILES, HD); o += TILES * HD
        raw = [at(o + s * 512, 512) for s in range(2)]; o += 1024
        roped = [at(o + s * 1024, 1024) for s in range(2)]; o += 2048
        rtmp = [at(o + s * 512, 512) for s in range(2)]; o += 1024
        MP = o
        maskp = {i: at(MP + P * (i * (i + 1) // 2 - 1), P * (i + 1)) for i in range(1, PT_TILES)}
        o += P * 9
        msk = arena[0:NS, o:o + LS // 2].bitcast(BF16); o += LS // 2
        QZ = o
        qz = at(o, NH, SEQ)
        idxk = at(o, DB, RP * HD)
        o += NH * SEQ
        ZA = o
        score = {i: at(ZA + P * (i * (i + 1) // 2 - 1), P * (i + 1)) for i in range(1, PT_TILES)}
        o = ZA + P * 9
        sc_s = at(o, LS, rows=NS); o += LS
        work = at(o, LS); o += LS
        gtm = at(o, LS); o += LS
        eqm = at(o, LS); o += LS
        rnk = at(o, LS); o += LS
        ZB = o
        o = ZA
        ml = [at(o + s * 512, 512) for s in range(2)]; o += 1024
        prob = [at(o + s * 512, 512) for s in range(2)]; o += 1024
        probT = [at(o + s * 512, 4, P) for s in range(2)]; o += 1024
        o = ZA
        probs = at(o, LS); o += LS
        probsT = at(o, 9, P); o += 9 * P
        onat = at(o, NKV * HD); o += NKV * HD
        o = max(o, ZA + 3072)
        kTb1 = at(o, 2, LS); o += 2 * LS
        assert o <= ZB
        o = ZB
        xin = [at(ZB + i * D, D) for i in range(TILES)]
        qiz = [at(o + s * 1024, NI, P) for s in range(2)]; o += 2048
        qlo = at(o, DB, 64); o += 512
        qhi = at(o, DB, 64); o += 512
        kst = at(o, 2, 512); o += 1024
        rls = at(o, LS); o += LS
        wl = at(o, DB // 2, NS); o += DB // 2 * NS
        rl = [at(o + s * 512, 512) for s in range(2)]; o += 1024
        xs = [at(o + s * D, D) for s in range(2)]
        unat = at(o, TILES, UW)
        o += 2560
        kiww = at(o, KD, KIW); o += KD * KIW
        hist = at(o, UW); o += UW
        wpool = at(o, NG, P); o += NG * P
        assert o <= AW
        kb = at(ZB, 2, RP * 256)
        vb = at(ZB + 4096, 2, RP * 256)
        kTb = [at(ZB + 8192, 2, LS), kTb1]
        vnew = at(KIR, DB, 256, rows=DS)
        BANDS, GAR = where["bandcur"][0], KIR + 2048
        assert where["bandhist"][0] + 512 >= BANDS + 4 * NT and GAR + 4 * NT <= MP
        sgA = [at(BANDS + k * NT, NT) for k in range(4)] + [at(GAR + k * NT, NT) for k in range(4)]
        gb_raw = [at(QZ + k * NT, NT) for k in range(4)]
        pgi = at(XNT - 80, 8).bitcast(I32)
        gidx = at(XNT - 72, 8).bitcast(I32)
        dT = attnT
        rmax, nmax, esum, rsum = (cols[:, 4 * j:4 * j + 4] for j in range(4))
        smax, snmax, ssum, srec = (cols[:, 25 + j:26 + j] for j in range(4))
        o = SMALL
        SG = o
        sgB = [at(o + k * NT, NT) for k in range(KD)]
        assert SG + KD * NT <= GAR
        o = GAR + 4 * NT
        W0 = max(o, SG + 7000); o = W0 + 12288
        resid = at(o, TILES, D); o += TILES * D
        g2row = at(o, D); o += D
        fgrow = at(o, D); o += D
        wr = at(o, KD, P); o += KD * P
        rbias = at(o, EG + NE); o += EG + NE
        lg = at(o, TILES, EG + NE); o += TILES * (EG + NE)
        RT = o
        t32 = [at(o + j * 160, TILES, NE) for j in range(5)]; o += 800
        gmax, least, top1, top2, vdf, vex, gw, s2, w1, w2 = (at(o + j * TILES, TILES) for j in range(10)); o += 10 * TILES
        ghot, gsh, gex = (at(o + j * TILES * EG, TILES, EG) for j in range(3)); o += 3 * TILES * EG
        ab = at(o, 80).bitcast(BF16).rearrange("p (t e) -> p t e", e=NE); o += 80
        dest = arena[:, o:o + 2 * TILES].bitcast(I32).rearrange("p (k t) -> p k t", t=TILES); o += 2 * TILES
        toki = arena[:, o:o + TILES].bitcast(I32); o += TILES
        flag = arena[:, o:o + 1].bitcast(I32); o += 1
        assert o <= AW, o
        W1 = SMALL - 12288
        assert W1 - D >= XNT + 4096 and SG + 128 + 5 * D <= GAR
        wg2 = at(XNT, KD, DE)
        o = SG + 128
        xs2 = [at(o, D), at(W1 - D, D)]
        xn2 = [at(o + D + s * D, D) for s in range(2)]
        xn2T = [at(o + 3 * D + s * D, KD, P) for s in range(2)]
        o = SG
        trib = at(o, 64).bitcast(BF16); o += 64
        oneb = at(o, 64).bitcast(BF16); o += 64
        xg = [at(o + s * D, D, rows=CAP) for s in range(2)]; o += 2 * D
        xT = [at(o + s * 512, KD, CAP) for s in range(2)]; o += 1024
        sg = [at(o + s * 512, DE, rows=CAP) for s in range(2)]; o += 1024
        hb = [at(o + s * 512, DE, rows=CAP) for s in range(2)]; o += 1024
        hT = [at(o + s * 256, KE, CAP) for s in range(2)]; o += 512
        yo = [at(o + s * 512, 512) for s in range(2)]; o += 1024
        sidx = [arena[0:CAP, o + s:o + s + 1].bitcast(I32) for s in range(2)]; o += 2
        assert o <= W0
        wg = [at(b, KD, DE) for b in (W0, W1)]
        wu = [at(b + 4096, KD, DE) for b in (W0, W1)]
        wd = [at(b + 8192, KE, D) for b in (W0, W1)]
        zeros = at(W1, 8 * D)
        YZ = (SLOTS - FIRST) // (8 * P)
        yg = [[at(W0 + (2 * s + k) * D, D) for k in range(2)] for s in range(2)]
        yout = [at(W0 + (4 + s) * D, D) for s in range(2)]

        xn2_d = nc.dram_tensor("xn2_d", (NT, D), F32, kind="Internal").ap()
        tab_d = nc.dram_tensor("tab_d", (SLOTS, 1), I32, kind="Internal").ap()
        y_d = nc.dram_tensor("y_d", (SLOTS, D), F32, kind="Internal").ap()

        ident = const("ident")
        tab3 = {n: const(n).rearrange("p (t c) -> p t c", c=HALF) for n in ("cos", "nsin", "sin")}
        band = {n: const(n).rearrange("p (g c) -> p g c", g=NG)
                for n in ("bandcur", "bandprev", "bandfirst", "bandnew", "bandhist")}
        dmask = const("dmask").rearrange("p (b c) -> p b c", c=NS)
        expand_f = const("expand", NS)

        S = {n: sem(n) for n in ("""
            const_in const2_in page_in gain_in kiww_in hist_in wpool_in vnew_in late_in st_ready
            gi_ready sq_done rt_done rstd_ready xs_ready xt_done xn_ready
            jp je ki_roped rope_done tp te qiz_zero qz_zero qs_zero wr_zero
            wi_done wl_ready is_done rl_ready acc_done ss_done ss_relu sw_done acc_ev 
            ki_out v_out u_out hist_out dt_done dt_ev po_done po_ev
            lg_done ml_done mx_done ex_done pn_done pv_done ot_ev mask_s ebf_ready
            sl_done smx_done sex_done srec_done spv_done son_done sot_done sot_ev knew_ev att_all
            g_done raw_ev gs_done gate_ev br_ev m_done h_done h_add sq2 rt2 rs2 xs2_r x2t x2e xn2_r r_done r_add
            gexp_in gexp_out tri_ready a_ready rank_done flag_ready zero_st zero_w dest_ready sc_st
            y_comb sq3 rt3 rs3 fin_ready dvc plc passed y_zero""").split()}
        s_x = [sem(f"x_in{i}") for i in range(TILES)]
        s_res = sem("resid_in")
        s_ring = [sem(f"ring_in{s}") for s in range(2)]
        s_rs = [sem(f"roped_stored{s}") for s in range(2)]
        s_idx = sem("idxpage_in")
        s_kin = [sem(f"kpage_in{b}") for b in range(2)]
        s_vin = [sem(f"vpage_in{b}") for b in range(2)]
        s_xst = [sem(f"xn2_stored{s}") for s in range(2)]
        s_ygi = [[sem(f"ygather{s}{k}") for k in range(2)] for s in range(2)]
        s_yw = [sem(f"yout_stored{s}") for s in range(2)]
        M = [{n: sem(f"{n}{s}") for n in
              ("wg_in wu_in wd_in sidx_in xg_in xt_done xt_ev gu_done silu h_ready "
               "ht_done ht_ev y_done y_ev y_st").split()} for s in range(2)]
        OV, N0 = M[0], NE // 2

        RING_LOADS = [w_in_v[:, :, c:c + 512] for c in (C_QI, C_Q, C_K, C_U)]
        RING_LOADS += [w_in_v[:, :, c + 512 * mg:c + 512 * mg + 512] for c in (C_GA, C_GB) for mg in range(2)]
        RING_LOADS += [("branch", mg) for mg in range(2)]
        w_out_v = w_out[0].rearrange("(k p) n -> p k n", p=P)
        RING_LOADS += [w_out_v[:, :, 0:512], w_out_v[:, :, 512:1024]]
        R_QI, R_Q, R_KV, R_U, R_GATES, R_OUT = 0, 1, 2, 3, 4, 10
        ring_total = [0, 0]
        RING_AT = []
        for n, what in enumerate(RING_LOADS):
            ring_total[n % 2] += 32 if isinstance(what, tuple) else 16
            RING_AT.append(ring_total[n % 2])

        RING_USED = [(S["jp"], v) for v in (9, 14, 19, 24)] + [(S["g_done"], v) for v in (8, 16, 24, 32, 48, 64)]
        EARLY = 24

        QI_ORDER = [1, 2, 3, 4]
        JOBS = [("qi", i) for i in QI_ORDER] + [("q", i) for i in range(TILES)] + [("k", i) for i in range(TILES)]
        T_JOB = [3, 4, 5, 6] + list(range(15, 25))
        T0 = T_JOB[-1]
        stored = {s: 0 for s in range(2)}
        STORED_AT = []
        for n, (kind, _) in enumerate(JOBS):
            if kind == "k":
                stored[n % 2] += 16
            STORED_AT.append(stored[n % 2])

        def stores_done(eng):
            eng.wait_ge(S["ki_out"], 16 * TILES)
            eng.wait_ge(S["v_out"], 16 * TILES)
            eng.wait_ge(S["u_out"], 32)
            for s in range(2):
                eng.wait_ge(s_rs[s], stored[s])

        block = ctx.enter_context(nc.Block())

        @block.sync
        def _(sp):
            c0 = where["lane"][0] + 1
            sp.dma_start(arena[:, 0:c0], consts[:, 0:c0]).then_inc(S["const_in"], 16)
            for i in range(TILES):
                sp.dma_start(xin[i][0:rows_of(i), :], x_rows[i]).then_inc(s_x[i], 16)
            with nc.allow_non_contiguous_dma(reason="a few small columns"):
                for j in range(NPAGE):
                    src = page_table[:, j:j + 1].rearrange("b j -> j b").to_broadcast([GR, DB])
                    sp.dma_start(pgi[GR * j:GR * (j + 1), :], src).then_inc(S["page_in"], 16)
                sp.dma_start(gain1, attn_norm_g[0].rearrange("(k p) -> p k", p=P)).then_inc(S["gain_in"], 16)
                sp.dma_start(pscale, pool_scale[0].rearrange("(k p) -> p k", p=P)).then_inc(S["gain_in"], 16)
                sp.dma_start(gain2, ffn_norm_g[0].rearrange("(k p) -> p k", p=P)).then_inc(S["gain_in"], 16)
                sp.dma_start(kiww, w_in_v[:, :, C_KI:C_KI + KIW]).then_inc(S["kiww_in"], 16)

            def load_ring(n):
                if n >= 2:
                    sp.wait_ge(*RING_USED[n - 2])
                s, what = n % 2, RING_LOADS[n]
                if isinstance(what, tuple):
                    c = slice(512 * what[1], 512 * what[1] + 512)
                    sp.dma_start(ring[s][:, 0:4, :], w_branch_attn[0].rearrange("(k p) n -> p k n", p=P)[:, :, c]).then_inc(s_ring[s], 16)
                    sp.dma_start(ring[s][:, 4:8, :], w_branch_pool[0].rearrange("(k p) n -> p k n", p=P)[:, :, c]).then_inc(s_ring[s], 16)
                else:
                    sp.dma_start(ring[s], what).then_inc(s_ring[s], 16)

            load_ring(0)
            sp.dma_start(arena[:, c0:cst_w], consts[:, c0:]).then_inc(S["const2_in"], 16)
            sp.dma_start(hist[0:DB * HIST, :], state_pool[0].rearrange("b t c -> (b t) c")).then_inc(S["hist_in"], 16)
            sp.dma_start(wpool, w_pool[0].rearrange("g c d -> c g d")).then_inc(S["wpool_in"], 16)
            sp.dma_start(np_sample[0, :, 0:HIST - DS, :], state_pool[0, :, DS:HIST, :]).then_inc(S["hist_out"], 16)
            for n in range(1, 5):
                load_ring(n)
            sp.wait_ge(S["je"], 19)
            sp.wait_ge(S["tp"], T_JOB[-1])
            for s in range(2):
                sp.wait_ge(s_rs[s], stored[s])
            sp.wait_ge(S["ki_out"], 16 * TILES)
            for b in range(DB):
                sp.dma_start(vnew[:, b, :], vnat[b * DS:(b + 1) * DS, PT_TILES, :]).then_inc(S["vnew_in"], 16)
            for n in range(5, 8):
                load_ring(n)
            sp.wait_ge(S["att_all"], 1)
            stores_done(sp)
            load_ring(8)
            for i in range(TILES):
                sp.dma_start(resid[0:rows_of(i), i, :], x_rows[i]).then_inc(s_res, 16)
            with nc.allow_non_contiguous_dma(reason="router weights and rows for all partitions"):
                sp.dma_start(g2row, ffn_norm_g.to_broadcast([P, D])).then_inc(S["late_in"], 16)
                sp.dma_start(fgrow, final_norm_g.unsqueeze(0).to_broadcast([P, D])).then_inc(S["late_in"], 16)
                sp.dma_start(rbias[:, 0:EG], b_router_group.to_broadcast([P, EG])).then_inc(S["late_in"], 16)
                sp.dma_start(rbias[:, EG:], b_router_expert.to_broadcast([P, NE])).then_inc(S["late_in"], 16)
                sp.wait_ge(S["wr_zero"], 1)
                sp.dma_start(wr[:, :, 0:EG], w_router_group[0].rearrange("(k p) n -> p k n", p=P)).then_inc(S["late_in"], 16)
                sp.dma_start(wr[:, :, EG:EG + NE], w_router_expert[0].rearrange("(k p) n -> p k n", p=P)).then_inc(S["late_in"], 16)
            g_v = w_exp_gate[0].rearrange("e (p k) n -> e p (k n)", k=KD)
            u_v = w_exp_up[0].rearrange("e (p k) n -> e p (k n)", k=KD)
            d_v = w_exp_down[0].rearrange("e (p k) n -> e p (k n)", k=KE)

            def flat(t):
                return t.rearrange("p k n -> p (k n)")

            def load_expert(i, s, first=False, gate=True):
                e = 2 * i + s
                m = M[s]
                if not first:
                    sp.wait_ge(m["gu_done"], i)
                if gate:
                    sp.dma_start(flat(wg[s]), g_v[bass.ds(e, 1), :, :].squeeze(0)).then_inc(m["wg_in"], 16)
                sp.dma_start(flat(wu[s]), u_v[bass.ds(e, 1), :, :].squeeze(0)).then_inc(m["wu_in"], 16)
                if not first:
                    sp.wait_ge(m["y_done"], i)
                sp.dma_start(flat(wd[s]), d_v[bass.ds(e, 1), :, :].squeeze(0)).then_inc(m["wd_in"], 16)

            sp.wait_ge(S["gs_done"], 4)
            load_expert(0, 0, first=True)
            load_ring(9)
            sp.wait_ge(M[0]["wg_in"], 16)
            sp.dma_start(flat(wg2), g_v[2]).then_inc(M[0]["wg_in"], 16)
            load_ring(10)
            load_ring(11)
            sp.dma_start(flat(wg[1]), g_v[1]).then_inc(M[1]["wg_in"], 16)
            sp.wait_ge(S["h_done"], TILES)
            load_expert(0, 1, first=True, gate=False)
            load_expert(1, 0, gate=False)
            load_expert(1, 1)
            with sp.Fori(2, NE // 2) as i:
                for s in range(2):
                    load_expert(i, s)
            sp.wait_ge(S["flag_ready"], 1)
            over = sp.value_load(flag[0:1, 0:1], min_val=0, max_val=NT)
            with sp.If(over > CAP):
                with sp.Fori(0, NE) as e:
                    sp.wait_ge(OV["y_done"], e * NB + N0)
                    sp.dma_start(flat(wg[0]), g_v[bass.ds(e, 1), :, :].squeeze(0)).then_inc(OV["wg_in"], 16)
                    sp.dma_start(flat(wu[0]), u_v[bass.ds(e, 1), :, :].squeeze(0)).then_inc(OV["wu_in"], 16)
                    sp.dma_start(flat(wd[0]), d_v[bass.ds(e, 1), :, :].squeeze(0)).then_inc(OV["wd_in"], 16)
            with sp.Else():
                sp.nop()
            for i in range(TILES):
                sp.wait_ge(S["fin_ready"], i + 1)
                sp.dma_start(y_rows[i], yout[i % 2][0:rows_of(i), :]).then_inc(s_yw[i % 2], 16)
            sp.wait_ge(s_yw[0], 48)
            sp.wait_ge(s_yw[1], 32)
            sp.wait_ge(S["hist_out"], 16)
            stores_done(sp)

        @block.tensor
        def _(pe):
            jn, tn = [0], [0]

            def j_bank():
                if jn[0] >= 2:
                    pe.wait_ge(S["je"], jn[0] - 1)
                jn[0] += 1
                return 2 + (jn[0] - 1) % 2

            def t_bank():
                if tn[0] >= 2:
                    pe.wait_ge(S["te"], tn[0] - 1)
                tn[0] += 1
                return (tn[0] - 1) % 2

            pe.wait_ge(S["const_in"], 16)
            for i in range(TILES):
                r = rows_of(i)
                pe.wait_ge(S["xs_ready"], i + 1)
                for half in range(2):
                    g = 2 * i + half
                    if g >= 2:
                        pe.wait_ge(S["xn_ready"], g - 1)
                    for k in range(4):
                        kk = 4 * half + k
                        last = pe.transpose(bank(g % 2, r, at0=k * P), xs[i % 2][0:r, kk * P:(kk + 1) * P], ident[0:r, 0:r])
                    last.then_inc(S["xt_done"], 1)

            def project(i, w, n):
                r = rows_of(i)
                b = j_bank()
                for k in range(KD):
                    lhs = xnT[:, k, i * P:i * P + r]
                    if split_rows(i, n):
                        for half in range(2):
                            last = pe.matmul(bank(b, n // 2, slice(64 * half, 64 * half + 64)), lhs, w[:, k, n // 2 * half:n // 2 * half + n // 2],
                                             start=(k == 0), stop=(k == KD - 1))
                    else:
                        last = pe.matmul(bank(b, n, slice(0, r)), lhs, w[:, k, 0:n], start=(k == 0), stop=(k == KD - 1))
                last.then_inc(S["jp"], 1)

            def ring_ready(n):
                pe.wait_ge(s_ring[n % 2], RING_AT[n])

            pe.wait_ge(S["kiww_in"], 16)
            for i in range(TILES):
                pe.wait_ge(S["xn_ready"], 2 * (i + 1))
                project(i, kiww, KIW)
            ring_ready(R_QI)
            project(QI_ORDER[0], ring[0], 512)
            pe.wait_ge(S["ki_roped"], PT_TILES)
            b = t_bank()
            for i in range(PT_TILES):
                last = pe.transpose(bank(b, P, at0=i * P), kir[:, i, :], ident)
            last.then_inc(S["tp"], 1)
            pe.wait_ge(S["ki_roped"], TILES)
            b = t_bank()
            pe.transpose(bank(b, NS), kir[0:NS, PT_TILES, :], ident[0:NS, 0:NS])
            pe.wait_ge(S["je"], TILES)
            pe.transpose(bank(b, NS, slice(0, NI), at0=NS), wiS[0:NS, PT_TILES, :], ident[0:NS, 0:NS]).then_inc(S["tp"], 1)

            def turn(job, n_blocks, rows, width):
                pe.wait_ge(S["rope_done"], job + 1)
                b = t_bank()
                for k in range(n_blocks):
                    last = pe.transpose(bank(b, rows, at0=k * width), roped[job % 2][0:rows, k * P:(k + 1) * P], ident[0:rows, 0:rows])
                last.then_inc(S["tp"], 1)

            def index_prompt(j):
                i = QI_ORDER[j]
                L = P * (i + 1)
                for h in range(NI):
                    u = j * NI + h
                    if h == 0:
                        pe.wait_ge(S["te"], tn[0])
                    if u >= 2:
                        pe.wait_ge(S["rl_ready"], u - 1)
                    pe.matmul(bank(4 + u % 2, L), qiz[j % 2][:, h, :], kiT2[:, 0:L], start=True, stop=True).then_inc(S["is_done"], 1)

            for j in range(3):
                project(QI_ORDER[j + 1], ring[0], 512)
                turn(j, 4, P, P)
                index_prompt(j)
            turn(3, 8, NS, NS)
            pe.wait_ge(S["te"], tn[0])
            pe.wait_ge(S["rl_ready"], 3 * NI)
            pe.wait_ge(S["const2_in"], 16)
            pe.matmul(bank(6, NS), const("headrep", NI), w2T, start=True, stop=True).then_inc(S["wi_done"], 1)
            pe.wait_ge(S["je"], jn[0])
            pe.wait_ge(S["wl_ready"], 1)
            for bp in range(DB // 2):
                for b2 in range(2):
                    if bp == b2 == 0:
                        pe.wait_ge(s_idx, 16 * DB)
                    b = t_bank()
                    for rr in range(4):
                        last = pe.transpose(bank(b, P, at0=rr * P), idxk[:, 2 * bp + b2, rr * P:(rr + 1) * P], ident)
                    last.then_inc(S["tp"], 1)
                if bp:
                    pe.wait_ge(S["ss_relu"], bp)
                pe.wait_ge(S["te"], tn[0])
                for par, q in enumerate((qlo, qhi)):
                    for b2 in range(2):
                        pe.matmul(bank(4 + par, 512, slice(64 * b2, 64 * b2 + 64)), q[:, 2 * bp + b2, :], kst[:, b2, :], start=True, stop=True)
                for b2 in range(2):
                    bb = 2 * bp + b2
                    last = pe.matmul(bank(6, DS, slice(64 * b2, 64 * b2 + 64)), qlo[:, bb, :],
                                     kiT2[:, SEQ + bb * DS:SEQ + (bb + 1) * DS], start=True, stop=True)
                last.then_inc(S["ss_done"], 1)
                pe.wait_ge(S["ss_relu"], bp + 1)
                for c, (b, n) in enumerate(((2, 512), (3, 512), (7, DS))):
                    last = pe.matmul(bank(b, n, slice(0, NS)), wl[:, bp, :], rls[:, 512 * c:512 * c + n],
                                     start=(bp == 0), stop=(bp == DB // 2 - 1), skip_group_check=True)
                last.then_inc(S["sw_done"], 1)
            pe.wait_ge(S["acc_ev"], 3)
            for what, slot, first in (("q", R_Q, 4), ("k", R_KV, 9)):
                ring_ready(slot)
                for i in range(TILES):
                    project(i, ring[slot % 2], 512)
                    if i:
                        turn(first + i - 1, 4 if what == "q" else 2, rows_of(i - 1), P)
                if what == "q":
                    turn(first + TILES - 1, 8, NS, NS)
                else:
                    turn(first + TILES - 1, 2, NS, P)
            ring_ready(R_U)
            for i in range(TILES):
                project(i, ring[R_U % 2], 512)
            pe.wait_ge(S["hist_in"], 16)
            for i in range(TILES):
                r = rows_of(i)
                pe.wait_ge(S["je"], jn[0] - TILES + i + 1)
                if i >= 2:
                    pe.wait_ge(S["dt_ev"], i - 1)
                for g in range(NG):
                    out = bank(4 + i % 2, r, at0=g * P)
                    c = slice(g * P, (g + 1) * P)
                    if i == 0:
                        last = pe.matmul(out, unat[:, 0, c], band["bandfirst"][:, g, :], start=True, stop=True)
                    elif i < PT_TILES:
                        pe.matmul(out, unat[:, i - 1, c], band["bandprev"][:, g, :], start=True, stop=False)
                        last = pe.matmul(out, unat[:, i, c], band["bandcur"][:, g, :], start=False, stop=True)
                    else:
                        pe.matmul(out, hist[0:DB * HIST, c], band["bandhist"][0:DB * HIST, g, :], start=True, stop=False)
                        last = pe.matmul(out, unat[0:NS, i, c], band["bandnew"][0:NS, g, :], start=False, stop=True)
                last.then_inc(S["dt_done"], 1)
            pe.wait_ge(S["dt_ev"], TILES)
            pe.wait_ge(S["wpool_in"], 16)
            for g in range(NG):
                if g >= 2:
                    pe.wait_ge(S["po_ev"], g - 1)
                pe.matmul(bank(6 + g % 2), wpool[:, g, :], dT[:, g, 0:SEQ], start=True, stop=True)
                pe.matmul(bank(4 + g % 2, NS), wpool[:, g, :], dT[:, g, SEQ:NT], start=True, stop=True).then_inc(S["po_done"], 1)
            units = [(i, h) for i in range(PT_TILES) for h in range(NH)]
            U = len(units)
            pe.wait_ge(S["po_ev"], NG)
            pe.wait_ge(S["te"], tn[0])
            t0 = tn[0]

            def gate_part(n, k0, k1):
                slot, m, hh = R_GATES + n // 8, n % 8 // 2, n % 2
                if k0 == 0:
                    if n % 8 == 0:
                        ring_ready(slot)
                    if n >= 2:
                        pe.wait_ge(S["raw_ev"], n - 1 if n <= 16 else n)
                for k in range(k0, k1):
                    last = pe.matmul(bank(2 + n % 2 if n < 16 else 2, HN), ring[slot % 2][:, k, m * P:(m + 1) * P],
                                     xnT[:, k, HN * hh:HN * hh + HN], start=(k == 0), stop=(k == KD - 1))
                if k1 == KD:
                    last.then_inc(S["g_done"], 1)

            for u in range(U + 2):
                if u < U:
                    i, h = units[u]
                    if u >= 2:
                        pe.wait_ge(S["ml_done"], u - 1)
                    pe.matmul(bank(4 + u % 2, P * (i + 1)), qz[:, h, i * P:(i + 1) * P], kT[:, h // 4, 0:P * (i + 1)],
                              start=True, stop=True).then_inc(S["lg_done"], 1)
                    gate_part(u // 2, KD // 2 * (u % 2), KD // 2 * (u % 2 + 1))
                if 1 <= u <= U:
                    i, h = units[u - 1]
                    pe.wait_ge(S["pn_done"], u)
                    b = t_bank()
                    for j in range(i + 1):
                        last = pe.transpose(bank(b, P, at0=j * P), prob[(u - 1) % 2][:, j * P:(j + 1) * P], ident)
                    last.then_inc(S["tp"], 1)
                if u >= 2:
                    v = u - 2
                    i, h = units[v]
                    pe.wait_ge(S["te"], t0 + v + 1)
                    if h % 2 == 0 and v >= 4:
                        pe.wait_ge(S["ot_ev"], v // 2 - 1)
                    half = slice(64 * (h % 2), 64 * (h % 2) + 64)
                    for j in range(i + 1):
                        last = pe.matmul(bank(6 + (v // 2) % 2, P, half), vnat[:, j, (h // 2) * HD:(h // 2 + 1) * HD],
                                         probT[v % 2][:, j, :], start=(j == 0), stop=(j == i))
                    last.then_inc(S["pv_done"], 1)
            pe.wait_ge(S["ot_ev"], U // 2)
            pe.wait_ge(S["vnew_in"], 16 * DB)
            pe.wait_ge(S["ebf_ready"], 1)
            pe.wait_ge(S["mask_s"], 1)
            for bp in range(DB // 2):
                for b2 in range(2):
                    pe.wait_ge(s_kin[b2], 16 * (bp + 1))
                    for pr in range(2):
                        for rh in range(2):
                            b = t_bank()
                            for r in range(4):
                                c = (4 * rh + r) * 256 + pr * P
                                last = pe.transpose(bank(b, P, at0=r * P), kb[:, b2, c:c + P], ident)
                            last.then_inc(S["tp"], 1)
                pe.wait_ge(S["te"], tn[0])
                pe.wait_ge(S["knew_ev"], bp + 1)
                if bp:
                    pe.wait_ge(S["sex_done"], bp)
                for c, n in enumerate((512, 512, DS)):
                    cs = slice(512 * c, 512 * c + n)
                    pe.matmul(bank(4 + c, n), expand_b[:, bp * P:(bp + 1) * P], msk[:, cs], start=True, stop=False, skip_group_check=True)
                    for b2 in range(2):
                        for pr in range(2):
                            at_row = 64 * b2 + 32 * pr
                            last = pe.matmul(bank(4 + c, n, slice(at_row, at_row + 32)), qs[:, 2 * bp + b2, pr, :], kTb[b2][:, pr, cs],
                                             start=False, stop=True, skip_group_check=True, tile_position=(0, at_row))
                last.then_inc(S["sl_done"], 1)
                gate_part(16 + 2 * bp, 0, KD)
                pe.wait_ge(S["sex_done"], bp + 1)
                for g in range(2):
                    b = t_bank()
                    for r in range(4):
                        last = pe.transpose(bank(b, P, at0=r * P), probs[:, (4 * g + r) * P:(4 * g + r + 1) * P], ident)
                    last.then_inc(S["tp"], 1)
                b = t_bank()
                pe.transpose(bank(b, P, slice(0, DS)), probs[:, PAST:LS], ident).then_inc(S["tp"], 1)
                pe.wait_ge(S["te"], tn[0])
                if bp:
                    pe.wait_ge(S["son_done"], bp)
                for b2 in range(2):
                    pe.wait_ge(s_vin[b2], 16 * (bp + 1))
                    rows = slice(64 * b2, 64 * b2 + 64)
                    for r in range(RP):
                        pe.matmul(bank(7, 256, rows), probsT[:, r, 64 * b2:64 * b2 + 64], vb[:, b2, r * 256:(r + 1) * 256],
                                  start=(r == 0), stop=False)
                    last = pe.matmul(bank(7, 256, rows), probsT[0:DS, RP, 64 * b2:64 * b2 + 64], vnew[:, 2 * bp + b2, :],
                                     start=False, stop=True)
                last.then_inc(S["spv_done"], 1)
                gate_part(17 + 2 * bp, 0, KD)
                pe.wait_ge(S["son_done"], bp + 1)
                if bp:
                    pe.wait_ge(S["sot_ev"], bp)
                for pr in range(2):
                    last = pe.transpose(bank(3, P, at0=pr * P), onat[:, pr * P:(pr + 1) * P], ident)
                last.then_inc(S["sot_done"], 1)
            pe.wait_ge(S["sot_ev"], DB // 2)
            pe.sem_inc(S["att_all"], 1)
            evs = []
            counts = {"gate_ev": 0, "br_ev": 0}

            def g_bank():
                n = len(evs)
                if n >= 4:
                    name, v = evs[n - 4]
                    pe.wait_ge(S[name], v)
                return 4 + n % 4

            def g_evac(name):
                counts[name] += 1
                evs.append((name, counts[name]))

            for p3 in range(3):
                slot = R_GATES + EARLY // 8 + p3
                ring_ready(slot)
                w = ring[slot % 2]
                for m in range(4):
                    for hh in range(2):
                        tc = slice(HN * hh, HN * hh + HN)
                        if p3 == 0:
                            b = g_bank()
                            for k in range(KD):
                                last = pe.matmul(bank(b, HN), w[:, k, m * P:(m + 1) * P], xnT[:, k, tc], start=(k == 0), stop=(k == KD - 1))
                            last.then_inc(S["g_done"], 1)
                            g_evac("gate_ev")
                        else:
                            for br, src in enumerate((attnT, poT)):
                                b = g_bank()
                                for k in range(4):
                                    last = pe.matmul(bank(b, HN), w[:, 4 * br + k, m * P:(m + 1) * P], src[:, k, tc], start=(k == 0), stop=(k == 3))
                                last.then_inc(S["g_done"], 1)
                                g_evac("br_ev")
            ring_ready(R_OUT)
            pe.wait_ge(S["m_done"], KD * 2)
            pe.wait_ge(S["late_in"], 96)

            def out_proj(i, half):
                if i >= 2 and half == 0:
                    pe.wait_ge(S["h_add"], i - 1)
                if i == PT_TILES:
                    for k in range(4 * half, 4 * half + 4):
                        for c in range(2):
                            last = pe.matmul(bank(4, 512, slice(64 * c, 64 * c + 64)), sgA[k][:, SEQ:NT], ring[c][:, k, :],
                                             start=(k == 0), stop=(k == KD - 1))
                else:
                    for k in range(KD):
                        last = pe.matmul(bank(4 + 2 * (i % 2) + half), sgA[k][:, i * P:(i + 1) * P], ring[half][:, k, :],
                                         start=(k == 0), stop=(k == KD - 1))
                if half:
                    last.then_inc(S["h_done"], 1)

            def turn_2(i):
                r = rows_of(i)
                pe.wait_ge(S["h_add"], i + 1)
                for half in range(2):
                    g = 2 * i + half
                    if g >= 2:
                        pe.wait_ge(S["x2e"], g - 1)
                    for k in range(4):
                        kk = 4 * half + k
                        last = pe.transpose(bank(g % 2, r, at0=k * P), resid[0:r, i, kk * P:(kk + 1) * P], ident[0:r, 0:r])
                    last.then_inc(S["x2t"], 1)

            def route(i):
                r = rows_of(i)
                pe.wait_ge(S["x2e"], 2 * i + 2)
                if i >= 2:
                    pe.wait_ge(S["r_add"], i - 1)
                for k in range(KD):
                    last = pe.matmul(bank(2 + i % 2, P, slice(0, r)), xn2T[i % 2][:, k, 0:r], wr[:, k, :], start=(k == 0), stop=(k == KD - 1))
                last.then_inc(S["r_done"], 1)

            out_proj(0, 0)
            out_proj(1, 0)
            ring_ready(R_OUT + 1)
            out_proj(0, 1)
            out_proj(1, 1)
            for i in range(2, TILES):
                turn_2(i - 2)
                out_proj(i, 0)
                route(i - 2)
                if i == TILES - 1:
                    turn_2(i - 1)
                out_proj(i, 1)
            route(TILES - 2)
            turn_2(TILES - 1)
            route(TILES - 1)
            pe.wait_ge(S["a_ready"], 1)
            pe.wait_ge(S["tri_ready"], 1)
            pe.wait_ge(S["h_add"], TILES)
            for i in range(TILES + 1):
                for j in range(min(i, TILES - 1) + 1):
                    lhs = trib if j == i else oneb
                    last = pe.matmul(bank(4, NE, at0=i * NE), lhs, ab[:, j, :], start=(j == 0), stop=(j == min(i, TILES - 1)))
            last.then_inc(S["rank_done"], 1)

            def turn_x(m, s, n):
                pe.wait_ge(m["xg_in"], 16 * (n + 1))
                pe.sem_inc(S["passed"], 1)
                for k in range(KD):
                    last = pe.transpose(bank(0, CAP, at0=k * CAP), xg[s][:, k:KD * (P - 1) + k + 1:KD], ident[0:CAP, 0:CAP])
                last.then_inc(m["xt_done"], 1)

            def gate_up(m, s, n, w_gate=None):
                pe.wait_ge(m["xt_ev"], n + 1)
                for k in range(KD):
                    for half, w in enumerate((wg[s] if w_gate is None else w_gate, wu[s])):
                        last = pe.matmul(bank(2 + s, 512, slice(64 * half, 64 * half + 64)), xT[s][:, k, :], w[:, k, :],
                                         start=(k == 0), stop=(k == KD - 1))
                last.then_inc(m["gu_done"], 1)

            def turn_h(m, s, n):
                pe.wait_ge(m["h_ready"], n + 1)
                pe.sem_inc(S["passed"], 1)
                for k in range(KE):
                    last = pe.transpose(bank(1, CAP, at0=k * CAP), hb[s][:, k:KE * (P - 1) + k + 1:KE], ident[0:CAP, 0:CAP])
                last.then_inc(m["ht_done"], 1)

            def down(m, s, n):
                pe.wait_ge(m["ht_ev"], n + 1)
                for k in range(KE):
                    for half in range(2):
                        last = pe.matmul(bank(4 + s, 512, slice(64 * half, 64 * half + 64)), hT[s][:, k, :], wd[s][:, k, 512 * half:512 * half + 512],
                                         start=(k == 0), stop=(k == KE - 1))
                last.then_inc(m["y_done"], 1)

            def expert_pair(i, last_pair=False):
                for s in range(2):
                    m = M[s]
                    pe.wait_ge(m["wg_in"], 16 * (i + 1))
                    pe.wait_ge(m["wu_in"], 16 * (i + 1))
                    gate_up(m, s, i, wg2 if isinstance(i, int) and i == 1 and s == 0 else None)
                    if not (last_pair and s == 1):
                        turn_x(M[1 - s], 1 - s, i + s)
                    turn_h(m, s, i)
                    pe.wait_ge(m["wd_in"], 16 * (i + 1))
                    down(m, s, i)

            turn_x(M[0], 0, 0)
            expert_pair(0)
            expert_pair(1)
            with pe.Fori(2, NE // 2 - 1) as i:
                expert_pair(i)
            expert_pair(NE // 2 - 1, True)
            pe.wait_ge(S["flag_ready"], 1)
            over = pe.value_load(flag[0:1, 0:1], min_val=0, max_val=NT)
            with pe.If(over > CAP):
                with pe.Fori(0, NE) as e:
                    for w in ("wg_in", "wu_in", "wd_in"):
                        pe.wait_ge(OV[w], 16 * (e + N0 + 1))
                    pe.sem_inc(S["passed"], 1)
                    with pe.Fori(0, NB) as b:
                        n = e * NB + b + N0
                        turn_x(OV, 0, n)
                        gate_up(OV, 0, n)
                        turn_h(OV, 0, n)
                        down(OV, 0, n)
            with pe.Else():
                pe.nop()

        @block.scalar
        def _(act):
            tn = [0]

            def turned(*copies):
                tn[0] += 1
                act.wait_ge(S["tp"], tn[0])
                b = (tn[0] - 1) % 2
                for out, src in copies:
                    last = act.copy(out, src(b))
                last.then_inc(S["te"], 1)

            act.wait_ge(S["st_ready"], 1)
            for i in range(TILES):
                r = rows_of(i)
                act.wait_ge(s_x[i], 16)
                if i >= 2:
                    act.wait_ge(S["sq_done"], i - 1)
                act.activation(psum[0:r, (4 + 2 * (i % 2)) * 512:(4 + 2 * (i % 2)) * 512 + D], xin[i][0:r, :], ACT.Square,
                               accum_out=ss1[0:r, i:i + 1]).then_inc(S["sq_done"], 1)
            act.wait_ge(S["sq_done"], TILES)
            act.activation(rt1, ss1, ACT.Sqrt, bias=eps, scale=1.0 / D).then_inc(S["rt_done"], 1)
            act.wait_ge(S["rstd_ready"], 1)
            for i in range(TILES):
                r = rows_of(i)
                if i >= 2:
                    act.wait_ge(S["xt_done"], 2 * (i - 1))
                act.activation(xs[i % 2][0:r, :], xin[i][0:r, :], ACT.Copy, scale=rstd1[0:r, i:i + 1]).then_inc(S["xs_ready"], 1)
            for i in range(TILES):
                r = rows_of(i)
                act.wait_ge(S["jp"], i + 1)
                act.copy(kiraw[0:r, i, :], bank(2 + i % 2, HD, slice(0, r)))
                act.activation(wiS[0:r, i, :], bank(2 + i % 2, NI, slice(0, r), HD), ACT.Copy,
                               scale=float(HD ** -0.5 * NI ** -0.5)).then_inc(S["je"], 1)

            def take_raw(job, jnum, n):
                r = rows_of(JOBS[job][1])
                act.wait_ge(S["jp"], jnum)
                if job >= 2:
                    act.wait_ge(S["rope_done"], job - 1)
                b = 2 + (jnum - 1) % 2
                i = JOBS[job][1]
                if split_rows(i, 512):
                    act.copy(raw[job % 2][0:r, 0:256], bank(b, 256, slice(0, r)))
                    dst = vnat[0:r, i, :] if JOBS[job][0] == "k" else raw[job % 2][0:r, 256:512]
                    last = act.copy(dst, bank(b, 256, slice(r, 2 * r)))
                else:
                    last = act.copy(raw[job % 2][0:r, 0:n], bank(b, n, slice(0, r)))
                    if JOBS[job][0] == "k":
                        last = act.copy(vnat[0:r, i, :], bank(b, NKV * HD, slice(0, r), n))
                last.then_inc(S["je"], 1)

            take_raw(0, 6, 512)
            turned((kiT2[:, 0:SEQ], lambda b: bank(b)))
            turned((kiT2[:, SEQ:NT], lambda b: bank(b, NS)), (w2T, lambda b: bank(b, NS, slice(0, NI), NS)))
            act.wait_ge(S["qiz_zero"], 1)
            for j in range(3):
                take_raw(j + 1, 7 + j, 512)
                if j >= 2:
                    act.wait_ge(S["is_done"], (j - 1) * NI)
                pairs = qiz[j % 2].rearrange("p (k a) t -> p k a t", a=2)
                turned(*[(pairs[64 * a:64 * a + 64, :, a, :],
                          lambda b, a=a: bank(b, 512, slice(64 * a, 64 * a + 64)).rearrange("p (k t) -> p k t", t=P))
                         for a in range(2)])
                L = P * (QI_ORDER[j] + 1)
                for h in range(NI):
                    u = j * NI + h
                    act.wait_ge(S["is_done"], u + 1)
                    if u >= 2:
                        act.wait_ge(S["acc_done"], u - 1)
                    act.activation(rl[u % 2][:, 0:L], bank(4 + u % 2, L), ACT.Relu).then_inc(S["rl_ready"], 1)
            turned(*[(q[64 * a:64 * a + 64].rearrange("p b (h q) -> p b h q", q=DS),
                      lambda b, a=a: bank(b, 512, slice(64 * a, 64 * a + 64)).rearrange("p (h b q) -> p b h q", b=DB, q=DS))
                     for a, q in enumerate((qlo, qhi))])
            for bp in range(DB // 2):
                if bp:
                    act.wait_ge(S["ss_done"], bp)
                for b2 in range(2):
                    turned((kst[:, b2, :], lambda b: bank(b)))
                act.wait_ge(S["ss_done"], bp + 1)
                if bp:
                    act.wait_ge(S["sw_done"], bp)
                act.activation(rls, psum[:, 4 * 512:4 * 512 + LS], ACT.Relu).then_inc(S["ss_relu"], 1)
            act.wait_ge(S["sw_done"], DB // 2)
            natural = sc_s[:, 0:PAST].rearrange("q (p r) -> q r p", r=RP)
            for par in range(2):
                act.copy(natural[:, par::2, :], bank(2 + par, 512, slice(0, NS)).rearrange("q (r p) -> q r p", p=P)).then_inc(S["acc_ev"], 1)
            act.copy(sc_s[:, PAST:LS], bank(7, DS, slice(0, NS))).then_inc(S["acc_ev"], 1)

            def q_turned(i):
                if i < PT_TILES:
                    q4 = qz.rearrange("p (k a) t -> p k a t", a=2)
                    turned(*[(q4[64 * g:64 * g + 64, g::2, a, i * P:(i + 1) * P],
                              lambda b, g=g, a=a: bank(b, 512, slice(64 * a, 64 * a + 64)).rearrange("p (k t) -> p k t", t=P)[:, g::2, :])
                             for g in range(2) for a in range(2)])
                else:
                    copies = []
                    for pr in range(2):
                        for g in range(2):
                            out = qs[64 * g:64 * g + 64, :, pr, 16 * g:16 * g + 16].rearrange("p b (j q) -> p b j q", q=DS)
                            copies.append((out, lambda b, g=g, pr=pr: bank(b, 512, slice(64 * g, 64 * g + 64)).rearrange(
                                "p (h b q) -> p b h q", b=DB, q=DS)[:, :, 4 * pr + 2 * g:4 * pr + 2 * g + 2, :]))
                    turned(*copies)

            act.wait_ge(S["qz_zero"], 1)
            for i in range(TILES):
                take_raw(4 + i, 10 + i, 512)
                if i:
                    q_turned(i - 1)
            act.wait_ge(S["qs_zero"], 1)
            q_turned(PT_TILES)

            def k_turned(i):
                r = rows_of(i)
                turned((kT[:, :, i * P:i * P + r], lambda b: bank(b, 2 * P).rearrange("p (k t) -> p k t", t=P)[:, :, 0:r]))

            for i in range(TILES):
                take_raw(9 + i, 15 + i, 256)
                if i:
                    k_turned(i - 1)
            k_turned(PT_TILES)
            for i in range(TILES):
                r = rows_of(i)
                act.wait_ge(S["jp"], 20 + i)
                b = 2 + (19 + i) % 2
                if split_rows(i, 512):
                    act.copy(unat[0:r, i, 0:256], bank(b, 256, slice(0, r)))
                    act.copy(unat[0:r, i, 256:512], bank(b, 256, slice(r, 2 * r))).then_inc(S["je"], 1)
                else:
                    act.copy(unat[0:r, i, :], bank(b, 512, slice(0, r))).then_inc(S["je"], 1)
            for i in range(TILES):
                r = rows_of(i)
                act.wait_ge(S["dt_done"], i + 1)
                act.copy(dT[:, :, i * P:i * P + r], bank(4 + i % 2).rearrange("p (g t) -> p g t", t=P)[:, :, 0:r]).then_inc(S["dt_ev"], 1)
            for g in range(NG):
                act.wait_ge(S["po_done"], g + 1)
                act.activation(poT[:, g, 0:SEQ], bank(6 + g % 2), ACT.Copy, scale=pscale[:, g:g + 1])
                act.activation(poT[:, g, SEQ:NT], bank(4 + g % 2, NS), ACT.Copy, scale=pscale[:, g:g + 1]).then_inc(S["po_ev"], 1)
            units = [(i, h) for i in range(PT_TILES) for h in range(NH)]
            U = len(units)
            for u in range(U + 2):
                if u < U:
                    L = P * (units[u][0] + 1)
                    act.wait_ge(S["mx_done"], u + 1)
                    if u >= 2:
                        act.wait_ge(S["tp"], T0 + u - 1)
                    act.activation(prob[u % 2][:, 0:L], ml[u % 2][:, 0:L], ACT.Exp, bias=nmax[:, u % 4:u % 4 + 1], scale=SCALE,
                                   accum_out=esum[:, u % 4:u % 4 + 1]).then_inc(S["ex_done"], 1)
                if 1 <= u <= U:
                    n = units[u - 1][0] + 1
                    if u >= 3:
                        act.wait_ge(S["pv_done"], u - 2)
                    turned((probT[(u - 1) % 2][:, 0:n, :], lambda b: bank(b, n * P).rearrange("p (j t) -> p j t", t=P)))
                if u >= 2 and units[u - 2][1] % 2:
                    i, h = units[u - 2]
                    act.wait_ge(S["pv_done"], u - 1)
                    act.copy(attnT[:, h // 2, i * P:(i + 1) * P], bank(6 + (u - 2) // 2 % 2, P)).then_inc(S["ot_ev"], 1)
            act.wait_ge(S["pv_done"], U)
            for bp in range(DB // 2):
                if bp:
                    act.wait_ge(S["sl_done"], bp)
                for b2 in range(2):
                    for pr in range(2):
                        for rh in range(2):
                            turned((kTb[b2][:, pr, 512 * rh:512 * rh + 512], lambda b: bank(b)))
                act.wait_ge(S["smx_done"], bp + 1)
                act.activation(probs, psum[:, 4 * 512:4 * 512 + LS], ACT.Exp, bias=snmax, scale=SCALE, accum_out=ssum).then_inc(S["sex_done"], 1)
                if bp:
                    act.wait_ge(S["spv_done"], bp)
                for g in range(2):
                    turned((probsT[:, 4 * g:4 * g + 4, :], lambda b: bank(b).rearrange("p (j t) -> p j t", t=P)))
                turned((probsT[0:DS, RP, :], lambda b: bank(b, P, slice(0, DS))))
                act.wait_ge(S["spv_done"], bp + 1)
                act.wait_ge(S["srec_done"], bp + 1)
                if bp:
                    act.wait_ge(S["sot_done"], bp)
                act.activation(onat, bank(7, 256), ACT.Copy, scale=srec).then_inc(S["son_done"], 1)
            stores_done(act)
            act.wait_ge(S["raw_ev"], EARLY)
            for k in range(4):
                act.activation(sgB[k], gb_raw[k], ACT.Sigmoid).then_inc(S["gs_done"], 1)
            for k in range(KD):
                act.activation(sgA[k], sgA[k], ACT.Sigmoid).then_inc(S["gs_done"], 1)
            for n in range(8):
                act.wait_ge(S["g_done"], EARLY + n + 1)
                act.activation(sgB[4 + n // 2][:, HN * (n % 2):HN * (n % 2) + HN], bank(4 + n % 4, HN), ACT.Sigmoid).then_inc(S["gate_ev"], 1)
            for i in range(TILES):
                r = rows_of(i)
                act.wait_ge(S["h_add"], i + 1)
                if i >= 2:
                    act.wait_ge(S["xn2_r"], i - 1)
                act.activation(xs2[i % 2][0:r, :], resid[0:r, i, :], ACT.Square, accum_out=ss2[0:r, i:i + 1]).then_inc(S["sq2"], 1)
                act.wait_ge(S["sq2"], i + 1)
                act.activation(rt2[0:r, i:i + 1], ss2[0:r, i:i + 1], ACT.Sqrt, bias=eps[0:r], scale=1.0 / D).then_inc(S["rt2"], 1)
                act.wait_ge(S["rs2"], i + 1)
                act.activation(xs2[i % 2][0:r, :], resid[0:r, i, :], ACT.Copy, scale=rstd2[0:r, i:i + 1]).then_inc(S["xs2_r"], 1)
            for n, (src, dst) in enumerate(((gsh, gex), (vdf, vex))):
                act.wait_ge(S["gexp_in"], n + 1)
                act.activation(dst, src, ACT.Exp).then_inc(S["gexp_out"], 1)

            def take_x(m, s, n):
                act.wait_ge(m["xt_done"], n + 1)
                act.copy(xT[s].rearrange("p k t -> p (k t)"), bank(0)).then_inc(m["xt_ev"], 1)

            def silu(m, s, n):
                act.wait_ge(m["gu_done"], n + 1)
                act.activation(sg[s], bank(2 + s, DE, slice(0, CAP)), ACT.Silu).then_inc(m["silu"], 1)

            def take_h(m, s, n):
                act.wait_ge(m["ht_done"], n + 1)
                act.copy(hT[s].rearrange("p k t -> p (k t)"), bank(1, KE * CAP)).then_inc(m["ht_ev"], 1)

            def store_y(m, s, n, rows):
                act.wait_ge(m["y_ev"], n + 1)
                for half in range(2):
                    act.dma_start(rows[:, 512 * half:512 * half + 512], yo[s][64 * half:64 * half + 64, :]).then_inc(m["y_st"], 16)

            def expert_pair(i, last_pair=False):
                for s in range(2):
                    silu(M[s], s, i)
                    if not (last_pair and s == 1):
                        take_x(M[1 - s], 1 - s, i + s)
                    take_h(M[s], s, i)
                    store_y(M[s], s, i, y_d[bass.ds((2 * i + s) * CAP, CAP), :])

            take_x(M[0], 0, 0)
            expert_pair(0)
            with act.Fori(1, NE // 2 - 1) as i:
                expert_pair(i)
            expert_pair(NE // 2 - 1, True)
            act.wait_ge(S["flag_ready"], 1)
            over = act.value_load(flag[0:1, 0:1], min_val=0, max_val=NT)
            with act.If(over > CAP):
                act.wait_ge(S["y_zero"], 16 * YZ)
                with act.Fori(0, NE) as e:
                    with act.Fori(0, NB) as b:
                        n = e * NB + b + N0
                        take_x(OV, 0, n)
                        silu(OV, 0, n)
                        take_h(OV, 0, n)
                        store_y(OV, 0, n, y_d[bass.ds((e * NB + b) * CAP + FIRST, CAP), :])
            with act.Else():
                act.nop()
            for i in range(TILES):
                r = rows_of(i)
                act.wait_ge(S["y_comb"], i + 1)
                if i >= 2:
                    act.wait_ge(s_yw[i % 2], 16 * (i // 2))
                act.activation(yout[i % 2][0:r, :], resid[0:r, i, :], ACT.Square, accum_out=ss3[0:r, i:i + 1]).then_inc(S["sq3"], 1)
                act.wait_ge(S["sq3"], i + 1)
                act.activation(rt3[0:r, i:i + 1], ss3[0:r, i:i + 1], ACT.Sqrt, bias=eps[0:r], scale=1.0 / D).then_inc(S["rt3"], 1)

        @block.vector
        def _(dve):
            chain = [0]

            def link(ins):
                chain[0] += 1
                ins.then_inc(S["dvc"], 1)
                dve.wait_ge(S["dvc"], chain[0])

            dve.memset(stats[:, 20:60], 1.0)
            dve.memset(eps, EPS).then_inc(S["st_ready"], 1)
            dve.wait_ge(S["const_in"], 16)
            dve.wait_ge(S["page_in"], 16 * NPAGE)
            dve.tensor_scalar(gidx, pgi, float(GR), const("lane"), ALU.mult, ALU.add).then_inc(S["gi_ready"], 1)
            dve.wait_ge(S["rt_done"], 1)
            dve.reciprocal(rstd1, rt1).then_inc(S["rstd_ready"], 1)
            dve.wait_ge(S["gain_in"], 48)
            for g in range(2 * TILES):
                i, half = g // 2, g % 2
                r = rows_of(i)
                dve.wait_ge(S["xt_done"], g + 1)
                dve.tensor_tensor(xnT[:, 4 * half:4 * half + 4, i * P:i * P + r], bank(g % 2).rearrange("p (k t) -> p k t", t=P)[:, :, 0:r],
                                  gain1[:, 4 * half:4 * half + 4].unsqueeze(2).to_broadcast([P, 4, r]), ALU.mult).then_inc(S["xn_ready"], 1)
            dve.wait_ge(S["const2_in"], 16)
            dve.tensor_copy(expand_b, expand_f).then_inc(S["ebf_ready"], 1)
            for j in range(3):
                i = QI_ORDER[j]
                L = P * (i + 1)
                for h in range(NI):
                    u = j * NI + h
                    dve.wait_ge(S["rl_ready"], u + 1)
                    w = wiS[:, i, h:h + 1]
                    if h == 0:
                        dve.tensor_scalar(score[i], rl[u % 2][:, 0:L], w, None, ALU.mult).then_inc(S["acc_done"], 1)
                    else:
                        dve.wait_ge(S["acc_done"], u)
                        dve.scalar_tensor_tensor(score[i], rl[u % 2][:, 0:L], w, score[i], ALU.mult, ALU.add).then_inc(S["acc_done"], 1)
            dve.wait_ge(S["wi_done"], 1)
            dve.tensor_tensor(wl, dmask, bank(6, NS).unsqueeze(1).to_broadcast([P, DB // 2, NS]), ALU.mult).then_inc(S["wl_ready"], 1)
            dve.wait_ge(S["zero_st"], 16)

            mx8, thr, ngt = cols[:, 16:24], cols[:, 23:24], cols[:, 24:25]

            def select(sc, L, k, rows, write_mask):
                w, gt, eq, rk = (a[0:rows, 0:L] for a in (work, gtm, eqm, rnk))
                m8, th, n = mx8[0:rows], thr[0:rows], ngt[0:rows]
                src = sc
                for rnd in range(k // 8):
                    link(dve.max(m8, src))
                    if rnd < k // 8 - 1:
                        link(dve.match_replace(w, m8, src, LOW))
                        src = w
                link(dve.tensor_scalar(gt, sc, th, 0.0, ALU.is_gt, ALU.add, accum_out=n))
                link(dve.tensor_scalar(eq, sc, th, None, ALU.is_equal))
                link(dve.tensor_tensor_scan(rk, eq, eq, 0.0, ALU.add, ALU.max))
                link(dve.tensor_scalar(n, n, -1.0, float(k), ALU.mult, ALU.add))
                link(dve.scalar_tensor_tensor(rk, rk, n, eq, ALU.is_le, ALU.mult))
                link(dve.tensor_tensor(gt, gt, rk, ALU.add))
                write_mask(gt)

            for i in range(1, PT_TILES):
                if i == 1:
                    dve.wait_ge(S["acc_done"], 3 * NI)
                L = P * (i + 1)
                link(dve.tensor_tensor(score[i][:, i * P:L], score[i][:, i * P:L], const("causal"), ALU.add))
                select(score[i], L, SEL_P, P, lambda g: link(dve.tensor_scalar(maskp[i], g, -1.0, NEG, ALU.add, ALU.mult)))
            dve.wait_ge(S["acc_ev"], 3)
            link(dve.tensor_tensor(sc_s[:, PAST:LS], sc_s[:, PAST:LS], const("newcausal", NS), ALU.add))

            def sample_mask(g):
                link(dve.tensor_scalar(msk[:, 0:PAST].rearrange("q (r p) -> q r p", p=P), g[:, 0:PAST].rearrange("q (p r) -> q r p", r=RP),
                                       -1.0, NEG, ALU.add, ALU.mult))
                dve.tensor_scalar(msk[:, PAST:LS], g[:, PAST:LS], -1.0, NEG, ALU.add, ALU.mult).then_inc(S["mask_s"], 1)

            select(sc_s, LS, SEL_S, NS, sample_mask)
            units = [(i, h) for i in range(PT_TILES) for h in range(NH)]
            U = len(units)

            def take_gate(n):
                m, cols_h = n % 8 // 2, slice(HN * (n % 2), HN * (n % 2) + HN)
                if n == 8:
                    dve.wait_ge(S["rope_done"], len(JOBS))
                    for s in range(2):
                        dve.wait_ge(s_rs[s], stored[s])
                dve.wait_ge(S["g_done"], n + 1)
                dst = sgA[4 * (n // 8) + m] if n < 16 else gb_raw[m]
                dve.tensor_copy(dst[:, cols_h], bank(2 + n % 2 if n < 16 else 2, HN)).then_inc(S["raw_ev"], 1)

            for u in range(U + 1):
                if u < U:
                    i = units[u][0]
                    L = P * (i + 1)
                    c = slice(u % 4, u % 4 + 1)
                    dve.wait_ge(S["lg_done"], u + 1)
                    if u >= 2:
                        dve.wait_ge(S["ex_done"], u - 1)
                    dve.tensor_tensor_reduce(ml[u % 2][:, 0:L], bank(4 + u % 2, L), maskp[i] if i else const("causal"), 1.0, LOW,
                                             ALU.add, ALU.max, rmax[:, c]).then_inc(S["ml_done"], 1)
                    dve.wait_ge(S["ml_done"], u + 1)
                    dve.tensor_scalar(nmax[:, c], rmax[:, c], -SCALE, None, ALU.mult).then_inc(S["mx_done"], 1)
                if u:
                    v = u - 1
                    L = P * (units[v][0] + 1)
                    c = slice(v % 4, v % 4 + 1)
                    dve.wait_ge(S["ex_done"], v + 1)
                    link(dve.reciprocal(rsum[:, c], esum[:, c]))
                    dve.tensor_scalar(prob[v % 2][:, 0:L], prob[v % 2][:, 0:L], rsum[:, c], None, ALU.mult).then_inc(S["pn_done"], 1)
                if u >= 2 and u % 2 == 0:
                    take_gate(u // 2 - 1)
            for bp in range(DB // 2):
                dve.wait_ge(S["sl_done"], bp + 1)
                link(dve.reduce_max(smax, psum[:, 4 * 512:4 * 512 + LS], AX))
                dve.tensor_scalar(snmax, smax, -SCALE, None, ALU.mult).then_inc(S["smx_done"], 1)
                take_gate(16 + 2 * bp)
                dve.wait_ge(S["sex_done"], bp + 1)
                if bp:
                    dve.wait_ge(S["son_done"], bp)
                dve.reciprocal(srec, ssum).then_inc(S["srec_done"], 1)
                take_gate(17 + 2 * bp)
                dve.wait_ge(S["sot_done"], bp + 1)
                turned = bank(3, 2 * P).rearrange("p (k b h q) -> p k b h q", k=2, b=2, h=NH)
                for pr in range(2):
                    for g in range(2):
                        for j in range(2):
                            out = attnT[64 * j:64 * j + 64, 2 * pr + g, SEQ + 2 * DS * bp:SEQ + 2 * DS * (bp + 1)].rearrange("p (b q) -> p b q", q=DS)
                            last = dve.tensor_copy(out, turned[64 * g:64 * g + 64, pr, :, 4 * pr + 2 * g + j, :])
                last.then_inc(S["sot_ev"], 1)
            n = 0
            for mg in range(2):
                dve.wait_ge(S["gs_done"], 12)
                if mg:
                    dve.wait_ge(S["gate_ev"], 8)
                for m in range(4):
                    for hh in range(2):
                        a, b = (t[4 * mg + m][:, HN * hh:HN * hh + HN] for t in (sgA, sgB))
                        for v in (a, b):
                            dve.wait_ge(S["g_done"], EARLY + 8 + n + 1)
                            dve.tensor_tensor(v, bank(4 + n % 4, HN), v, ALU.mult).then_inc(S["br_ev"], 1)
                            n += 1
                        dve.wait_ge(S["br_ev"], n)
                        dve.tensor_tensor(a, a, b, ALU.add).then_inc(S["m_done"], 1)
            stores_done(dve)
            dve.memset(lg, 0.0)

            def add_residual(i):
                r = rows_of(i)
                dve.wait_ge(S["h_done"], i + 1)
                b = (4 + 2 * (i % 2)) * 512
                if i == PT_TILES:
                    dve.tensor_tensor(resid[0:r, i, 0:512], bank(4, 512, slice(0, r)), resid[0:r, i, 0:512], ALU.add)
                    dve.tensor_tensor(resid[0:r, i, 512:D], bank(4, 512, slice(r, 2 * r)), resid[0:r, i, 512:D], ALU.add).then_inc(S["h_add"], 1)
                else:
                    dve.tensor_tensor(resid[0:r, i, :], psum[0:r, b:b + D], resid[0:r, i, :], ALU.add).then_inc(S["h_add"], 1)

            def take_turned(i):
                r = rows_of(i)
                for half in range(2):
                    g = 2 * i + half
                    dve.wait_ge(S["x2t"], g + 1)
                    if i >= 2:
                        dve.wait_ge(S["r_done"], i - 1)
                    dve.tensor_tensor(xn2T[i % 2][:, 4 * half:4 * half + 4, 0:r], bank(g % 2).rearrange("p (k t) -> p k t", t=P)[:, :, 0:r],
                                      gain2[:, 4 * half:4 * half + 4].unsqueeze(2).to_broadcast([P, 4, r]), ALU.mult).then_inc(S["x2e"], 1)
                dve.wait_ge(S["rt2"], i + 1)
                dve.reciprocal(rstd2[0:r, i:i + 1], rt2[0:r, i:i + 1]).then_inc(S["rs2"], 1)

            def take_logits(i):
                r = rows_of(i)
                dve.wait_ge(S["rs2"], i + 1)
                dve.wait_ge(S["r_done"], i + 1)
                dve.scalar_tensor_tensor(lg[0:r, i, :], bank(2 + i % 2, EG + NE, slice(0, r)), rstd2[0:r, i:i + 1], rbias[0:r, :],
                                         ALU.mult, ALU.add).then_inc(S["r_add"], 1)

            dve.wait_ge(s_res, 16 * TILES)
            dve.wait_ge(S["late_in"], 96)
            add_residual(0)
            add_residual(1)
            for i in range(2, TILES):
                take_turned(i - 2)
                take_logits(i - 2)
                if i == TILES - 1:
                    take_turned(i - 1)
                add_residual(i)
            take_logits(TILES - 2)
            take_turned(TILES - 1)
            take_logits(TILES - 1)
            dve.wait_ge(S["r_add"], TILES)
            iota = const("iota")

            def first_of(v, n, top, hot, a, b):
                def over(x):
                    return x.unsqueeze(2).to_broadcast([P, TILES, n])
                link(dve.tensor_reduce(top, v, AX, ALU.max))
                link(dve.tensor_tensor(a, v, over(top), ALU.is_equal))
                link(dve.scalar_tensor_tensor(b, a, -64.0, iota[:, 0:n].unsqueeze(1).to_broadcast([P, TILES, n]), ALU.mult, ALU.add))
                link(dve.tensor_reduce(least, b, AX, ALU.min))
                link(dve.tensor_tensor(hot, b, over(least), ALU.is_equal))

            gl, el = lg[:, :, 0:EG], lg[:, :, EG:]
            first_of(gl, EG, gmax, ghot, t32[0][:, :, 0:EG], t32[1][:, :, 0:EG])
            dve.tensor_tensor(gsh, gl, gmax.unsqueeze(2).to_broadcast([P, TILES, EG]), ALU.subtract).then_inc(S["gexp_in"], 1)
            link(dve.tensor_scalar(ghot, ghot, NEG, -NEG, ALU.mult, ALU.add))
            for t in range(TILES):
                v = t32[2][:, t, :].rearrange("p (g e) -> p g e", e=EPG)
                link(dve.tensor_tensor(v, el[:, t, :].rearrange("p (g e) -> p g e", e=EPG), ghot[:, t, :].unsqueeze(2).to_broadcast([P, EG, EPG]), ALU.add))
            first_of(t32[2], NE, top1, t32[3], t32[0], t32[1])
            link(dve.scalar_tensor_tensor(t32[2], t32[3], -2 * NEG, t32[2], ALU.mult, ALU.add))
            first_of(t32[2], NE, top2, t32[4], t32[0], t32[1])
            dve.tensor_tensor(vdf, top2, top1, ALU.subtract).then_inc(S["gexp_in"], 1)
            dve.wait_ge(S["gexp_out"], 2)
            link(dve.tensor_reduce(gw, gex, AX, ALU.add))
            link(dve.tensor_scalar(s2, vex, 1.0, None, ALU.add))
            link(dve.tensor_tensor(gw, gw, s2, ALU.mult))
            link(dve.reciprocal(w1, gw))
            link(dve.tensor_tensor(w2, w1, vex, ALU.mult))
            valid = const("valid").unsqueeze(2).to_broadcast([P, TILES, NE])
            for hot in (t32[3], t32[4]):
                link(dve.tensor_tensor(hot, hot, valid, ALU.mult))
            dve.tensor_copy(trib, const("tri"))
            dve.tensor_copy(oneb, const("ones")).then_inc(S["tri_ready"], 1)
            dve.tensor_tensor(ab, t32[3], t32[4], ALU.add).then_inc(S["a_ready"], 1)
            dve.wait_ge(S["rank_done"], 1)
            link(dve.tensor_reduce(least[:, 0:1], bank(4, NE, at0=TILES * NE), AX, ALU.max))
            dve.tensor_copy(flag, least[:, 0:1]).then_inc(S["flag_ready"], 1)
            rank = bank(4, TILES * NE).rearrange("p (t e) -> p t e", e=NE)
            link(dve.scalar_tensor_tensor(t32[1], rank, CAP - 0.5, const("jump").unsqueeze(1).to_broadcast([P, TILES, NE]), ALU.is_gt, ALU.mult))
            link(dve.tensor_tensor(t32[0], rank, const("base").unsqueeze(1).to_broadcast([P, TILES, NE]), ALU.add))
            link(dve.tensor_tensor(t32[0], t32[0], t32[1], ALU.add))
            for k, hot in enumerate((t32[3], t32[4])):
                link(dve.tensor_tensor(t32[1], t32[0], hot, ALU.mult))
                link(dve.tensor_reduce(s2, t32[1], AX, ALU.add))
                link(dve.tensor_copy(dest[:, k, :], s2))
            dve.tensor_copy(toki, const("tok")).then_inc(S["dest_ready"], 1)

            def block_(m, s, n, first):
                dve.wait_ge(m["silu"], n + 1)
                dve.tensor_tensor(hb[s], sg[s], bank(2 + s, DE, slice(CAP, 2 * CAP)), ALU.mult).then_inc(m["h_ready"], 1)
                dve.wait_ge(m["y_done"], n + 1)
                if not first:
                    dve.wait_ge(m["y_st"], 32 * n)
                dve.tensor_copy(yo[s], bank(4 + s)).then_inc(m["y_ev"], 1)

            for s in range(2):
                block_(M[s], s, 0, True)
            with dve.Fori(1, NE // 2) as i:
                for s in range(2):
                    block_(M[s], s, i, False)
            dve.wait_ge(S["flag_ready"], 1)
            over = dve.value_load(flag[0:1, 0:1], min_val=0, max_val=NT)
            with dve.If(over > CAP):
                with dve.Fori(N0, N0 + NE * NB) as n:
                    block_(OV, 0, n, False)
            with dve.Else():
                dve.nop()
            for i in range(TILES):
                r = rows_of(i)
                for k, w in enumerate((w1, w2)):
                    dve.wait_ge(s_ygi[i % 2][k], 16 * (i // 2 + 1))
                    ins = dve.scalar_tensor_tensor(resid[0:r, i, :], yg[i % 2][k][0:r, :], w[0:r, i:i + 1], resid[0:r, i, :], ALU.mult, ALU.add)
                    if k == 0:
                        link(ins)
                ins.then_inc(S["y_comb"], 1)
                dve.wait_ge(S["rt3"], i + 1)
                dve.reciprocal(rstd3[0:r, i:i + 1], rt3[0:r, i:i + 1]).then_inc(S["rs3"], 1)
                dve.wait_ge(S["rs3"], i + 1)
                dve.scalar_tensor_tensor(yout[i % 2][0:r, :], resid[0:r, i, :], rstd3[0:r, i:i + 1], fgrow[0:r, :], ALU.mult, ALU.mult).then_inc(S["fin_ready"], 1)

        @block.gpsimd
        def _(pool):
            chain = [0]

            def link(ins):
                chain[0] += 1
                ins.then_inc(S["plc"], 1)
                pool.wait_ge(S["plc"], chain[0])

            def gather(out, src, index, done):
                pool.indirect_dma_start(out, None, src, bass.IndirectOffsetOnAxis(ap=index, axis=0)).then_inc(done, 16)

            pool.wait_ge(S["gi_ready"], 1)
            for b in range(DB):
                gather(idxk[:, b, :], i_groups, gidx[:, b:b + 1], s_idx)
            pool.memset(work[:, 0:SLOTS // P], 0.0).then_inc(S["zero_w"], 1)
            pool.wait_ge(S["zero_w"], 1)
            pool.dma_start(tab_d.rearrange("(p n) a -> p (n a)", p=P), work[:, 0:SLOTS // P].bitcast(I32)).then_inc(S["zero_st"], 16)
            pool.memset(qs, 0.0).then_inc(S["qs_zero"], 1)
            pool.wait_ge(S["xs_ready"], TILES)
            for t in (qiz[0], qiz[1], qlo):
                pool.memset(t, 0.0)
            pool.memset(qhi, 0.0).then_inc(S["qiz_zero"], 1)

            def rotate(src, i, heads, outs):
                r = rows_of(i)
                x = src.rearrange("p (h a c) -> p h a c", a=2, c=HALF)
                a = rtmp[0][0:r, 0:heads * HD].rearrange("p (h a c) -> p h a c", a=2, c=HALF)
                b = rtmp[1][0:r, 0:heads * HD].rearrange("p (h a c) -> p h a c", a=2, c=HALF)
                full = [r, heads, HALF]

                def t(name):
                    return tab3[name][0:r, i, :].unsqueeze(1).to_broadcast(full)

                for half in range(2):
                    pool.tensor_tensor(a[:, :, half, :], x[:, :, half, :], t("cos"), ALU.mult)
                pool.tensor_tensor(b[:, :, 0, :], x[:, :, 1, :], t("nsin"), ALU.mult)
                link(pool.tensor_tensor(b[:, :, 1, :], x[:, :, 0, :], t("sin"), ALU.mult))
                for n, out in enumerate(outs):
                    last = pool.tensor_tensor(out, rtmp[0][0:r, 0:heads * HD].rearrange("p (h c) -> p h c", c=HD),
                                              rtmp[1][0:r, 0:heads * HD].rearrange("p (h c) -> p h c", c=HD), ALU.add)
                return last

            pool.wait_ge(S["const2_in"], 16)
            for i in range(TILES):
                r = rows_of(i)
                pool.wait_ge(S["je"], i + 1)
                if i:
                    pool.wait_ge(S["ki_roped"], i)
                rotate(kiraw[0:r, i, :], i, 1, [kir[0:r, i, HD * d:HD * d + HD].unsqueeze(1) for d in range(2)]).then_inc(S["ki_roped"], 1)
                pool.wait_ge(S["ki_roped"], i + 1)
                pool.dma_start(ni_rows[i], kir[0:r, i, 0:HD]).then_inc(S["ki_out"], 16)
            for job, (kind, i) in enumerate(JOBS):
                r = rows_of(i)
                if kind == "q" and i == 0:
                    pool.wait_ge(S["tp"], T_JOB[3] + DB)
                    pool.memset(qz, 0.0).then_inc(S["qz_zero"], 1)
                pool.wait_ge(S["je"], 6 + job)
                if job:
                    pool.wait_ge(S["rope_done"], job)
                if job >= 2:
                    pool.wait_ge(S["tp"], T_JOB[job - 2])
                    if STORED_AT[job - 2]:
                        pool.wait_ge(s_rs[job % 2], STORED_AT[job - 2])
                heads = NKV if kind == "k" else NH
                if kind != "k" and i == PT_TILES:
                    twice = roped[job % 2][0:r, :].rearrange("p (h d c) -> p h d c", d=2, c=HD)
                    outs = [twice[:, :, d, :] for d in range(2)]
                else:
                    outs = [roped[job % 2][0:r, 0:heads * HD].rearrange("p (h c) -> p h c", c=HD)]
                rotate(raw[job % 2][0:r, 0:heads * HD], i, heads, outs).then_inc(S["rope_done"], 1)
                if kind == "k":
                    pool.wait_ge(S["rope_done"], job + 1)
                    pool.dma_start(nk_rows[i], roped[job % 2][0:r, 0:NKV * HD]).then_inc(s_rs[job % 2], 16)
                    pool.dma_start(nv_rows[i], vnat[0:r, i, :]).then_inc(S["v_out"], 16)
            pool.wait_ge(S["je"], 24)
            pool.dma_start(np_prompt[0, 0], unat[P - HIST:P, PT_TILES - 1, :]).then_inc(S["u_out"], 16)
            pool.dma_start(np_sample[0, :, HIST - DS:HIST, :], unat[0:NS, PT_TILES, :]).then_inc(S["u_out"], 16)
            pool.wait_ge(S["po_done"], NG)
            pool.wait_ge(S["u_out"], 32)
            for bp in range(DB // 2):
                if bp:
                    pool.wait_ge(S["tp"], T0 + 32 + 11 * (bp - 1) + 8)
                for b2 in range(2):
                    gather(kb[:, b2, :], k_groups, gidx[:, 2 * bp + b2:2 * bp + b2 + 1], s_kin[b2])
                if bp:
                    pool.wait_ge(S["spv_done"], bp)
                for b2 in range(2):
                    gather(vb[:, b2, :], v_groups, gidx[:, 2 * bp + b2:2 * bp + b2 + 1], s_vin[b2])
                if bp == 0:
                    pool.wait_ge(S["mask_s"], 1)
                    pool.wait_ge(S["te"], T0)
                else:
                    pool.wait_ge(S["sl_done"], bp)
                for b2 in range(2):
                    c = SEQ + (2 * bp + b2) * DS
                    last = pool.tensor_copy(kTb[b2][:, :, PAST:LS], kT[:, :, c:c + DS])
                last.then_inc(S["knew_ev"], 1)
            pool.wait_ge(S["att_all"], 1)
            stores_done(pool)
            pool.memset(wr, 0.0).then_inc(S["wr_zero"], 1)
            pool.wait_ge(S["late_in"], 96)
            for i in range(TILES):
                r = rows_of(i)
                pool.wait_ge(S["xs2_r"], i + 1)
                if i >= 2:
                    pool.wait_ge(s_xst[i % 2], 16 * (i // 2))
                pool.tensor_tensor(xn2[i % 2][0:r, :], xs2[i % 2][0:r, :], g2row[0:r, :], ALU.mult).then_inc(S["xn2_r"], 1)
                pool.wait_ge(S["xn2_r"], i + 1)
                pool.dma_start(xn2_d[i * P:i * P + r, :], xn2[i % 2][0:r, :]).then_inc(s_xst[i % 2], 16)
            pool.wait_ge(S["dest_ready"], 1)
            pool.wait_ge(S["zero_st"], 16)
            for i in range(TILES):
                r = rows_of(i)
                for k in range(2):
                    pool.indirect_dma_start(tab_d, bass.IndirectOffsetOnAxis(ap=dest[0:r, k, i:i + 1], axis=0),
                                            toki[0:r, i:i + 1], None).then_inc(S["sc_st"], 16)
            pool.wait_ge(S["sc_st"], 16 * 2 * TILES)
            pool.wait_ge(s_xst[0], 48)
            pool.wait_ge(s_xst[1], 32)

            def fetch(m, s, n, rows, first):
                if not first:
                    pool.wait_ge(m["xt_done"], n)
                pool.dma_start(sidx[s], rows).then_inc(m["sidx_in"], 16)
                pool.wait_ge(m["sidx_in"], 16 * (n + 1))
                pool.sem_inc(S["passed"], 1)
                gather(xg[s], xn2_d, sidx[s], m["xg_in"])

            for s in range(2):
                fetch(M[s], s, 0, tab_d[s * CAP:s * CAP + CAP, :], True)
            with pool.Fori(1, NE // 2) as i:
                for s in range(2):
                    fetch(M[s], s, i, tab_d[bass.ds((2 * i + s) * CAP, CAP), :], False)
            pool.wait_ge(S["flag_ready"], 1)
            over = pool.value_load(flag[0:1, 0:1], min_val=0, max_val=NT)
            for s in range(2):
                pool.wait_ge(M[s]["y_st"], 32 * (NE // 2))
                pool.wait_ge(M[s]["y_done"], NE // 2)

            def combine(rows):
                for i in range(TILES):
                    r = rows_of(i)
                    if i >= 2:
                        pool.wait_ge(S["y_comb"], i - 1)
                    for k in range(2):
                        gather(yg[i % 2][k][0:r, :], rows, dest[0:r, k, i:i + 1], s_ygi[i % 2][k])

            with pool.If(over > CAP):
                pool.memset(zeros, 0.0).then_inc(S["zero_w"], 1)
                pool.wait_ge(S["zero_w"], 2)
                beyond = y_d[FIRST:SLOTS, :].rearrange("(n p r) d -> n p (r d)", p=P, n=YZ)
                for n in range(YZ):
                    pool.dma_start(beyond[n], zeros).then_inc(S["y_zero"], 16)
                with pool.Fori(0, NE) as e:
                    with pool.Fori(0, NB) as b:
                        fetch(OV, 0, e * NB + b + N0, tab_d[bass.ds((e * NB + b) * CAP + FIRST, CAP), :], False)
                pool.wait_ge(OV["y_st"], 32 * (N0 + NE * NB))
                combine(y_d)
            with pool.Else():
                combine(y_d[0:FIRST, :])


INS = ("x_prompt", "x_sample", "cache_k", "cache_v", "cache_idx_k", "state_pool", "page_table", "attn_norm_g",
       "w_in", "w_pool", "pool_scale", "w_branch_attn", "w_branch_pool", "w_out", "ffn_norm_g", "w_router_group",
       "b_router_group", "w_router_expert", "b_router_expert", "w_exp_gate", "w_exp_up", "w_exp_down", "final_norm_g")
OUTS = ((1, SEQ, D), (DB, DS, D), (1, 1, SEQ, NKV, HD), (1, 1, SEQ, NKV, HD), (1, 1, SEQ, HD), (1, 1, HIST, UW),
        (1, DB, DS, NKV, HD), (1, DB, DS, NKV, HD), (1, DB, DS, HD), (1, DB, HIST, UW))


def kernel(**inputs):
    import concourse.bacc as bacc
    from concourse.bass_utils import run_bass_kernel_spmd

    nc = bacc.Bacc("TRN2", target_bir_lowering=False, num_devices=1)
    where, consts = constants()
    arrays = {"in_consts": consts}
    for name in INS:
        arrays["in_" + name] = np.ascontiguousarray(inputs[name])
    ins = [nc.dram_tensor(n, a.shape, mybir.dt.from_np(a.dtype), kind="ExternalInput").ap() for n, a in arrays.items()]
    outs = [nc.dram_tensor(f"out_{i}", s, F32, kind="ExternalOutput").ap() for i, s in enumerate(OUTS)]
    program(nc, ins[0], where, *ins[1:], *outs)
    r = run_bass_kernel_spmd(nc, [arrays], core_ids=[0])
    return tuple(r.results[0][f"out_{i}"] for i in range(len(OUTS)))
```

```python
import numpy as np
from contextlib import ExitStack

import concourse.bass as bass
from concourse import mybir

F32 = mybir.dt.float32
BF16 = mybir.dt.bfloat16
I32 = mybir.dt.int32
ALU = mybir.AluOpType
ACT = mybir.ActivationFunctionType
AX = mybir.AxisListType.X

P = 128
D = 1024
KD = D // P
SEQ, DB, DS = 512, 8, 8
NS = DB * DS
NT = SEQ + NS
PAST, PAGE = 1024, 128
NPAGE = PAST // PAGE
NPHYS = DB * NPAGE * 5 // 4
LS = PAST + DS
HD, NH, NKV, NI = 64, 8, 4, 8
HALF = HD // 2
TILES = 5
PT_TILES = SEQ // P
SEL_P = min(256, SEQ // 4)
SEL_S = min(256, LS // 4)
WINDOWS = (2, 4, 8, 16)
NG = len(WINDOWS)
HIST = max(WINDOWS) - 1
UW = D // 2
EG, EPG = 4, 8
NE = EG * EPG
DE = D // 2
KE = DE // P
CAP = 64
MAXB = -(-NT // CAP)
NB = MAXB - 1
FIRST = NE * CAP
SLOTS = NE * CAP * MAXB
NEG = 1e30
LOW = -3e38
SCALE = HD ** -0.5
EPS = 1e-6
C_Q, C_K, C_QI, C_KI, C_U, C_GA, C_GB = 0, 512, 1024, 1536, 1608, 2120, 3144
KIW = HD + NI
HN = NT // 2


def rows_of(i):
    return P if i < PT_TILES else NS


def split_rows(i, n):
    return rows_of(i) == 64 and n == 512


def constants():
    parts = {}
    t_in, t_out = np.arange(P)[:, None], np.arange(P)[None, :]
    parts["ident"] = np.eye(P)
    parts["lane"] = t_in % (P // NPAGE)
    pos = np.zeros((TILES, P))
    pos[:PT_TILES] = np.arange(SEQ).reshape(PT_TILES, P)
    pos[PT_TILES, :NS] = PAST + np.arange(NS) % DS
    inv = (np.float32(1) / np.float32(10000.0) ** (np.arange(HALF, dtype=np.float32) / np.float32(HALF))).astype(np.float32)
    ang = (pos.astype(np.float32)[:, :, None] * inv).astype(np.float64)
    for name, t in (("cos", np.cos(ang)), ("nsin", -np.sin(ang)), ("sin", np.sin(ang))):
        parts[name] = t.transpose(1, 0, 2).reshape(P, TILES * HALF)
    cur, prev, first, new, hist = [], [], [], [], []
    for w in WINDOWS:
        inside = (t_in <= t_out) & (t_in > t_out - w)
        cur.append(inside / w - (t_in == t_out))
        prev.append((t_in - P > t_out - w) / w)
        first.append(inside / np.minimum(t_out + 1, w) - (t_in == t_out))
        b_out, s_out = np.arange(NS)[None, :] // DS, np.arange(NS)[None, :] % DS
        b_in, s_in = np.arange(P)[:, None] // DS, np.arange(P)[:, None] % DS
        new.append(((b_in == b_out) & (s_in <= s_out) & (s_in > s_out - w)) / w
                   - ((b_in == b_out) & (s_in == s_out)))
        b_in, s_in = np.arange(P)[:, None] // HIST, np.arange(P)[:, None] % HIST - HIST
        hist.append(((b_in == b_out) & (s_in > s_out - w)) / w)
    for name, m in (("bandcur", cur), ("bandprev", prev), ("bandfirst", first),
                    ("bandnew", new), ("bandhist", hist)):
        parts[name] = np.concatenate(m, axis=1)
    parts["newcausal"] = np.where(np.arange(DS)[None, :] <= t_in % DS, 0.0, -NEG)
    c = np.arange(P)
    cb, ch, cq = c // (NH * DS), c // DS % NH, c % DS
    parts["headrep"] = (t_in == ch[None, :]) * 1.0
    r = np.arange(NS)
    dmask = [(2 * bp + cb[:, None] == r[None, :] // DS) & (cq[:, None] == r[None, :] % DS) for bp in range(DB // 2)]
    parts["dmask"] = np.concatenate(dmask, axis=1) * 1.0
    parts["causal"] = np.where(t_out <= t_in, 0.0, -NEG)
    expand = np.zeros((P, DB // 2, P))
    for bp in range(DB // 2):
        expand[:NS, bp] = dmask[bp].T
    parts["expand"] = expand.reshape(P, -1)
    parts["tri"] = (t_in < t_out) * 1.0
    parts["iota"] = np.tile(np.arange(max(NE, CAP)), (P, 1))
    parts["base"] = np.tile(np.arange(NE) * CAP, (P, 1))
    parts["jump"] = np.tile(FIRST - CAP + np.arange(NE) * (NB - 1) * CAP, (P, 1))
    parts["tok"] = np.arange(TILES)[None, :] * P + t_in
    parts["valid"] = (np.arange(TILES)[None, :] * P + t_in < NT) * 1.0
    where, at = {}, 0
    for name, a in parts.items():
        where[name] = (at, a.shape[1])
        at += a.shape[1]
    return where, np.concatenate([np.asarray(a, np.float32) for a in parts.values()], axis=1)


def program(nc, consts, where, x_prompt, x_sample, cache_k, cache_v, cache_idx_k, state_pool, page_table,
            attn_norm_g, w_in, w_pool, pool_scale, w_branch_attn, w_branch_pool, w_out, ffn_norm_g,
            w_router_group, b_router_group, w_router_expert, b_router_expert,
            w_exp_gate, w_exp_up, w_exp_down, final_norm_g,
            y_prompt, y_sample, nk_prompt, nv_prompt, ni_prompt, np_prompt,
            nk_sample, nv_sample, ni_sample, np_sample):
    x_rows = [x_prompt[0, i * P:(i + 1) * P, :] for i in range(PT_TILES)] + [x_sample.rearrange("b s d -> (b s) d")]
    y_rows = [y_prompt[0, i * P:(i + 1) * P, :] for i in range(PT_TILES)] + [y_sample.rearrange("b s d -> (b s) d")]

    def token_rows(prompt, sample, tail):
        p = prompt[0, 0].rearrange(f"s {tail} -> s ({tail})") if " " in tail else prompt[0, 0]
        s = sample[0].rearrange(f"b s {tail} -> (b s) ({tail})")
        return [p[i * P:(i + 1) * P, :] for i in range(PT_TILES)] + [s]

    nk_rows = token_rows(nk_prompt, nk_sample, "h d")
    nv_rows = token_rows(nv_prompt, nv_sample, "h d")
    ni_rows = token_rows(ni_prompt, ni_sample, "d")
    GR = P // NPAGE
    RP = PAGE // GR
    k_groups = cache_k[0].rearrange("n (g r) h d -> (n g) (r h d)", g=GR)
    v_groups = cache_v[0].rearrange("n (g r) h d -> (n g) (r h d)", g=GR)
    i_groups = cache_idx_k[0].rearrange("n (g r) d -> (n g) (r d)", g=GR)
    w_in_v = w_in[0].rearrange("(k p) n -> p k n", p=P)

    ctx = ExitStack()
    with ctx:
        AW = 53200
        arena = ctx.enter_context(nc.sbuf_tensor("arena", [P, AW], F32))
        psum = ctx.enter_context(nc.psum_tensor("psum", [P, 8 * 512], F32))
        sems = {}

        def sem(name):
            sems[name] = ctx.enter_context(nc.semaphore(name))
            return sems[name]

        def at(off, *dims, rows=P):
            n = int(np.prod(dims))
            assert off + n <= AW, (off, dims)
            v = arena[0:rows, off:off + n]
            if len(dims) == 2:
                return v.rearrange("p (a b) -> p a b", b=dims[1])
            if len(dims) == 3:
                return v.rearrange("p (a b c) -> p a b c", b=dims[1], c=dims[2])
            return v

        def const(name, rows=P):
            o, n = where[name]
            return arena[0:rows, o:o + n]

        def bank(b, n=512, rows=slice(0, P), at0=0):
            return psum[rows, b * 512 + at0:b * 512 + at0 + n]

        cst_w = sum(n for _, n in where.values())
        XNT = 4160
        ATT = XNT + KD * NT
        POT = ATT + 4 * NT
        RING = POT + 4 * NT
        SLOT = KD * 512
        SMALL = RING + 2 * SLOT
        assert cst_w <= XNT - 80
        xnT = at(XNT, KD, NT)
        attnT = at(ATT, 4, NT)
        poT = at(POT, 4, NT)
        ring = [at(RING + s * SLOT, KD, 512) for s in range(2)]
        stats = at(XNT - 64, 64)
        gain1 = stats[:, 0:8]
        gain2 = stats[:, 8:16]
        pscale = stats[:, 16:20]
        ss1, rt1, rstd1 = stats[:, 20:25], stats[:, 25:30], stats[:, 30:35]
        ss2, rt2, rstd2 = stats[:, 35:40], stats[:, 40:45], stats[:, 45:50]
        ss3, rt3, rstd3 = stats[:, 50:55], stats[:, 55:60], stats[:, 20:25]
        eps = stats[:, 60:61]
        warm = stats[:, 61:62]
        o = SMALL
        kiT2 = at(o, NT); o += NT
        vnat = at(o, TILES, NKV * HD); o += TILES * NKV * HD
        kT = at(o, 2, NT); o += 2 * NT
        qs = at(o, DB, 2, 32); o += DB * 64
        wiS = at(o, TILES, NI); o += TILES * NI
        w2T = at(o, NS, rows=NI); o += NS
        expand_b = arena[0:NS, o:o + 256].bitcast(BF16); o += 256
        cols = at(o, 40); o += 40
        KIR = o
        kir = at(o, TILES, P); o += TILES * P
        kiraw = at(o, TILES, HD); o += TILES * HD
        raw = [at(o + s * 512, 512) for s in range(2)]; o += 1024
        roped = [at(o + s * 1024, 1024) for s in range(2)]; o += 2048
        rtmp = [at(o + s * 512, 512) for s in range(2)]; o += 1024
        MP = o
        maskp = {i: at(MP + P * (i * (i + 1) // 2 - 1), P * (i + 1)) for i in range(1, PT_TILES)}
        o += P * 9
        msk = arena[0:NS, o:o + LS // 2].bitcast(BF16); o += LS // 2
        QZ = o
        qz = at(o, NH, SEQ)
        idxk = at(o, DB, RP * HD)
        o += NH * SEQ
        ZA = o
        score = {i: at(ZA + P * (i * (i + 1) // 2 - 1), P * (i + 1)) for i in range(1, PT_TILES)}
        o = ZA + P * 9
        sc_s = at(o, LS, rows=NS); o += LS
        work = at(o, LS); o += LS
        gtm = at(o, LS); o += LS
        eqm = at(o, LS); o += LS
        rnk = at(o, LS); o += LS
        ZB = o
        o = ZA
        ml = [at(o + s * 512, 512) for s in range(2)]; o += 1024
        prob = [at(o + s * 512, 512) for s in range(2)]; o += 1024
        probT = [at(o + s * 512, 4, P) for s in range(2)]; o += 1024
        o = ZA
        probs = at(o, LS); o += LS
        probsT = at(o, 9, P); o += 9 * P
        onat = at(o, NKV * HD); o += NKV * HD
        o = max(o, ZA + 3072)
        kTb1 = at(o, 2, LS); o += 2 * LS
        assert o <= ZB
        o = ZB
        xin = [at(ZB + i * D, D) for i in range(TILES)]
        qiz = [at(o + s * 1024, NI, P) for s in range(2)]; o += 2048
        qlo = at(o, DB, 64); o += 512
        qhi = at(o, DB, 64); o += 512
        kst = at(o, 2, 512); o += 1024
        rls = at(o, LS); o += LS
        wl = at(o, DB // 2, NS); o += DB // 2 * NS
        rl = [at(o + s * 512, 512) for s in range(2)]; o += 1024
        xs = [at(o + s * D, D) for s in range(2)]
        unat = at(o, TILES, UW)
        o += 2560
        kiww = at(o, KD, KIW); o += KD * KIW
        hist = at(o, UW); o += UW
        wpool = at(o, NG, P); o += NG * P
        assert o <= AW
        kb = at(ZB, 2, RP * 256)
        vb = at(ZB + 4096, 2, RP * 256)
        kTb = [at(ZB + 8192, 2, LS), kTb1]
        vnew = at(KIR, DB, 256, rows=DS)
        BANDS, GAR = where["bandcur"][0], KIR + 2048
        assert where["causal"][0] >= BANDS + 4 * NT and GAR + 4 * NT <= MP
        sgA = [at(BANDS + k * NT, NT) for k in range(4)] + [at(GAR + k * NT, NT) for k in range(4)]
        gb_raw = [at(ZB - 2 * NT + k * NT, NT) for k in range(2)] + [at(MP, NT)] + [at(QZ + k * NT, NT) for k in range(4)]
        assert ZA + 3072 + 2 * LS <= ZB - 2 * NT and NT <= 5 * P
        pgi = at(XNT - 80, 8).bitcast(I32)
        gidx = at(XNT - 72, 8).bitcast(I32)
        dT = attnT
        rmax, nmax, esum, rsum = (cols[:, 4 * j:4 * j + 4] for j in range(4))
        smax, snmax, ssum, srec = (cols[:, 25 + j:26 + j] for j in range(4))
        o = SMALL
        SG = o
        sgB = [at(o + k * NT, NT) for k in range(KD)]
        assert SG + KD * NT <= GAR
        o = GAR + 4 * NT
        W0 = max(o, SG + 7000); o = W0 + 12288
        resid = at(o, TILES, D); o += TILES * D
        g2row = at(o, D); o += D
        fgrow = at(o, D); o += D
        wr = at(o, KD, P); o += KD * P
        rbias = at(o, EG + NE); o += EG + NE
        lg = at(o, TILES, EG + NE); o += TILES * (EG + NE)
        RT = o
        t32 = [at(o + j * 160, TILES, NE) for j in range(5)]; o += 800
        gmax, least, top1, top2, vdf, vex, gw, s1, s2, w1, w2, w_lo, w_hi = (at(o + j * TILES, TILES) for j in range(13)); o += 13 * TILES
        ghot, gsh, gex = (at(o + j * TILES * EG, TILES, EG) for j in range(3)); o += 3 * TILES * EG
        ab = at(o, 80).bitcast(BF16).rearrange("p (t e) -> p t e", e=NE); o += 80
        dest = arena[:, o:o + 2 * TILES].bitcast(I32).rearrange("p (k t) -> p k t", t=TILES); o += 2 * TILES
        toki = arena[:, o:o + TILES].bitcast(I32); o += TILES
        flag = arena[:, o:o + 1].bitcast(I32); o += 1
        assert o <= AW, o
        W1 = SMALL - 12288
        assert W1 - D >= XNT + 4096 and SG + 128 + 5 * D <= GAR
        wg2 = at(XNT, KD, DE)
        o = SG + 128
        xs2 = [at(o, D), at(W1 - D, D)]
        xn2 = [at(o + D + s * D, D) for s in range(2)]
        xn2T = [at(o + 3 * D + s * D, KD, P) for s in range(2)]
        wu2 = [at(BANDS, 4, DE), at(GAR, 4, DE)]
        o = SG
        trib = at(o, 64).bitcast(BF16); o += 64
        oneb = at(o, 64).bitcast(BF16); o += 64
        xg = [at(o + s * D, D, rows=CAP) for s in range(2)]; o += 2 * D
        xT = [at(o + s * 512, KD, CAP) for s in range(2)]; o += 1024
        sg = [at(o + s * 512, DE, rows=CAP) for s in range(2)]; o += 1024
        hb = [at(o + s * 512, DE, rows=CAP) for s in range(2)]; o += 1024
        hT = [at(o + s * 256, KE, CAP) for s in range(2)]; o += 512
        yo = [at(W1 - D + s * 512, 512) for s in range(2)]
        onehot = at(SG + 128 + 4 * D, TILES, 2, CAP)
        assert TILES * 2 * CAP <= D and 2 * CAP == P
        sidx = [arena[0:CAP, o + s:o + s + 1].bitcast(I32) for s in range(2)]; o += 2
        slots = arena[0:CAP, o:o + NE].bitcast(I32); o += NE
        assert o <= GAR
        wg = [at(b, KD, DE) for b in (W0, W1)]
        wu = [at(b + 4096, KD, DE) for b in (W0, W1)]
        wd = [at(b + 8192, KE, D) for b in (W0, W1)]
        zeros = at(W1, 8 * D)
        YZ = (SLOTS - FIRST) // (8 * P)
        yg = [[at(W0 + (TILES * k + i) * D, D) for k in range(2)] for i in range(TILES)]
        yout = [at(W1 + i * D, D) for i in range(TILES)]

        xn2_d = nc.dram_tensor("xn2_d", (NT, D), F32, kind="Internal").ap()
        tab_d = nc.dram_tensor("tab_d", (SLOTS, 1), I32, kind="Internal").ap()
        y_d = nc.dram_tensor("y_d", (SLOTS, D), F32, kind="Internal").ap()

        ident = const("ident")
        tab3 = {n: const(n).rearrange("p (t c) -> p t c", c=HALF) for n in ("cos", "nsin", "sin")}
        band = {n: const(n).rearrange("p (g c) -> p g c", g=NG)
                for n in ("bandcur", "bandprev", "bandfirst", "bandnew", "bandhist")}
        dmask = const("dmask").rearrange("p (b c) -> p b c", c=NS)
        expand_f = const("expand", NS)

        S = {n: sem(n) for n in ("""
            const_in const2_in page_in gain_in kiww_in hist_in wpool_in vnew_in late_in st_ready
            gi_ready sq_done rt_done rstd_ready xs_ready xt_done xn_ready
            jp je ki_roped rope_done tp te qiz_zero qz_zero qs_zero wr_zero
            wi_done wl_ready is_done rl_ready acc_done ss_done ss_relu sw_done acc_ev 
            ki_out v_out u_out hist_out dt_done dt_ev po_done po_ev
            lg_done ml_done mx_done ex_done pn_done pv_done ot_ev mask_s ebf_ready
            sl_done smx_done sex_done srec_done spv_done son_done sot_done sot_ev knew_ev att_all
            g_done raw_ev gs_done gate_ev br_ev m_done h_done h_add sq2 rt2 rs2 xs2_r x2t x2e xn2_r r_done r_add
            gexp_in gexp_out tri_ready a_ready rank_done flag_ready zero_st zero_w dest_ready sc_st
            y_comb sq3 rt3 rs3 fin_ready y_out part_in sidx_set oh_ready tok_done tok_out sidx_in slots_in dvc plc passed y_zero""").split()}
        s_x = [sem(f"x_in{i}") for i in range(TILES)]
        s_y = [sem(f"y_rows_in{i}") for i in range(TILES)]
        s_res = sem("resid_in")
        s_ring = [sem(f"ring_in{s}") for s in range(2)]
        s_rs = [sem(f"roped_stored{s}") for s in range(2)]
        s_idx = sem("idxpage_in")
        s_kin = [sem(f"kpage_in{b}") for b in range(2)]
        s_vin = [sem(f"vpage_in{b}") for b in range(2)]
        s_xst = [sem(f"xn2_stored{s}") for s in range(2)]
        M = [{n: sem(f"{n}{s}") for n in
              ("wg_in wu_in wd_in xg_in xt_done xt_ev gu_done silu h_ready "
               "ht_done ht_ev y_done y_ev y_st").split()} for s in range(2)]
        OV, N0 = M[0], NE // 2

        RING_LOADS = [w_in_v[:, :, c:c + 512] for c in (C_QI, C_Q, C_K, C_U)]
        RING_LOADS += [w_in_v[:, :, c + 512 * mg:c + 512 * mg + 512] for c in (C_GA, C_GB) for mg in range(2)]
        RING_LOADS += [("branch", mg) for mg in range(2)]
        w_out_v = w_out[0].rearrange("(k p) n -> p k n", p=P)
        RING_LOADS += [w_out_v[:, :, 0:512], w_out_v[:, :, 512:1024]]
        R_QI, R_Q, R_KV, R_U, R_GATES, R_OUT = 0, 1, 2, 3, 4, 10
        ring_total = [0, 0]
        RING_AT = []
        for n, what in enumerate(RING_LOADS):
            ring_total[n % 2] += 32 if isinstance(what, tuple) else 16
            RING_AT.append(ring_total[n % 2])

        RING_USED = [(S["jp"], v) for v in (9, 14, 19, 24)] + [(S["g_done"], v) for v in (8, 16, 24, 32, 48, 64)]
        PRE, SAMPLE_G = 6, 22
        EARLY = SAMPLE_G + DB
        assert PRE <= 8 and EARLY <= 32 and EARLY - 16 <= 2 * len(gb_raw)

        QI_ORDER = [1, 2, 3, 4]
        JOBS = [("qi", i) for i in QI_ORDER] + [("q", i) for i in range(TILES)] + [("k", i) for i in range(TILES)]
        T_JOB = [3, 4, 5, 6] + list(range(15, 25))
        T0 = T_JOB[-1]
        stored = {s: 0 for s in range(2)}
        STORED_AT = []
        for n, (kind, _) in enumerate(JOBS):
            if kind == "k":
                stored[n % 2] += 16
            STORED_AT.append(stored[n % 2])

        def stores_done(eng):
            eng.wait_ge(S["ki_out"], 16 * TILES)
            eng.wait_ge(S["v_out"], 16 * TILES)
            eng.wait_ge(S["u_out"], 32)
            for s in range(2):
                eng.wait_ge(s_rs[s], stored[s])

        block = ctx.enter_context(nc.Block())

        @block.sync
        def _(sp):
            c0 = where["lane"][0] + 1
            sp.dma_start(arena[:, 0:c0], consts[:, 0:c0]).then_inc(S["const_in"], 16)
            for i in range(TILES):
                sp.dma_start(xin[i][0:rows_of(i), :], x_rows[i]).then_inc(s_x[i], 16)
            with nc.allow_non_contiguous_dma(reason="a few small columns"):
                for j in range(NPAGE):
                    src = page_table[:, j:j + 1].rearrange("b j -> j b").to_broadcast([GR, DB])
                    sp.dma_start(pgi[GR * j:GR * (j + 1), :], src).then_inc(S["page_in"], 16)
                sp.dma_start(gain1, attn_norm_g[0].rearrange("(k p) -> p k", p=P)).then_inc(S["gain_in"], 16)
                sp.dma_start(pscale, pool_scale[0].rearrange("(k p) -> p k", p=P)).then_inc(S["gain_in"], 16)
                sp.dma_start(gain2, ffn_norm_g[0].rearrange("(k p) -> p k", p=P)).then_inc(S["gain_in"], 16)
                sp.dma_start(kiww, w_in_v[:, :, C_KI:C_KI + KIW]).then_inc(S["kiww_in"], 16)

            def load_ring(n):
                if n >= 2:
                    sp.wait_ge(*RING_USED[n - 2])
                s, what = n % 2, RING_LOADS[n]
                if isinstance(what, tuple):
                    c = slice(512 * what[1], 512 * what[1] + 512)
                    sp.dma_start(ring[s][:, 0:4, :], w_branch_attn[0].rearrange("(k p) n -> p k n", p=P)[:, :, c]).then_inc(s_ring[s], 16)
                    sp.dma_start(ring[s][:, 4:8, :], w_branch_pool[0].rearrange("(k p) n -> p k n", p=P)[:, :, c]).then_inc(s_ring[s], 16)
                else:
                    sp.dma_start(ring[s], what).then_inc(s_ring[s], 16)

            load_ring(0)
            sp.dma_start(arena[:, c0:cst_w], consts[:, c0:]).then_inc(S["const2_in"], 16)
            sp.dma_start(hist[0:DB * HIST, :], state_pool[0].rearrange("b t c -> (b t) c")).then_inc(S["hist_in"], 16)
            sp.dma_start(wpool, w_pool[0].rearrange("g c d -> c g d")).then_inc(S["wpool_in"], 16)
            sp.dma_start(np_sample[0, :, 0:HIST - DS, :], state_pool[0, :, DS:HIST, :]).then_inc(S["hist_out"], 16)
            for n in range(1, 5):
                load_ring(n)
            sp.wait_ge(S["je"], 19)
            sp.wait_ge(S["tp"], T_JOB[-1])
            for s in range(2):
                sp.wait_ge(s_rs[s], stored[s])
            sp.wait_ge(S["ki_out"], 16 * TILES)
            for b in range(DB):
                sp.dma_start(vnew[:, b, :], vnat[b * DS:(b + 1) * DS, PT_TILES, :]).then_inc(S["vnew_in"], 16)
            for n in range(5, 8):
                load_ring(n)
            sp.wait_ge(S["att_all"], 1)
            stores_done(sp)
            load_ring(8)
            sp.wait_ge(S["gs_done"], len(gb_raw))
            for i in range(TILES):
                sp.dma_start(resid[0:rows_of(i), i, :], x_rows[i]).then_inc(s_res, 16)
            with nc.allow_non_contiguous_dma(reason="router weights and rows for all partitions"):
                sp.dma_start(g2row, ffn_norm_g.to_broadcast([P, D])).then_inc(S["late_in"], 16)
                sp.dma_start(fgrow, final_norm_g.unsqueeze(0).to_broadcast([P, D])).then_inc(S["late_in"], 16)
                sp.dma_start(rbias[:, 0:EG], b_router_group.to_broadcast([P, EG])).then_inc(S["late_in"], 16)
                sp.dma_start(rbias[:, EG:], b_router_expert.to_broadcast([P, NE])).then_inc(S["late_in"], 16)
                sp.wait_ge(S["wr_zero"], 1)
                sp.dma_start(wr[:, :, 0:EG], w_router_group[0].rearrange("(k p) n -> p k n", p=P)).then_inc(S["late_in"], 16)
                sp.dma_start(wr[:, :, EG:EG + NE], w_router_expert[0].rearrange("(k p) n -> p k n", p=P)).then_inc(S["late_in"], 16)
            g_v = w_exp_gate[0].rearrange("e (p k) n -> e p (k n)", k=KD)
            u_v = w_exp_up[0].rearrange("e (p k) n -> e p (k n)", k=KD)
            d_v = w_exp_down[0].rearrange("e (p k) n -> e p (k n)", k=KE)

            def flat(t):
                return t.rearrange("p k n -> p (k n)")

            def load_expert(i, s, first=False, gate=True, up=True):
                e = 2 * i + s
                m = M[s]
                if up and not first:
                    sp.wait_ge(m["gu_done"], i)
                if gate:
                    sp.dma_start(flat(wg[s]), g_v[bass.ds(e, 1), :, :].squeeze(0)).then_inc(m["wg_in"], 16)
                if up:
                    sp.dma_start(flat(wu[s]), u_v[bass.ds(e, 1), :, :].squeeze(0)).then_inc(m["wu_in"], 16)
                if not first:
                    sp.wait_ge(m["y_done"], i)
                sp.dma_start(flat(wd[s]), d_v[bass.ds(e, 1), :, :].squeeze(0)).then_inc(m["wd_in"], 16)

            load_expert(0, 0, first=True)
            load_ring(9)
            sp.wait_ge(M[0]["wg_in"], 16)
            sp.dma_start(flat(wg2), g_v[2]).then_inc(M[0]["wg_in"], 16)
            load_ring(10)
            load_ring(11)
            sp.dma_start(flat(wg[1]), g_v[1]).then_inc(M[1]["wg_in"], 16)
            sp.wait_ge(S["h_done"], TILES)
            sp.dma_start(flat(wu[1]), u_v[1]).then_inc(M[1]["wu_in"], 16)
            sp.wait_ge(s_xst[0], 48)
            sp.wait_ge(s_xst[1], 32)
            sp.dma_start(flat(wd[1]), d_v[1]).then_inc(M[1]["wd_in"], 16)
            sp.wait_ge(M[1]["xg_in"], 16)
            sp.dma_start(flat(wu2[0]), u_v[2, :, 0:4 * DE]).then_inc(S["part_in"], 16)
            sp.dma_start(flat(wu2[1]), u_v[2, :, 4 * DE:]).then_inc(M[0]["wu_in"], 16)
            sp.wait_ge(M[0]["gu_done"], 1)
            sp.wait_ge(M[0]["wg_in"], 32)
            sp.dma_start(flat(wg[0]), g_v[4]).then_inc(M[0]["wg_in"], 16)
            load_expert(1, 0, gate=False, up=False)
            sp.wait_ge(M[0]["wu_in"], 32)
            sp.dma_start(flat(wu[0]), u_v[4]).then_inc(M[0]["wu_in"], 16)
            load_expert(1, 1)
            load_expert(2, 0, gate=False, up=False)
            load_expert(2, 1)
            with sp.Fori(3, NE // 2 - 1) as i:
                for s in range(2):
                    load_expert(i, s)
            load_expert(NE // 2 - 1, 0)
            sp.wait_ge(M[1]["gu_done"], NE // 2 - 1)
            for half, names in enumerate((("part_in", "part_in"), ("wg_in", "wu_in"))):
                ks = slice(4 * half, 4 * half + 4)
                for w, v, name in zip((wg[1], wu[1]), (g_v, u_v), names):
                    sp.dma_start(flat(w[:, ks, :]), v[NE - 1, :, 4 * half * DE:4 * (half + 1) * DE]).then_inc((M[1] if half else S)[name], 16)
            sp.wait_ge(M[1]["y_done"], NE // 2 - 1)
            sp.dma_start(flat(wd[1]), d_v[NE - 1]).then_inc(M[1]["wd_in"], 16)
            sp.wait_ge(S["flag_ready"], 1)
            over = sp.value_load(flag[0:1, 0:1], min_val=0, max_val=NT)
            with sp.If(over > CAP):
                with sp.Fori(0, NE) as e:
                    sp.wait_ge(OV["y_done"], e * NB + N0)
                    sp.dma_start(flat(wg[0]), g_v[bass.ds(e, 1), :, :].squeeze(0)).then_inc(OV["wg_in"], 16)
                    sp.dma_start(flat(wu[0]), u_v[bass.ds(e, 1), :, :].squeeze(0)).then_inc(OV["wu_in"], 16)
                    sp.dma_start(flat(wd[0]), d_v[bass.ds(e, 1), :, :].squeeze(0)).then_inc(OV["wd_in"], 16)
            with sp.Else():
                sp.nop()
            for i in range(TILES):
                sp.wait_ge(S["fin_ready"], i + 1)
                sp.dma_start(y_rows[i], yout[i][0:rows_of(i), :]).then_inc(S["y_out"], 16)
            sp.wait_ge(S["y_out"], 16 * TILES)
            sp.wait_ge(S["hist_out"], 16)
            stores_done(sp)

        @block.tensor
        def _(pe):
            jn, tn = [0], [0]

            def j_bank():
                if jn[0] >= 2:
                    pe.wait_ge(S["je"], jn[0] - 1)
                jn[0] += 1
                return 2 + (jn[0] - 1) % 2

            def t_bank():
                if tn[0] >= 2:
                    pe.wait_ge(S["te"], tn[0] - 1)
                tn[0] += 1
                return (tn[0] - 1) % 2

            def project(i, w, n, late=None):
                r = rows_of(i)
                b = j_bank()
                for k in range(KD):
                    if late and k == KD - 2:
                        late()
                    lhs = xnT[:, k, i * P:i * P + r]
                    if split_rows(i, n):
                        for half in range(2):
                            last = pe.matmul(bank(b, n // 2, slice(64 * half, 64 * half + 64)), lhs, w[:, k, n // 2 * half:n // 2 * half + n // 2],
                                             start=(k == 0), stop=(k == KD - 1))
                    else:
                        last = pe.matmul(bank(b, n, slice(0, r)), lhs, w[:, k, 0:n], start=(k == 0), stop=(k == KD - 1))
                last.then_inc(S["jp"], 1)

            def ring_ready(n):
                pe.wait_ge(s_ring[n % 2], RING_AT[n])

            def first_product(i):
                if i == 0:
                    pe.wait_ge(S["kiww_in"], 16)
                pe.wait_ge(S["xn_ready"], 2 * (i + 1))
                project(i, kiww, KIW)

            pe.wait_ge(S["const_in"], 16)
            for i in range(TILES):
                r = rows_of(i)
                pe.wait_ge(S["xs_ready"], i + 1)
                for half in range(2):
                    g = 2 * i + half
                    if g >= 2:
                        pe.wait_ge(S["xn_ready"], g - 1)
                    for k in range(4):
                        kk = 4 * half + k
                        last = pe.transpose(bank(g % 2, r, at0=k * P), xs[i % 2][0:r, kk * P:(kk + 1) * P], ident[0:r, 0:r])
                    last.then_inc(S["xt_done"], 1)
                if i:
                    first_product(i - 1)
            first_product(TILES - 1)
            ring_ready(R_QI)
            project(QI_ORDER[0], ring[0], 512)
            def turn(job, n_blocks, rows, width):
                pe.wait_ge(S["rope_done"], job + 1)
                b = t_bank()
                for k in range(n_blocks):
                    last = pe.transpose(bank(b, rows, at0=k * width), roped[job % 2][0:rows, k * P:(k + 1) * P], ident[0:rows, 0:rows])
                last.then_inc(S["tp"], 1)

            def turn_keys():
                pe.wait_ge(S["ki_roped"], PT_TILES)
                b = t_bank()
                for i in range(PT_TILES):
                    last = pe.transpose(bank(b, P, at0=i * P), kir[:, i, :], ident)
                last.then_inc(S["tp"], 1)
                pe.wait_ge(S["ki_roped"], TILES)
                b = t_bank()
                pe.transpose(bank(b, NS), kir[0:NS, PT_TILES, :], ident[0:NS, 0:NS])
                pe.wait_ge(S["je"], TILES)
                pe.transpose(bank(b, NS, slice(0, NI), at0=NS), wiS[0:NS, PT_TILES, :], ident[0:NS, 0:NS]).then_inc(S["tp"], 1)

            def index_prompt(j):
                i = QI_ORDER[j]
                L = P * (i + 1)
                for h in range(NI):
                    u = j * NI + h
                    if h == 0:
                        pe.wait_ge(S["te"], tn[0])
                    if u >= 2:
                        pe.wait_ge(S["rl_ready"], u - 1)
                    pe.matmul(bank(4 + u % 2, L), qiz[j % 2][:, h, :], kiT2[:, 0:L], start=True, stop=True).then_inc(S["is_done"], 1)

            project(QI_ORDER[1], ring[0], 512, late=turn_keys)
            for j in range(3):
                if j < 2:
                    project(QI_ORDER[j + 2], ring[0], 512, late=lambda: turn(j, 4, P, P))
                else:
                    ring_ready(R_Q)
                    project(0, ring[R_Q % 2], 512, late=lambda: turn(j, 4, P, P))
                index_prompt(j)
            turn(3, 8, NS, NS)
            pe.wait_ge(S["te"], tn[0])
            pe.wait_ge(S["rl_ready"], 3 * NI)
            pe.wait_ge(S["const2_in"], 16)
            pe.matmul(bank(6, NS), const("headrep", NI), w2T, start=True, stop=True).then_inc(S["wi_done"], 1)
            pe.wait_ge(S["je"], jn[0])
            pe.wait_ge(S["wl_ready"], 1)
            def turn_pages(bp):
                for b2 in range(2):
                    b = t_bank()
                    for rr in range(4):
                        last = pe.transpose(bank(b, P, at0=rr * P), idxk[:, 2 * bp + b2, rr * P:(rr + 1) * P], ident)
                    last.then_inc(S["tp"], 1)

            pe.wait_ge(s_idx, 16 * DB)
            turn_pages(0)
            for bp in range(DB // 2):
                if bp:
                    pe.wait_ge(S["ss_relu"], bp)
                pe.wait_ge(S["te"], tn[0])
                for par, q in enumerate((qlo, qhi)):
                    for b2 in range(2):
                        pe.matmul(bank(4 + par, 512, slice(64 * b2, 64 * b2 + 64)), q[:, 2 * bp + b2, :], kst[:, b2, :], start=True, stop=True)
                for b2 in range(2):
                    bb = 2 * bp + b2
                    last = pe.matmul(bank(6, DS, slice(64 * b2, 64 * b2 + 64)), qlo[:, bb, :],
                                     kiT2[:, SEQ + bb * DS:SEQ + (bb + 1) * DS], start=True, stop=True)
                last.then_inc(S["ss_done"], 1)
                if bp < DB // 2 - 1:
                    turn_pages(bp + 1)
                pe.wait_ge(S["ss_relu"], bp + 1)
                for c, (b, n) in enumerate(((2, 512), (3, 512), (7, DS))):
                    last = pe.matmul(bank(b, n, slice(0, NS)), wl[:, bp, :], rls[:, 512 * c:512 * c + n],
                                     start=(bp == 0), stop=(bp == DB // 2 - 1), skip_group_check=True)
                last.then_inc(S["sw_done"], 1)
            pe.wait_ge(S["acc_ev"], 3)
            for what, slot, first in (("q", R_Q, 4), ("k", R_KV, 9), ("u", R_U, 14)):
                ring_ready(slot)
                for i in range(TILES):
                    if what != "q" or i:
                        project(i, ring[slot % 2], 512)
                    if i == 0:
                        if what == "k":
                            turn(first - 1, 8, NS, NS)
                        elif what == "u":
                            turn(first - 1, 2, NS, P)
                    elif what != "u":
                        turn(first + i - 1, 4 if what == "q" else 2, rows_of(i - 1), P)
            pe.wait_ge(S["hist_in"], 16)
            for i in range(TILES):
                r = rows_of(i)
                pe.wait_ge(S["je"], jn[0] - TILES + i + 1)
                if i >= 2:
                    pe.wait_ge(S["dt_ev"], i - 1)
                for g in range(NG):
                    out = bank(4 + i % 2, r, at0=g * P)
                    c = slice(g * P, (g + 1) * P)
                    if i == 0:
                        last = pe.matmul(out, unat[:, 0, c], band["bandfirst"][:, g, :], start=True, stop=True)
                    elif i < PT_TILES:
                        pe.matmul(out, unat[:, i - 1, c], band["bandprev"][:, g, :], start=True, stop=False)
                        last = pe.matmul(out, unat[:, i, c], band["bandcur"][:, g, :], start=False, stop=True)
                    else:
                        pe.matmul(out, hist[0:DB * HIST, c], band["bandhist"][0:DB * HIST, g, :], start=True, stop=False)
                        last = pe.matmul(out, unat[0:NS, i, c], band["bandnew"][0:NS, g, :], start=False, stop=True)
                last.then_inc(S["dt_done"], 1)
            pe.wait_ge(S["dt_ev"], TILES)
            pe.wait_ge(S["wpool_in"], 16)
            for g in range(NG):
                if g >= 2:
                    pe.wait_ge(S["po_ev"], g - 1)
                pe.matmul(bank(6 + g % 2), wpool[:, g, :], dT[:, g, 0:SEQ], start=True, stop=True)
                pe.matmul(bank(4 + g % 2, NS), wpool[:, g, :], dT[:, g, SEQ:NT], start=True, stop=True).then_inc(S["po_done"], 1)
            units = [(i, h) for i in range(PT_TILES) for h in range(NH)]
            U = len(units)
            pe.wait_ge(S["te"], tn[0])
            t0 = tn[0]

            def gate_part(n, k0, k1):
                slot, m, hh = R_GATES + n // 8, n % 8 // 2, n % 2
                if k0 == 0:
                    if n % 8 == 0:
                        ring_ready(slot)
                    if n >= 2:
                        pe.wait_ge(S["raw_ev"], n - 1 if n <= SAMPLE_G else n)
                for k in range(k0, k1):
                    last = pe.matmul(bank(2 + n % 2 if n < SAMPLE_G else 2, HN), ring[slot % 2][:, k, m * P:(m + 1) * P],
                                     xnT[:, k, HN * hh:HN * hh + HN], start=(k == 0), stop=(k == KD - 1))
                if k1 == KD:
                    last.then_inc(S["g_done"], 1)

            for n in range(PRE):
                gate_part(n, 0, KD)
            for u in range(U + 2):
                if u < U:
                    i, h = units[u]
                    if u < 2:
                        pe.wait_ge(S["po_ev"], NG - 1 + u)
                    else:
                        pe.wait_ge(S["ml_done"], u - 1)
                    pe.matmul(bank(4 + u % 2, P * (i + 1)), qz[:, h, i * P:(i + 1) * P], kT[:, h // 4, 0:P * (i + 1)],
                              start=True, stop=True).then_inc(S["lg_done"], 1)
                    gate_part(PRE + u // 2, KD // 2 * (u % 2), KD // 2 * (u % 2 + 1))
                if 1 <= u <= U:
                    i, h = units[u - 1]
                    pe.wait_ge(S["pn_done"], u)
                    b = t_bank()
                    for j in range(i + 1):
                        last = pe.transpose(bank(b, P, at0=j * P), prob[(u - 1) % 2][:, j * P:(j + 1) * P], ident)
                    last.then_inc(S["tp"], 1)
                if u >= 2:
                    v = u - 2
                    i, h = units[v]
                    pe.wait_ge(S["te"], t0 + v + 1)
                    if h % 2 == 0 and v >= 4:
                        pe.wait_ge(S["ot_ev"], v // 2 - 1)
                    half = slice(64 * (h % 2), 64 * (h % 2) + 64)
                    for j in range(i + 1):
                        last = pe.matmul(bank(6 + (v // 2) % 2, P, half), vnat[:, j, (h // 2) * HD:(h // 2 + 1) * HD],
                                         probT[v % 2][:, j, :], start=(j == 0), stop=(j == i))
                    last.then_inc(S["pv_done"], 1)
            pe.wait_ge(S["ot_ev"], U // 2)
            pe.wait_ge(S["vnew_in"], 16 * DB)
            pe.wait_ge(S["ebf_ready"], 1)
            pe.wait_ge(S["mask_s"], 1)
            for bp in range(DB // 2):
                for b2 in range(2):
                    pe.wait_ge(s_kin[b2], 16 * (bp + 1))
                    for pr in range(2):
                        for rh in range(2):
                            b = t_bank()
                            for r in range(4):
                                c = (4 * rh + r) * 256 + pr * P
                                last = pe.transpose(bank(b, P, at0=r * P), kb[:, b2, c:c + P], ident)
                            last.then_inc(S["tp"], 1)
                gate_part(SAMPLE_G + 2 * bp, 0, 2)
                pe.wait_ge(S["te"], tn[0])
                pe.wait_ge(S["knew_ev"], bp + 1)
                if bp:
                    pe.wait_ge(S["sex_done"], bp)
                for c, n in enumerate((512, 512, DS)):
                    cs = slice(512 * c, 512 * c + n)
                    pe.matmul(bank(4 + c, n), expand_b[:, bp * P:(bp + 1) * P], msk[:, cs], start=True, stop=False, skip_group_check=True)
                    for b2 in range(2):
                        for pr in range(2):
                            at_row = 64 * b2 + 32 * pr
                            last = pe.matmul(bank(4 + c, n, slice(at_row, at_row + 32)), qs[:, 2 * bp + b2, pr, :], kTb[b2][:, pr, cs],
                                             start=False, stop=True, skip_group_check=True, tile_position=(0, at_row))
                last.then_inc(S["sl_done"], 1)
                gate_part(SAMPLE_G + 2 * bp, 2, KD)
                pe.wait_ge(S["sex_done"], bp + 1)
                for g in range(2):
                    b = t_bank()
                    for r in range(4):
                        last = pe.transpose(bank(b, P, at0=r * P), probs[:, (4 * g + r) * P:(4 * g + r + 1) * P], ident)
                    last.then_inc(S["tp"], 1)
                b = t_bank()
                pe.transpose(bank(b, P, slice(0, DS)), probs[:, PAST:LS], ident).then_inc(S["tp"], 1)
                gate_part(SAMPLE_G + 1 + 2 * bp, 0, 2)
                pe.wait_ge(S["te"], tn[0])
                if bp:
                    pe.wait_ge(S["son_done"], bp)
                for b2 in range(2):
                    pe.wait_ge(s_vin[b2], 16 * (bp + 1))
                    rows = slice(64 * b2, 64 * b2 + 64)
                    for r in range(RP):
                        pe.matmul(bank(7, 256, rows), probsT[:, r, 64 * b2:64 * b2 + 64], vb[:, b2, r * 256:(r + 1) * 256],
                                  start=(r == 0), stop=False)
                    last = pe.matmul(bank(7, 256, rows), probsT[0:DS, RP, 64 * b2:64 * b2 + 64], vnew[:, 2 * bp + b2, :],
                                     start=False, stop=True)
                last.then_inc(S["spv_done"], 1)
                gate_part(SAMPLE_G + 1 + 2 * bp, 2, KD)
                pe.wait_ge(S["son_done"], bp + 1)
                if bp:
                    pe.wait_ge(S["sot_ev"], bp)
                for pr in range(2):
                    last = pe.transpose(bank(3, P, at0=pr * P), onat[:, pr * P:(pr + 1) * P], ident)
                last.then_inc(S["sot_done"], 1)
            pe.wait_ge(S["sot_ev"], DB // 2)
            pe.sem_inc(S["att_all"], 1)
            evs = []
            counts = {"gate_ev": 0, "br_ev": 0}

            def g_bank():
                n = len(evs)
                if n >= 4:
                    name, v = evs[n - 4]
                    pe.wait_ge(S[name], v)
                return 4 + n % 4

            def g_evac(name):
                counts[name] += 1
                evs.append((name, counts[name]))

            for p3 in range(3):
                slot = R_GATES + 3 + p3
                ring_ready(slot)
                w = ring[slot % 2]
                for m in range((EARLY - 24) // 2 if p3 == 0 else 0, 4):
                    for hh in range(2):
                        tc = slice(HN * hh, HN * hh + HN)
                        if p3 == 0:
                            b = g_bank()
                            for k in range(KD):
                                last = pe.matmul(bank(b, HN), w[:, k, m * P:(m + 1) * P], xnT[:, k, tc], start=(k == 0), stop=(k == KD - 1))
                            last.then_inc(S["g_done"], 1)
                            g_evac("gate_ev")
                        else:
                            for br, src in enumerate((attnT, poT)):
                                b = g_bank()
                                for k in range(4):
                                    last = pe.matmul(bank(b, HN), w[:, 4 * br + k, m * P:(m + 1) * P], src[:, k, tc], start=(k == 0), stop=(k == 3))
                                last.then_inc(S["g_done"], 1)
                                g_evac("br_ev")
            ring_ready(R_OUT)
            pe.wait_ge(S["m_done"], KD * 2)
            pe.wait_ge(S["late_in"], 96)

            def out_proj(i, half):
                if i >= 2 and half == 0:
                    pe.wait_ge(S["h_add"], i - 1)
                if i == PT_TILES:
                    for k in range(4 * half, 4 * half + 4):
                        for c in range(2):
                            last = pe.matmul(bank(4, 512, slice(64 * c, 64 * c + 64)), sgA[k][:, SEQ:NT], ring[c][:, k, :],
                                             start=(k == 0), stop=(k == KD - 1))
                else:
                    for k in range(KD):
                        last = pe.matmul(bank(4 + 2 * (i % 2) + half), sgA[k][:, i * P:(i + 1) * P], ring[half][:, k, :],
                                         start=(k == 0), stop=(k == KD - 1))
                if half:
                    last.then_inc(S["h_done"], 1)

            def turn_2(i):
                r = rows_of(i)
                pe.wait_ge(S["h_add"], i + 1)
                for half in range(2):
                    g = 2 * i + half
                    if g >= 2:
                        pe.wait_ge(S["x2e"], g - 1)
                    for k in range(4):
                        kk = 4 * half + k
                        last = pe.transpose(bank(g % 2, r, at0=k * P), resid[0:r, i, kk * P:(kk + 1) * P], ident[0:r, 0:r])
                    last.then_inc(S["x2t"], 1)

            def route(i):
                r = rows_of(i)
                pe.wait_ge(S["x2e"], 2 * i + 2)
                if i >= 2:
                    pe.wait_ge(S["r_add"], i - 1)
                for k in range(KD):
                    last = pe.matmul(bank(2 + i % 2, P, slice(0, r)), xn2T[i % 2][:, k, 0:r], wr[:, k, :], start=(k == 0), stop=(k == KD - 1))
                last.then_inc(S["r_done"], 1)

            out_proj(0, 0)
            out_proj(1, 0)
            ring_ready(R_OUT + 1)
            out_proj(0, 1)
            out_proj(1, 1)
            for i in range(2, TILES):
                turn_2(i - 2)
                out_proj(i, 0)
                route(i - 2)
                if i == TILES - 1:
                    turn_2(i - 1)
                out_proj(i, 1)
            route(TILES - 2)
            turn_2(TILES - 1)
            route(TILES - 1)
            pe.wait_ge(S["a_ready"], 1)
            pe.wait_ge(S["tri_ready"], 1)
            pe.wait_ge(S["h_add"], TILES)
            for i in range(TILES + 1):
                for j in range(min(i, TILES - 1) + 1):
                    lhs = trib if j == i else oneb
                    last = pe.matmul(bank(4, NE, at0=i * NE), lhs, ab[:, j, :], start=(j == 0), stop=(j == min(i, TILES - 1)))
            last.then_inc(S["rank_done"], 1)

            pe.wait_ge(S["oh_ready"], 1)
            for i in range(TILES):
                last = pe.matmul(bank(5, 1), onehot[:, i, :, :].rearrange("p e r -> p (e r)"), const("tok")[:, i:i + 1],
                                 start=(i == 0), stop=(i == TILES - 1))
            last.then_inc(S["tok_done"], 1)

            def turn_x(m, s, n):
                pe.wait_ge(m["xg_in"], 16 * (n + 1))
                pe.sem_inc(S["passed"], 1)
                for k in range(KD):
                    last = pe.transpose(bank(0, CAP, at0=k * CAP), xg[s][:, k:KD * (P - 1) + k + 1:KD], ident[0:CAP, 0:CAP])
                last.then_inc(m["xt_done"], 1)

            def gate_up(m, s, n, third=False, halves=False):
                pe.wait_ge(m["xt_ev"], n + 1)
                for k in range(KD):
                    if halves and k == 4:
                        pe.wait_ge(m["wg_in"], 16 * (n + 1))
                        pe.wait_ge(m["wu_in"], 16 * (n + 1))
                    pair = (wg2[:, k, :], wu2[k // 4][:, k % 4, :]) if third else (wg[s][:, k, :], wu[s][:, k, :])
                    for half, w in enumerate(pair):
                        last = pe.matmul(bank(2 + s, 512, slice(64 * half, 64 * half + 64)), xT[s][:, k, :], w,
                                         start=(k == 0), stop=(k == KD - 1))
                last.then_inc(m["gu_done"], 1)

            def turn_h(m, s, n):
                pe.wait_ge(m["h_ready"], n + 1)
                pe.sem_inc(S["passed"], 1)
                for k in range(KE):
                    last = pe.transpose(bank(1, CAP, at0=k * CAP), hb[s][:, k:KE * (P - 1) + k + 1:KE], ident[0:CAP, 0:CAP])
                last.then_inc(m["ht_done"], 1)

            def down(m, s, n):
                pe.wait_ge(m["ht_ev"], n + 1)
                for k in range(KE):
                    for half in range(2):
                        last = pe.matmul(bank(4 + s, 512, slice(64 * half, 64 * half + 64)), hT[s][:, k, :], wd[s][:, k, 512 * half:512 * half + 512],
                                         start=(k == 0), stop=(k == KE - 1))
                last.then_inc(m["y_done"], 1)

            def expert_pair(i, last_pair=False):
                for s in range(2):
                    m = M[s]
                    halves = last_pair and s == 1
                    if halves:
                        pe.wait_ge(S["part_in"], 48)
                    else:
                        pe.wait_ge(m["wg_in"], 16 * (i + 1))
                        pe.wait_ge(m["wu_in"], 16 * (i + 1))
                    third = isinstance(i, int) and 2 * i + s == 2
                    if third:
                        pe.wait_ge(S["part_in"], 16)
                    gate_up(m, s, i, third, halves)
                    if not (last_pair and s == 1):
                        turn_x(M[1 - s], 1 - s, i + s)
                    turn_h(m, s, i)
                    pe.wait_ge(m["wd_in"], 16 * (i + 1))
                    down(m, s, i)

            turn_x(M[0], 0, 0)
            pe.wait_ge(S["flag_ready"], 1)
            expert_pair(0)
            expert_pair(1)
            with pe.Fori(2, NE // 2 - 1) as i:
                expert_pair(i)
            expert_pair(NE // 2 - 1, True)
            pe.wait_ge(S["flag_ready"], 1)
            over = pe.value_load(flag[0:1, 0:1], min_val=0, max_val=NT)
            with pe.If(over > CAP):
                with pe.Fori(0, NE) as e:
                    for w in ("wg_in", "wu_in", "wd_in"):
                        pe.wait_ge(OV[w], 16 * (e + N0 + 1))
                    pe.sem_inc(S["passed"], 1)
                    with pe.Fori(0, NB) as b:
                        n = e * NB + b + N0
                        turn_x(OV, 0, n)
                        gate_up(OV, 0, n)
                        turn_h(OV, 0, n)
                        down(OV, 0, n)
            with pe.Else():
                pe.nop()

        @block.scalar
        def _(act):
            tn = [0]

            def turned(*copies):
                tn[0] += 1
                act.wait_ge(S["tp"], tn[0])
                b = (tn[0] - 1) % 2
                for out, src in copies:
                    last = act.copy(out, src(b))
                last.then_inc(S["te"], 1)

            def scale_x(i):
                r = rows_of(i)
                act.wait_ge(S["rstd_ready"], i + 1)
                if i >= 2:
                    act.wait_ge(S["xt_done"], 2 * (i - 1))
                act.activation(xs[i % 2][0:r, :], xin[i][0:r, :], ACT.Copy, scale=rstd1[0:r, i:i + 1]).then_inc(S["xs_ready"], 1)

            act.wait_ge(S["st_ready"], 1)
            act.activation(warm, eps, ACT.Sqrt)
            for i in range(TILES):
                r = rows_of(i)
                act.wait_ge(s_x[i], 16)
                if i >= 2:
                    act.wait_ge(S["sq_done"], i - 1)
                act.activation(psum[0:r, (4 + 2 * (i % 2)) * 512:(4 + 2 * (i % 2)) * 512 + D], xin[i][0:r, :], ACT.Square,
                               accum_out=ss1[0:r, i:i + 1]).then_inc(S["sq_done"], 1)
                act.wait_ge(S["sq_done"], i + 1)
                act.activation(rt1[:, i:i + 1], ss1[:, i:i + 1], ACT.Sqrt, bias=eps, scale=1.0 / D).then_inc(S["rt_done"], 1)
                if i:
                    scale_x(i - 1)
            scale_x(TILES - 1)
            for i in range(TILES):
                r = rows_of(i)
                act.wait_ge(S["jp"], i + 1)
                act.copy(kiraw[0:r, i, :], bank(2 + i % 2, HD, slice(0, r)))
                act.activation(wiS[0:r, i, :], bank(2 + i % 2, NI, slice(0, r), HD), ACT.Copy,
                               scale=float(HD ** -0.5 * NI ** -0.5)).then_inc(S["je"], 1)

            def take_raw(job, jnum, n):
                r = rows_of(JOBS[job][1])
                act.wait_ge(S["jp"], jnum)
                if job >= 2:
                    act.wait_ge(S["rope_done"], job - 1)
                b = 2 + (jnum - 1) % 2
                i = JOBS[job][1]
                if split_rows(i, 512):
                    act.copy(raw[job % 2][0:r, 0:256], bank(b, 256, slice(0, r)))
                    dst = vnat[0:r, i, :] if JOBS[job][0] == "k" else raw[job % 2][0:r, 256:512]
                    last = act.copy(dst, bank(b, 256, slice(r, 2 * r)))
                else:
                    last = act.copy(raw[job % 2][0:r, 0:n], bank(b, n, slice(0, r)))
                    if JOBS[job][0] == "k":
                        last = act.copy(vnat[0:r, i, :], bank(b, NKV * HD, slice(0, r), n))
                last.then_inc(S["je"], 1)

            take_raw(0, 6, 512)
            turned((kiT2[:, 0:SEQ], lambda b: bank(b)))
            turned((kiT2[:, SEQ:NT], lambda b: bank(b, NS)), (w2T, lambda b: bank(b, NS, slice(0, NI), NS)))
            take_raw(1, 7, 512)
            act.wait_ge(S["qiz_zero"], 1)
            for j in range(3):
                if j >= 2:
                    act.wait_ge(S["is_done"], (j - 1) * NI)
                pairs = qiz[j % 2].rearrange("p (k a) t -> p k a t", a=2)
                turned(*[(pairs[64 * a:64 * a + 64, :, a, :],
                          lambda b, a=a: bank(b, 512, slice(64 * a, 64 * a + 64)).rearrange("p (k t) -> p k t", t=P))
                         for a in range(2)])
                take_raw(j + 2, 8 + j, 512)
                L = P * (QI_ORDER[j] + 1)
                for h in range(NI):
                    u = j * NI + h
                    act.wait_ge(S["is_done"], u + 1)
                    if u >= 2:
                        act.wait_ge(S["acc_done"], u - 1)
                    act.activation(rl[u % 2][:, 0:L], bank(4 + u % 2, L), ACT.Relu).then_inc(S["rl_ready"], 1)
            turned(*[(q[64 * a:64 * a + 64].rearrange("p b (h q) -> p b h q", q=DS),
                      lambda b, a=a: bank(b, 512, slice(64 * a, 64 * a + 64)).rearrange("p (h b q) -> p b h q", b=DB, q=DS))
                     for a, q in enumerate((qlo, qhi))])
            for b2 in range(2):
                turned((kst[:, b2, :], lambda b: bank(b)))
            for bp in range(DB // 2):
                act.wait_ge(S["ss_done"], bp + 1)
                if bp:
                    act.wait_ge(S["sw_done"], bp)
                act.activation(rls, psum[:, 4 * 512:4 * 512 + LS], ACT.Relu).then_inc(S["ss_relu"], 1)
                if bp < DB // 2 - 1:
                    for b2 in range(2):
                        turned((kst[:, b2, :], lambda b: bank(b)))
            act.wait_ge(S["sw_done"], DB // 2)
            natural = sc_s[:, 0:PAST].rearrange("q (p r) -> q r p", r=RP)
            for par in range(2):
                act.copy(natural[:, par::2, :], bank(2 + par, 512, slice(0, NS)).rearrange("q (r p) -> q r p", p=P)).then_inc(S["acc_ev"], 1)
            act.copy(sc_s[:, PAST:LS], bank(7, DS, slice(0, NS))).then_inc(S["acc_ev"], 1)

            def q_turned(i):
                if i < PT_TILES:
                    q4 = qz.rearrange("p (k a) t -> p k a t", a=2)
                    turned(*[(q4[64 * g:64 * g + 64, g::2, a, i * P:(i + 1) * P],
                              lambda b, g=g, a=a: bank(b, 512, slice(64 * a, 64 * a + 64)).rearrange("p (k t) -> p k t", t=P)[:, g::2, :])
                             for g in range(2) for a in range(2)])
                else:
                    copies = []
                    for pr in range(2):
                        for g in range(2):
                            out = qs[64 * g:64 * g + 64, :, pr, 16 * g:16 * g + 16].rearrange("p b (j q) -> p b j q", q=DS)
                            copies.append((out, lambda b, g=g, pr=pr: bank(b, 512, slice(64 * g, 64 * g + 64)).rearrange(
                                "p (h b q) -> p b h q", b=DB, q=DS)[:, :, 4 * pr + 2 * g:4 * pr + 2 * g + 2, :]))
                    turned(*copies)

            act.wait_ge(S["qz_zero"], 1)
            for i in range(TILES):
                if i:
                    take_raw(4 + i, 10 + i, 512)
                    q_turned(i - 1)
            act.wait_ge(S["qs_zero"], 1)

            def k_turned(i):
                r = rows_of(i)
                turned((kT[:, :, i * P:i * P + r], lambda b: bank(b, 2 * P).rearrange("p (k t) -> p k t", t=P)[:, :, 0:r]))

            for i in range(TILES):
                take_raw(9 + i, 15 + i, 256)
                if i:
                    k_turned(i - 1)
                else:
                    q_turned(PT_TILES)
            for i in range(TILES):
                r = rows_of(i)
                act.wait_ge(S["jp"], 20 + i)
                b = 2 + (19 + i) % 2
                if split_rows(i, 512):
                    act.copy(unat[0:r, i, 0:256], bank(b, 256, slice(0, r)))
                    act.copy(unat[0:r, i, 256:512], bank(b, 256, slice(r, 2 * r))).then_inc(S["je"], 1)
                else:
                    act.copy(unat[0:r, i, :], bank(b, 512, slice(0, r))).then_inc(S["je"], 1)
                if i == 0:
                    k_turned(PT_TILES)
            for i in range(TILES):
                r = rows_of(i)
                act.wait_ge(S["dt_done"], i + 1)
                act.copy(dT[:, :, i * P:i * P + r], bank(4 + i % 2).rearrange("p (g t) -> p g t", t=P)[:, :, 0:r]).then_inc(S["dt_ev"], 1)
            for g in range(NG):
                act.wait_ge(S["po_done"], g + 1)
                act.activation(poT[:, g, 0:SEQ], bank(6 + g % 2), ACT.Copy, scale=pscale[:, g:g + 1])
                act.activation(poT[:, g, SEQ:NT], bank(4 + g % 2, NS), ACT.Copy, scale=pscale[:, g:g + 1]).then_inc(S["po_ev"], 1)
            for n in range(PRE):
                act.wait_ge(S["g_done"], n + 1)
                act.copy(sgA[n // 2][:, HN * (n % 2):HN * (n % 2) + HN], bank(2 + n % 2, HN)).then_inc(S["raw_ev"], 1)
            units = [(i, h) for i in range(PT_TILES) for h in range(NH)]
            U = len(units)
            for u in range(U + 2):
                if u < U:
                    L = P * (units[u][0] + 1)
                    act.wait_ge(S["mx_done"], u + 1)
                    if u >= 2:
                        act.wait_ge(S["tp"], T0 + u - 1)
                    act.activation(prob[u % 2][:, 0:L], ml[u % 2][:, 0:L], ACT.Exp, bias=nmax[:, u % 4:u % 4 + 1], scale=SCALE,
                                   accum_out=esum[:, u % 4:u % 4 + 1]).then_inc(S["ex_done"], 1)
                if 1 <= u <= U:
                    n = units[u - 1][0] + 1
                    if u >= 3:
                        act.wait_ge(S["pv_done"], u - 2)
                    turned((probT[(u - 1) % 2][:, 0:n, :], lambda b: bank(b, n * P).rearrange("p (j t) -> p j t", t=P)))
                if u >= 2 and units[u - 2][1] % 2:
                    i, h = units[u - 2]
                    act.wait_ge(S["pv_done"], u - 1)
                    act.copy(attnT[:, h // 2, i * P:(i + 1) * P], bank(6 + (u - 2) // 2 % 2, P)).then_inc(S["ot_ev"], 1)
            act.wait_ge(S["pv_done"], U)
            for bp in range(DB // 2):
                if bp:
                    act.wait_ge(S["sl_done"], bp)
                for b2 in range(2):
                    for pr in range(2):
                        for rh in range(2):
                            turned((kTb[b2][:, pr, 512 * rh:512 * rh + 512], lambda b: bank(b)))
                act.wait_ge(S["smx_done"], bp + 1)
                act.activation(probs, psum[:, 4 * 512:4 * 512 + LS], ACT.Exp, bias=snmax, scale=SCALE, accum_out=ssum).then_inc(S["sex_done"], 1)
                if bp:
                    act.wait_ge(S["spv_done"], bp)
                for g in range(2):
                    turned((probsT[:, 4 * g:4 * g + 4, :], lambda b: bank(b).rearrange("p (j t) -> p j t", t=P)))
                turned((probsT[0:DS, RP, :], lambda b: bank(b, P, slice(0, DS))))
                act.wait_ge(S["spv_done"], bp + 1)
                act.wait_ge(S["srec_done"], bp + 1)
                if bp:
                    act.wait_ge(S["sot_done"], bp)
                act.activation(onat, bank(7, 256), ACT.Copy, scale=srec).then_inc(S["son_done"], 1)
            stores_done(act)
            act.wait_ge(S["raw_ev"], EARLY)
            act.wait_ge(S["son_done"], DB // 2)
            for k in range(len(gb_raw)):
                act.activation(sgB[k], gb_raw[k], ACT.Sigmoid).then_inc(S["gs_done"], 1)
            for k in range(KD):
                act.activation(sgA[k], sgA[k], ACT.Sigmoid).then_inc(S["gs_done"], 1)
            for n in range(EARLY, 32):
                act.wait_ge(S["g_done"], n + 1)
                act.activation(sgB[(n - 16) // 2][:, HN * (n % 2):HN * (n % 2) + HN], bank(4 + (n - EARLY) % 4, HN), ACT.Sigmoid).then_inc(S["gate_ev"], 1)
            for i in range(TILES):
                r = rows_of(i)
                act.wait_ge(S["h_add"], i + 1)
                if i >= 2:
                    act.wait_ge(S["xn2_r"], i - 1)
                act.activation(xs2[i % 2][0:r, :], resid[0:r, i, :], ACT.Square, accum_out=ss2[0:r, i:i + 1]).then_inc(S["sq2"], 1)
                act.wait_ge(S["sq2"], i + 1)
                act.activation(rt2[0:r, i:i + 1], ss2[0:r, i:i + 1], ACT.Sqrt, bias=eps[0:r], scale=1.0 / D).then_inc(S["rt2"], 1)
                act.wait_ge(S["rs2"], i + 1)
                act.activation(xs2[i % 2][0:r, :], resid[0:r, i, :], ACT.Copy, scale=rstd2[0:r, i:i + 1]).then_inc(S["xs2_r"], 1)
            for n, (src, dst) in enumerate(((gsh, gex), (vdf, vex))):
                act.wait_ge(S["gexp_in"], n + 1)
                act.activation(dst, src, ACT.Exp).then_inc(S["gexp_out"], 1)

            def take_x(m, s, n):
                act.wait_ge(m["xt_done"], n + 1)
                act.copy(xT[s].rearrange("p k t -> p (k t)"), bank(0)).then_inc(m["xt_ev"], 1)

            def silu(m, s, n):
                act.wait_ge(m["gu_done"], n + 1)
                act.activation(sg[s], bank(2 + s, DE, slice(0, CAP)), ACT.Silu).then_inc(m["silu"], 1)

            def take_h(m, s, n):
                act.wait_ge(m["ht_done"], n + 1)
                act.copy(hT[s].rearrange("p k t -> p (k t)"), bank(1, KE * CAP)).then_inc(m["ht_ev"], 1)

            def store_y(m, s, n, rows):
                act.wait_ge(m["y_ev"], n + 1)
                for half in range(2):
                    act.dma_start(rows[:, 512 * half:512 * half + 512], yo[s][64 * half:64 * half + 64, :]).then_inc(m["y_st"], 16)

            def expert_pair(i, last_pair=False):
                for s in range(2):
                    silu(M[s], s, i)
                    if not (last_pair and s == 1):
                        take_x(M[1 - s], 1 - s, i + s)
                    take_h(M[s], s, i)
                    store_y(M[s], s, i, y_d[bass.ds((2 * i + s) * CAP, CAP), :])

            take_x(M[0], 0, 0)
            expert_pair(0)
            with act.Fori(1, NE // 2 - 1) as i:
                expert_pair(i)
            expert_pair(NE // 2 - 1, True)
            act.wait_ge(S["flag_ready"], 1)
            over = act.value_load(flag[0:1, 0:1], min_val=0, max_val=NT)
            with act.If(over > CAP):
                act.wait_ge(S["y_zero"], 16 * YZ)
                with act.Fori(0, NE) as e:
                    with act.Fori(0, NB) as b:
                        n = e * NB + b + N0
                        take_x(OV, 0, n)
                        silu(OV, 0, n)
                        take_h(OV, 0, n)
                        store_y(OV, 0, n, y_d[bass.ds((e * NB + b) * CAP + FIRST, CAP), :])
            with act.Else():
                act.nop()
            act.activation(warm, eps, ACT.Sqrt)
            for i in range(TILES):
                r = rows_of(i)
                act.wait_ge(S["y_comb"], i + 1)
                if i >= 2:
                    act.wait_ge(S["sq3"], i - 1)
                b = (4 + 2 * (i % 2)) * 512
                act.activation(psum[0:r, b:b + D], resid[0:r, i, :], ACT.Square, accum_out=ss3[0:r, i:i + 1]).then_inc(S["sq3"], 1)
                act.wait_ge(S["sq3"], i + 1)
                act.activation(rt3[0:r, i:i + 1], ss3[0:r, i:i + 1], ACT.Sqrt, bias=eps[0:r], scale=1.0 / D).then_inc(S["rt3"], 1)

        @block.vector
        def _(dve):
            chain = [0]

            def link(ins):
                chain[0] += 1
                ins.then_inc(S["dvc"], 1)
                dve.wait_ge(S["dvc"], chain[0])

            dve.memset(stats[:, 20:60], 1.0)
            dve.memset(eps, EPS).then_inc(S["st_ready"], 1)
            dve.wait_ge(S["const_in"], 16)
            def inverse_rms(i):
                dve.wait_ge(S["rt_done"], i + 1)
                dve.reciprocal(rstd1[:, i:i + 1], rt1[:, i:i + 1]).then_inc(S["rstd_ready"], 1)

            inverse_rms(0)
            inverse_rms(1)
            dve.wait_ge(S["gain_in"], 48)
            for g in range(2 * TILES):
                i, half = g // 2, g % 2
                r = rows_of(i)
                if half == 0 and i + 2 < TILES:
                    inverse_rms(i + 2)
                if g == 2:
                    dve.wait_ge(S["page_in"], 16 * NPAGE)
                    dve.tensor_scalar(gidx, pgi, float(GR), const("lane"), ALU.mult, ALU.add).then_inc(S["gi_ready"], 1)
                dve.wait_ge(S["xt_done"], g + 1)
                dve.tensor_tensor(xnT[:, 4 * half:4 * half + 4, i * P:i * P + r], bank(g % 2).rearrange("p (k t) -> p k t", t=P)[:, :, 0:r],
                                  gain1[:, 4 * half:4 * half + 4].unsqueeze(2).to_broadcast([P, 4, r]), ALU.mult).then_inc(S["xn_ready"], 1)
            dve.wait_ge(S["const2_in"], 16)
            dve.tensor_copy(expand_b, expand_f).then_inc(S["ebf_ready"], 1)
            for j in range(3):
                i = QI_ORDER[j]
                L = P * (i + 1)
                for h in range(NI):
                    u = j * NI + h
                    dve.wait_ge(S["rl_ready"], u + 1)
                    w = wiS[:, i, h:h + 1]
                    if h == 0:
                        dve.tensor_scalar(score[i], rl[u % 2][:, 0:L], w, None, ALU.mult).then_inc(S["acc_done"], 1)
                    else:
                        dve.wait_ge(S["acc_done"], u)
                        dve.scalar_tensor_tensor(score[i], rl[u % 2][:, 0:L], w, score[i], ALU.mult, ALU.add).then_inc(S["acc_done"], 1)
            dve.wait_ge(S["wi_done"], 1)
            dve.tensor_tensor(wl, dmask, bank(6, NS).unsqueeze(1).to_broadcast([P, DB // 2, NS]), ALU.mult).then_inc(S["wl_ready"], 1)
            dve.wait_ge(S["zero_st"], 16)

            mx8, thr, ngt = cols[:, 16:24], cols[:, 23:24], cols[:, 24:25]

            def select(sc, L, k, rows, write_mask):
                w, gt, eq, rk = (a[0:rows, 0:L] for a in (work, gtm, eqm, rnk))
                m8, th, n = mx8[0:rows], thr[0:rows], ngt[0:rows]
                src = sc
                for rnd in range(k // 8):
                    link(dve.max(m8, src))
                    if rnd < k // 8 - 1:
                        link(dve.match_replace(w, m8, src, LOW))
                        src = w
                link(dve.tensor_scalar(gt, sc, th, 0.0, ALU.is_gt, ALU.add, accum_out=n))
                link(dve.tensor_scalar(eq, sc, th, None, ALU.is_equal))
                link(dve.tensor_tensor_scan(rk, eq, eq, 0.0, ALU.add, ALU.max))
                link(dve.tensor_scalar(n, n, -1.0, float(k), ALU.mult, ALU.add))
                link(dve.scalar_tensor_tensor(rk, rk, n, eq, ALU.is_le, ALU.mult))
                link(dve.tensor_tensor(gt, gt, rk, ALU.add))
                write_mask(gt)

            for i in range(1, PT_TILES):
                if i == 1:
                    dve.wait_ge(S["acc_done"], 3 * NI)
                L = P * (i + 1)
                link(dve.tensor_tensor(score[i][:, i * P:L], score[i][:, i * P:L], const("causal"), ALU.add))
                select(score[i], L, SEL_P, P, lambda g: link(dve.tensor_scalar(maskp[i], g, -1.0, NEG, ALU.add, ALU.mult)))
            dve.wait_ge(S["acc_ev"], 3)
            link(dve.tensor_tensor(sc_s[:, PAST:LS], sc_s[:, PAST:LS], const("newcausal", NS), ALU.add))

            def sample_mask(g):
                link(dve.tensor_scalar(msk[:, 0:PAST].rearrange("q (r p) -> q r p", p=P), g[:, 0:PAST].rearrange("q (p r) -> q r p", r=RP),
                                       -1.0, NEG, ALU.add, ALU.mult))
                dve.tensor_scalar(msk[:, PAST:LS], g[:, PAST:LS], -1.0, NEG, ALU.add, ALU.mult).then_inc(S["mask_s"], 1)

            select(sc_s, LS, SEL_S, NS, sample_mask)
            units = [(i, h) for i in range(PT_TILES) for h in range(NH)]
            U = len(units)

            def take_gate(n):
                m, cols_h = n % 8 // 2, slice(HN * (n % 2), HN * (n % 2) + HN)
                if n == 8:
                    dve.wait_ge(S["rope_done"], len(JOBS))
                    for s in range(2):
                        dve.wait_ge(s_rs[s], stored[s])
                dve.wait_ge(S["g_done"], n + 1)
                dst = sgA[4 * (n // 8) + m] if n < 16 else gb_raw[(n - 16) // 2]
                dve.tensor_copy(dst[:, cols_h], bank(2 + n % 2 if n < SAMPLE_G else 2, HN)).then_inc(S["raw_ev"], 1)

            for u in range(U + 1):
                if u < U:
                    i = units[u][0]
                    L = P * (i + 1)
                    c = slice(u % 4, u % 4 + 1)
                    dve.wait_ge(S["lg_done"], u + 1)
                    if u >= 2:
                        dve.wait_ge(S["ex_done"], u - 1)
                    dve.tensor_tensor_reduce(ml[u % 2][:, 0:L], bank(4 + u % 2, L), maskp[i] if i else const("causal"), 1.0, LOW,
                                             ALU.add, ALU.max, rmax[:, c]).then_inc(S["ml_done"], 1)
                    dve.wait_ge(S["ml_done"], u + 1)
                    dve.tensor_scalar(nmax[:, c], rmax[:, c], -SCALE, None, ALU.mult).then_inc(S["mx_done"], 1)
                if u:
                    v = u - 1
                    L = P * (units[v][0] + 1)
                    c = slice(v % 4, v % 4 + 1)
                    dve.wait_ge(S["ex_done"], v + 1)
                    link(dve.reciprocal(rsum[:, c], esum[:, c]))
                    dve.tensor_scalar(prob[v % 2][:, 0:L], prob[v % 2][:, 0:L], rsum[:, c], None, ALU.mult).then_inc(S["pn_done"], 1)
                if u >= 2 and u % 2 == 0:
                    take_gate(PRE + u // 2 - 1)
            for bp in range(DB // 2):
                dve.wait_ge(S["sl_done"], bp + 1)
                link(dve.reduce_max(smax, psum[:, 4 * 512:4 * 512 + LS], AX))
                dve.tensor_scalar(snmax, smax, -SCALE, None, ALU.mult).then_inc(S["smx_done"], 1)
                take_gate(SAMPLE_G + 2 * bp)
                dve.wait_ge(S["sex_done"], bp + 1)
                if bp:
                    dve.wait_ge(S["son_done"], bp)
                dve.reciprocal(srec, ssum).then_inc(S["srec_done"], 1)
                take_gate(SAMPLE_G + 1 + 2 * bp)
                dve.wait_ge(S["sot_done"], bp + 1)
                turned = bank(3, 2 * P).rearrange("p (k b h q) -> p k b h q", k=2, b=2, h=NH)
                for pr in range(2):
                    for g in range(2):
                        for j in range(2):
                            out = attnT[64 * j:64 * j + 64, 2 * pr + g, SEQ + 2 * DS * bp:SEQ + 2 * DS * (bp + 1)].rearrange("p (b q) -> p b q", q=DS)
                            last = dve.tensor_copy(out, turned[64 * g:64 * g + 64, pr, :, 4 * pr + 2 * g + j, :])
                last.then_inc(S["sot_ev"], 1)
            n = 0
            for mg in range(2):
                dve.wait_ge(S["gs_done"], KD + len(gb_raw))
                if mg:
                    dve.wait_ge(S["gate_ev"], 32 - EARLY)
                for m in range(4):
                    for hh in range(2):
                        a, b = (t[4 * mg + m][:, HN * hh:HN * hh + HN] for t in (sgA, sgB))
                        for v in (a, b):
                            dve.wait_ge(S["g_done"], 32 + n + 1)
                            dve.tensor_tensor(v, bank(4 + (32 - EARLY + n) % 4, HN), v, ALU.mult).then_inc(S["br_ev"], 1)
                            n += 1
                        dve.wait_ge(S["br_ev"], n)
                        dve.tensor_tensor(a, a, b, ALU.add).then_inc(S["m_done"], 1)
            stores_done(dve)
            dve.memset(lg, 0.0)

            def add_residual(i):
                r = rows_of(i)
                dve.wait_ge(S["h_done"], i + 1)
                b = (4 + 2 * (i % 2)) * 512
                if i == PT_TILES:
                    dve.tensor_tensor(resid[0:r, i, 0:512], bank(4, 512, slice(0, r)), resid[0:r, i, 0:512], ALU.add)
                    dve.tensor_tensor(resid[0:r, i, 512:D], bank(4, 512, slice(r, 2 * r)), resid[0:r, i, 512:D], ALU.add).then_inc(S["h_add"], 1)
                else:
                    dve.tensor_tensor(resid[0:r, i, :], psum[0:r, b:b + D], resid[0:r, i, :], ALU.add).then_inc(S["h_add"], 1)

            def take_turned(i):
                r = rows_of(i)
                for half in range(2):
                    g = 2 * i + half
                    dve.wait_ge(S["x2t"], g + 1)
                    if i >= 2:
                        dve.wait_ge(S["r_done"], i - 1)
                    dve.tensor_tensor(xn2T[i % 2][:, 4 * half:4 * half + 4, 0:r], bank(g % 2).rearrange("p (k t) -> p k t", t=P)[:, :, 0:r],
                                      gain2[:, 4 * half:4 * half + 4].unsqueeze(2).to_broadcast([P, 4, r]), ALU.mult).then_inc(S["x2e"], 1)
                dve.wait_ge(S["rt2"], i + 1)
                dve.reciprocal(rstd2[0:r, i:i + 1], rt2[0:r, i:i + 1]).then_inc(S["rs2"], 1)

            def take_logits(i):
                r = rows_of(i)
                dve.wait_ge(S["rs2"], i + 1)
                dve.wait_ge(S["r_done"], i + 1)
                dve.scalar_tensor_tensor(lg[0:r, i, :], bank(2 + i % 2, EG + NE, slice(0, r)), rstd2[0:r, i:i + 1], rbias[0:r, :],
                                         ALU.mult, ALU.add).then_inc(S["r_add"], 1)

            dve.tensor_copy(trib, const("tri"))
            dve.memset(oneb, 1.0).then_inc(S["tri_ready"], 1)
            dve.tensor_copy(toki, const("tok")).then_inc(S["tri_ready"], 1)
            dve.wait_ge(s_res, 16 * TILES)
            dve.wait_ge(S["late_in"], 96)
            add_residual(0)
            add_residual(1)
            for i in range(2, TILES):
                take_turned(i - 2)
                take_logits(i - 2)
                if i == TILES - 1:
                    take_turned(i - 1)
                add_residual(i)
            take_logits(TILES - 2)
            take_turned(TILES - 1)
            take_logits(TILES - 1)
            dve.wait_ge(S["r_add"], TILES)
            iota = const("iota")

            def first_of(v, n, top, hot, a, b):
                def over(x):
                    return x.unsqueeze(2).to_broadcast([P, TILES, n])
                link(dve.tensor_reduce(top, v, AX, ALU.max))
                link(dve.tensor_tensor(a, v, over(top), ALU.is_equal))
                link(dve.scalar_tensor_tensor(b, a, -64.0, iota[:, 0:n].unsqueeze(1).to_broadcast([P, TILES, n]), ALU.mult, ALU.add))
                link(dve.tensor_reduce(least, b, AX, ALU.min))
                link(dve.tensor_tensor(hot, b, over(least), ALU.is_equal))

            gl, el = lg[:, :, 0:EG], lg[:, :, EG:]
            first_of(gl, EG, gmax, ghot, t32[0][:, :, 0:EG], t32[1][:, :, 0:EG])
            dve.tensor_tensor(gsh, gl, gmax.unsqueeze(2).to_broadcast([P, TILES, EG]), ALU.subtract).then_inc(S["gexp_in"], 1)
            link(dve.tensor_scalar(ghot, ghot, NEG, -NEG, ALU.mult, ALU.add))
            link(dve.tensor_tensor(t32[2].rearrange("p t (g e) -> p t g e", e=EPG), el.rearrange("p t (g e) -> p t g e", e=EPG),
                                   ghot.unsqueeze(3).to_broadcast([P, TILES, EG, EPG]), ALU.add))
            first_of(t32[2], NE, top1, t32[3], t32[0], t32[1])
            link(dve.scalar_tensor_tensor(t32[2], t32[3], -2 * NEG, t32[2], ALU.mult, ALU.add))
            first_of(t32[2], NE, top2, t32[4], t32[0], t32[1])
            dve.tensor_tensor(vdf, top2, top1, ALU.subtract).then_inc(S["gexp_in"], 1)
            link(dve.tensor_tensor(t32[0], t32[3], t32[4], ALU.add))
            dve.tensor_tensor(ab, t32[0], const("valid").unsqueeze(2).to_broadcast([P, TILES, NE]), ALU.mult).then_inc(S["a_ready"], 1)
            dve.wait_ge(S["rank_done"], 1)
            rank = bank(4, TILES * NE).rearrange("p (t e) -> p t e", e=NE)
            link(dve.scalar_tensor_tensor(t32[1][:, :, 0:2], ab[:, :, 0:2], -1000.0, rank[:, :, 0:2], ALU.mult, ALU.add))
            for e in range(2):
                ins = dve.scalar_tensor_tensor(onehot[:, :, e, :], iota[:, 0:CAP].unsqueeze(1).to_broadcast([P, TILES, CAP]), -1000.0,
                                               t32[1][:, :, e:e + 1].to_broadcast([P, TILES, CAP]), ALU.add, ALU.is_equal)
            ins.then_inc(S["oh_ready"], 1)
            dve.wait_ge(S["oh_ready"], 1)
            dve.scalar_tensor_tensor(t32[1], rank, CAP - 0.5, const("jump").unsqueeze(1).to_broadcast([P, TILES, NE]), ALU.is_gt, ALU.mult)
            link(dve.tensor_tensor(t32[0], rank, const("base").unsqueeze(1).to_broadcast([P, TILES, NE]), ALU.add))
            link(dve.tensor_tensor(t32[0], t32[0], t32[1], ALU.add))
            dve.wait_ge(S["tok_done"], 1)
            for e in range(2):
                dve.tensor_copy(sidx[e], bank(5, 1, slice(CAP * e, CAP * e + CAP))).then_inc(S["tok_out"], 1)
            dve.tensor_tensor(t32[1], t32[0], t32[3], ALU.mult)
            link(dve.tensor_tensor(t32[2], t32[0], t32[4], ALU.mult))
            dve.tensor_reduce(s1, t32[1], AX, ALU.add)
            link(dve.tensor_reduce(s2, t32[2], AX, ALU.add))
            dve.tensor_tensor(dest[:, 0, :], s1, s2, ALU.min)
            dve.tensor_tensor(dest[:, 1, :], s1, s2, ALU.max).then_inc(S["dest_ready"], 1)
            link(dve.tensor_reduce(least[:, 0:1], bank(4, NE, at0=TILES * NE), AX, ALU.max))
            dve.tensor_copy(flag, least[:, 0:1]).then_inc(S["flag_ready"], 1)
            dve.wait_ge(S["gexp_out"], 2)
            link(dve.tensor_reduce(gw, gex, AX, ALU.add))
            link(dve.tensor_scalar(gmax, vex, 1.0, None, ALU.add))
            link(dve.tensor_tensor(gw, gw, gmax, ALU.mult))
            link(dve.reciprocal(w1, gw))
            link(dve.tensor_tensor(w2, w1, vex, ALU.mult))
            link(dve.tensor_tensor(top1, s1, s2, ALU.is_lt))
            link(dve.tensor_scalar(top2, top1, -1.0, 1.0, ALU.mult, ALU.add))
            for w, first, second in ((w_lo, top1, top2), (w_hi, top2, top1)):
                link(dve.tensor_tensor(gw, w1, first, ALU.mult))
                link(dve.tensor_tensor(gmax, w2, second, ALU.mult))
                link(dve.tensor_tensor(w, gw, gmax, ALU.add))

            def expert(m, s, n, first=False):
                dve.wait_ge(m["silu"], n + 1)
                dve.tensor_tensor(hb[s], sg[s], bank(2 + s, DE, slice(CAP, 2 * CAP)), ALU.mult).then_inc(m["h_ready"], 1)
                dve.wait_ge(m["y_done"], n + 1)
                if not first:
                    dve.wait_ge(m["y_st"], 32 * n)
                dve.tensor_copy(yo[s], bank(4 + s)).then_inc(m["y_ev"], 1)

            for s in range(2):
                expert(M[s], s, 0, True)
            with dve.Fori(1, NE // 2) as i:
                for s in range(2):
                    expert(M[s], s, i)
            dve.wait_ge(S["flag_ready"], 1)
            over = dve.value_load(flag[0:1, 0:1], min_val=0, max_val=NT)
            with dve.If(over > CAP):
                with dve.Fori(N0, N0 + NE * NB) as n:
                    expert(OV, 0, n)
            with dve.Else():
                dve.nop()
            def add_expert(i, k, w):
                r = rows_of(i)
                dve.wait_ge(s_y[i], 16 * (k + 1))
                return dve.scalar_tensor_tensor(resid[0:r, i, :], yg[i][k][0:r, :], w[0:r, i:i + 1], resid[0:r, i, :], ALU.mult, ALU.add)

            def final(i):
                r = rows_of(i)
                dve.wait_ge(S["rt3"], i + 1)
                dve.reciprocal(rstd3[0:r, i:i + 1], rt3[0:r, i:i + 1]).then_inc(S["rs3"], 1)
                dve.wait_ge(S["rs3"], i + 1)
                dve.scalar_tensor_tensor(yout[i][0:r, :], resid[0:r, i, :], rstd3[0:r, i:i + 1], fgrow[0:r, :], ALU.mult, ALU.mult).then_inc(S["fin_ready"], 1)

            for i in range(TILES):
                last = add_expert(i, 0, w_lo)
            link(last)
            for i in range(TILES):
                add_expert(i, 1, w_hi).then_inc(S["y_comb"], 1)
                if i:
                    final(i - 1)
            final(TILES - 1)

        @block.gpsimd
        def _(pool):
            chain = [0]

            def link(ins):
                chain[0] += 1
                ins.then_inc(S["plc"], 1)
                pool.wait_ge(S["plc"], chain[0])

            def gather(out, src, index, done):
                pool.indirect_dma_start(out, None, src, bass.IndirectOffsetOnAxis(ap=index, axis=0)).then_inc(done, 16)

            pool.wait_ge(S["gi_ready"], 1)
            for b in range(DB):
                gather(idxk[:, b, :], i_groups, gidx[:, b:b + 1], s_idx)
            pool.memset(work[:, 0:SLOTS // P], 0.0).then_inc(S["zero_w"], 1)
            pool.wait_ge(S["zero_w"], 1)
            pool.dma_start(tab_d.rearrange("(p n) a -> p (n a)", p=P), work[:, 0:SLOTS // P].bitcast(I32)).then_inc(S["zero_st"], 16)
            pool.memset(qs, 0.0).then_inc(S["qs_zero"], 1)
            pool.wait_ge(S["xs_ready"], TILES)
            for t in (qiz[0], qiz[1], qlo):
                pool.memset(t, 0.0)
            pool.memset(qhi, 0.0).then_inc(S["qiz_zero"], 1)

            def rotate(src, i, heads, outs):
                r = rows_of(i)
                x = src.rearrange("p (h a c) -> p h a c", a=2, c=HALF)
                a = rtmp[0][0:r, 0:heads * HD].rearrange("p (h a c) -> p h a c", a=2, c=HALF)
                b = rtmp[1][0:r, 0:heads * HD].rearrange("p (h a c) -> p h a c", a=2, c=HALF)
                full = [r, heads, HALF]

                def t(name):
                    return tab3[name][0:r, i, :].unsqueeze(1).to_broadcast(full)

                for half in range(2):
                    pool.tensor_tensor(a[:, :, half, :], x[:, :, half, :], t("cos"), ALU.mult)
                pool.tensor_tensor(b[:, :, 0, :], x[:, :, 1, :], t("nsin"), ALU.mult)
                link(pool.tensor_tensor(b[:, :, 1, :], x[:, :, 0, :], t("sin"), ALU.mult))
                for n, out in enumerate(outs):
                    last = pool.tensor_tensor(out, rtmp[0][0:r, 0:heads * HD].rearrange("p (h c) -> p h c", c=HD),
                                              rtmp[1][0:r, 0:heads * HD].rearrange("p (h c) -> p h c", c=HD), ALU.add)
                return last

            pool.wait_ge(S["const2_in"], 16)
            for i in range(TILES):
                r = rows_of(i)
                pool.wait_ge(S["je"], i + 1)
                if i:
                    pool.wait_ge(S["ki_roped"], i)
                rotate(kiraw[0:r, i, :], i, 1, [kir[0:r, i, HD * d:HD * d + HD].unsqueeze(1) for d in range(2)]).then_inc(S["ki_roped"], 1)
                pool.wait_ge(S["ki_roped"], i + 1)
                pool.dma_start(ni_rows[i], kir[0:r, i, 0:HD]).then_inc(S["ki_out"], 16)
            for job, (kind, i) in enumerate(JOBS):
                r = rows_of(i)
                if kind == "q" and i == 0:
                    pool.wait_ge(S["tp"], T_JOB[3] + DB)
                    pool.memset(qz, 0.0).then_inc(S["qz_zero"], 1)
                pool.wait_ge(S["je"], 6 + job)
                if job:
                    pool.wait_ge(S["rope_done"], job)
                if job >= 2:
                    pool.wait_ge(S["tp"], T_JOB[job - 2])
                    if STORED_AT[job - 2]:
                        pool.wait_ge(s_rs[job % 2], STORED_AT[job - 2])
                heads = NKV if kind == "k" else NH
                if kind != "k" and i == PT_TILES:
                    twice = roped[job % 2][0:r, :].rearrange("p (h d c) -> p h d c", d=2, c=HD)
                    outs = [twice[:, :, d, :] for d in range(2)]
                else:
                    outs = [roped[job % 2][0:r, 0:heads * HD].rearrange("p (h c) -> p h c", c=HD)]
                rotate(raw[job % 2][0:r, 0:heads * HD], i, heads, outs).then_inc(S["rope_done"], 1)
                if kind == "k":
                    pool.wait_ge(S["rope_done"], job + 1)
                    pool.dma_start(nk_rows[i], roped[job % 2][0:r, 0:NKV * HD]).then_inc(s_rs[job % 2], 16)
                    pool.dma_start(nv_rows[i], vnat[0:r, i, :]).then_inc(S["v_out"], 16)
            pool.wait_ge(S["je"], 24)
            pool.dma_start(np_prompt[0, 0], unat[P - HIST:P, PT_TILES - 1, :]).then_inc(S["u_out"], 16)
            pool.dma_start(np_sample[0, :, HIST - DS:HIST, :], unat[0:NS, PT_TILES, :]).then_inc(S["u_out"], 16)
            pool.wait_ge(S["po_done"], NG)
            pool.wait_ge(S["u_out"], 32)
            for bp in range(DB // 2):
                if bp:
                    pool.wait_ge(S["tp"], T0 + 32 + 11 * (bp - 1) + 8)
                for b2 in range(2):
                    gather(kb[:, b2, :], k_groups, gidx[:, 2 * bp + b2:2 * bp + b2 + 1], s_kin[b2])
                if bp:
                    pool.wait_ge(S["spv_done"], bp)
                for b2 in range(2):
                    gather(vb[:, b2, :], v_groups, gidx[:, 2 * bp + b2:2 * bp + b2 + 1], s_vin[b2])
                if bp == 0:
                    pool.wait_ge(S["mask_s"], 1)
                    pool.wait_ge(S["te"], T0)
                else:
                    pool.wait_ge(S["sl_done"], bp)
                for b2 in range(2):
                    c = SEQ + (2 * bp + b2) * DS
                    last = pool.tensor_copy(kTb[b2][:, :, PAST:LS], kT[:, :, c:c + DS])
                last.then_inc(S["knew_ev"], 1)
            pool.wait_ge(S["att_all"], 1)
            stores_done(pool)
            pool.memset(wr, 0.0).then_inc(S["wr_zero"], 1)
            pool.wait_ge(S["late_in"], 96)
            for i in range(TILES):
                r = rows_of(i)
                pool.wait_ge(S["xs2_r"], i + 1)
                if i >= 2:
                    pool.wait_ge(s_xst[i % 2], 16 * (i // 2))
                pool.tensor_tensor(xn2[i % 2][0:r, :], xs2[i % 2][0:r, :], g2row[0:r, :], ALU.mult).then_inc(S["xn2_r"], 1)
                pool.wait_ge(S["xn2_r"], i + 1)
                pool.dma_start(xn2_d[i * P:i * P + r, :], xn2[i % 2][0:r, :]).then_inc(s_xst[i % 2], 16)
            pool.wait_ge(s_xst[0], 48)
            pool.wait_ge(s_xst[1], 32)
            for e in range(2):
                pool.wait_ge(S["tok_out"], e + 1)
                gather(xg[e], xn2_d, sidx[e], M[e]["xg_in"])
            pool.wait_ge(S["dest_ready"], 1)
            pool.wait_ge(S["zero_st"], 16)
            pool.wait_ge(S["tri_ready"], 2)
            for i in range(TILES):
                r = rows_of(i)
                for k in range(2):
                    pool.indirect_dma_start(tab_d, bass.IndirectOffsetOnAxis(ap=dest[0:r, k, i:i + 1], axis=0),
                                            toki[0:r, i:i + 1], None).then_inc(S["sc_st"], 16)
            pool.wait_ge(S["sc_st"], 16 * 2 * TILES)
            with nc.allow_non_contiguous_dma(reason="the slots' tokens, a column for each expert"):
                pool.dma_start(slots, tab_d[0:FIRST, :].rearrange("(e c) a -> c (e a)", c=CAP)).then_inc(S["slots_in"], 16)
            pool.wait_ge(S["slots_in"], 16)
            with pool.Fori(1, NE // 2) as i:
                for s in range(2):
                    pool.wait_ge(M[s]["xt_done"], i)
                    pool.tensor_copy(sidx[s], slots[:, bass.ds(2 * i + s, 1)]).then_inc(S["sidx_set"], 1)
                    pool.wait_ge(S["sidx_set"], 2 * i + s - 1)
                    pool.sem_inc(S["passed"], 1)
                    gather(xg[s], xn2_d, sidx[s], M[s]["xg_in"])
            pool.wait_ge(S["flag_ready"], 1)
            over = pool.value_load(flag[0:1, 0:1], min_val=0, max_val=NT)

            def combine(k, rows):
                for i in range(TILES):
                    r = rows_of(i)
                    if k:
                        pool.wait_ge(s_y[i], 16)
                    gather(yg[i][k][0:r, :], rows, dest[0:r, k, i:i + 1], s_y[i])

            with pool.If(over > CAP):
                for s in range(2):
                    pool.wait_ge(M[s]["y_st"], 32 * (NE // 2))
                    pool.wait_ge(M[s]["y_done"], NE // 2)
                pool.memset(zeros, 0.0).then_inc(S["zero_w"], 1)
                pool.wait_ge(S["zero_w"], 2)
                beyond = y_d[FIRST:SLOTS, :].rearrange("(n p r) d -> n p (r d)", p=P, n=YZ)
                for n in range(YZ):
                    pool.dma_start(beyond[n], zeros).then_inc(S["y_zero"], 16)
                with pool.Fori(0, NE) as e:
                    with pool.Fori(0, NB) as b:
                        n = e * NB + b
                        pool.wait_ge(OV["xt_done"], n + N0)
                        pool.dma_start(sidx[0], tab_d[bass.ds(n * CAP + FIRST, CAP), :]).then_inc(S["sidx_in"], 16)
                        pool.wait_ge(S["sidx_in"], 16 * (n + 1))
                        pool.sem_inc(S["passed"], 1)
                        gather(xg[0], xn2_d, sidx[0], OV["xg_in"])
                pool.wait_ge(OV["y_st"], 32 * (N0 + NE * NB))
                combine(0, y_d)
                combine(1, y_d)
            with pool.Else():
                pool.wait_ge(M[0]["y_st"], 32 * (NE // 2))
                pool.wait_ge(M[1]["y_st"], 32 * (NE // 2 - 1))
                combine(0, y_d[0:FIRST - CAP, :])
                pool.wait_ge(M[1]["y_st"], 32 * (NE // 2))
                combine(1, y_d[0:FIRST, :])


INS = ("x_prompt", "x_sample", "cache_k", "cache_v", "cache_idx_k", "state_pool", "page_table", "attn_norm_g",
       "w_in", "w_pool", "pool_scale", "w_branch_attn", "w_branch_pool", "w_out", "ffn_norm_g", "w_router_group",
       "b_router_group", "w_router_expert", "b_router_expert", "w_exp_gate", "w_exp_up", "w_exp_down", "final_norm_g")
OUTS = ((1, SEQ, D), (DB, DS, D), (1, 1, SEQ, NKV, HD), (1, 1, SEQ, NKV, HD), (1, 1, SEQ, HD), (1, 1, HIST, UW),
        (1, DB, DS, NKV, HD), (1, DB, DS, NKV, HD), (1, DB, DS, HD), (1, DB, HIST, UW))


def kernel(**inputs):
    import concourse.bacc as bacc
    from concourse.bass_utils import run_bass_kernel_spmd

    nc = bacc.Bacc("TRN2", target_bir_lowering=False, num_devices=1)
    where, consts = constants()
    arrays = {"in_consts": consts}
    for name in INS:
        arrays["in_" + name] = np.ascontiguousarray(inputs[name])
    ins = [nc.dram_tensor(n, a.shape, mybir.dt.from_np(a.dtype), kind="ExternalInput").ap() for n, a in arrays.items()]
    outs = [nc.dram_tensor(f"out_{i}", s, F32, kind="ExternalOutput").ap() for i, s in enumerate(OUTS)]
    program(nc, ins[0], where, *ins[1:], *outs)
    r = run_bass_kernel_spmd(nc, [arrays], core_ids=[0])
    return tuple(r.results[0][f"out_{i}"] for i in range(len(OUTS)))
```
